# Optimizing a Trainium2 kernel written in Bass

```python
import math
import jax, jax.numpy as jnp
from jax import lax
import numpy as np

D_MODEL = 1024
BATCH = 1
SEQ = 512
DEPTH = 2
DEC_BATCH = 1
DEC_SEQ = 32
PAST_LEN = 128

CHUNK = 64
Q_BLOCK = 128
N_A_LAYERS = DEPTH // 2
N_B_LAYERS = DEPTH - N_A_LAYERS
SB_HEAD_DIM = 64
SB_HEADS = D_MODEL // SB_HEAD_DIM
SB_WIDTH = SB_HEADS * SB_HEAD_DIM
MLA_NOPE = 128
MLA_ROPE = 64
MLA_V = 128
MLA_QK = MLA_NOPE + MLA_ROPE
MLA_HEADS = D_MODEL // MLA_V
MLA_WIDTH = MLA_HEADS * MLA_V
KV_LORA = D_MODEL // 2
Q_LORA = D_MODEL // 2
ROPE_THETA = 10000.0
EPS = 1e-6
NEG_BIG = -1e30

kernel_name = "sb_mla_yoco_stream_step"

def rms_norm(x, g):
    xf = x.astype(jnp.float32)
    y = xf * lax.rsqrt(jnp.mean(xf * xf, axis=-1, keepdims=True) + EPS)
    return (y * g.astype(jnp.float32)).astype(x.dtype)

def rope(x, pos):
    half = x.shape[-1] // 2
    inv = ROPE_THETA ** (-jnp.arange(half, dtype=jnp.float32) / half)
    ang = pos.astype(jnp.float32)[:, None] * inv[None, :]
    shape = (pos.shape[0],) + (1,) * (x.ndim - 3) + (half,)
    cos = jnp.cos(ang).reshape(shape)
    sin = jnp.sin(ang).reshape(shape)
    xf = x.astype(jnp.float32)
    x1, x2 = xf[..., :half], xf[..., half:]
    return jnp.concatenate([x1 * cos - x2 * sin, x2 * cos + x1 * sin], axis=-1).astype(x.dtype)

def sb_attend(q, k, v, t0):
    z = jnp.einsum('bqhd,bkhd->bhqk', q.astype(jnp.float32), k.astype(jnp.float32)) * (SB_HEAD_DIM ** -0.5)
    tq = t0 + jnp.arange(q.shape[1])
    tk = jnp.arange(k.shape[1])
    mask = tk[None, :] < tq[:, None]
    log_stay = jnp.where(mask, jax.nn.log_sigmoid(-z), 0.0)
    after = lax.cumsum(log_stay, axis=3, reverse=True) - log_stay
    w = jnp.where(mask, jnp.exp(jax.nn.log_sigmoid(z) + after), 0.0)
    return jnp.einsum('bhqk,bkhd->bqhd', w, v.astype(jnp.float32)).astype(v.dtype)

def mla_attend(q, k_nope, k_pe, v, t0):
    qf = q.astype(jnp.float32)
    s = (jnp.einsum('bqhd,bkhd->bhqk', qf[..., :MLA_NOPE], k_nope.astype(jnp.float32))
         + jnp.einsum('bqhr,bkr->bhqk', qf[..., MLA_NOPE:], k_pe.astype(jnp.float32))) * (MLA_QK ** -0.5)
    tq = t0 + jnp.arange(q.shape[1])
    tk = jnp.arange(k_nope.shape[1])
    mask = (tk[None, :] // CHUNK) <= (tq[:, None] // CHUNK)
    p = jax.nn.softmax(jnp.where(mask, s, NEG_BIG), axis=-1)
    return jnp.einsum('bhqk,bkhd->bqhd', p, v.astype(jnp.float32)).astype(v.dtype)

def sweep_query_blocks(fn, q, *kv):
    bsz, t_len = q.shape[:2]
    nb = t_len // Q_BLOCK
    qb = q.reshape((bsz, nb, Q_BLOCK) + q.shape[2:]).swapaxes(0, 1)
    t0s = jnp.arange(nb) * Q_BLOCK
    out = lax.map(lambda a: fn(a[0], *kv, a[1]), (qb, t0s))
    return out.swapaxes(0, 1).reshape((bsz, t_len) + out.shape[3:])

def gated_out(o, gate, w_o):
    o = o.reshape(o.shape[0], o.shape[1], -1)
    return (jax.nn.silu(gate) * o) @ w_o

def sb_project(h, w_in, g_q, g_k):
    bsz, t_len, _ = h.shape
    q, k, v, gate = jnp.split(h @ w_in, 4, axis=-1)
    hs = (bsz, t_len, SB_HEADS, SB_HEAD_DIM)
    return rms_norm(q.reshape(hs), g_q), rms_norm(k.reshape(hs), g_k), v.reshape(hs), gate

def shared_kv(x, g_kv, w_kv_a, g_kv_a, g_kpe, pos):
    a = rms_norm(x, g_kv) @ w_kv_a
    latent = rms_norm(a[..., :KV_LORA], g_kv_a)
    kpe = rope(rms_norm(a[..., KV_LORA:], g_kpe), pos)
    return latent, kpe

def expand_kv(latent, w_kv_b, g_knope):
    bsz, t_len, _ = latent.shape
    kv = (latent @ w_kv_b).reshape(bsz, t_len, MLA_HEADS, MLA_NOPE + MLA_V)
    return rms_norm(kv[..., :MLA_NOPE], g_knope), kv[..., MLA_NOPE:]

def mla_query(h, w_in, g_qa, w_q_b, g_qn, g_qp, pos):
    bsz, t_len, _ = h.shape
    proj = h @ w_in
    qa = rms_norm(proj[..., :Q_LORA], g_qa)
    gate = proj[..., Q_LORA:]
    q = (qa @ w_q_b).reshape(bsz, t_len, MLA_HEADS, MLA_QK)
    qn = rms_norm(q[..., :MLA_NOPE], g_qn)
    qp = rope(rms_norm(q[..., MLA_NOPE:], g_qp), pos)
    return jnp.concatenate([qn, qp], axis=-1), gate

def trunk(x, t0, past, p):
    bsz, t_len, _ = x.shape
    pos = t0 + jnp.arange(t_len)
    new_k, new_v = [], []
    latent = kpe = k_nope = v_mla = kpe_all = None
    for layer in range(DEPTH):
        if layer < N_A_LAYERS:
            i = layer
            h = rms_norm(x, p["g_pre_a"][i])
            q, k, v, gate = sb_project(h, p["w_in_a"][i], p["g_q_a"][i], p["g_k_a"][i])
            new_k.append(k)
            new_v.append(v)
            if past is None:
                o = sweep_query_blocks(sb_attend, q, k, v)
            else:
                o = sb_attend(q, jnp.concatenate([past[0][i], k], axis=1),
                              jnp.concatenate([past[1][i], v], axis=1), t0)
            x = x + gated_out(o, gate, p["w_o_a"][i])
        else:
            j = layer - N_A_LAYERS
            if j == 0:
                latent, kpe = shared_kv(x, p["g_kv"], p["w_kv_a"], p["g_kv_a"], p["g_kpe"], pos)
                if past is None:
                    lat_all, kpe_all = latent, kpe
                else:
                    lat_all = jnp.concatenate([past[2], latent], axis=1)
                    kpe_all = jnp.concatenate([past[3], kpe], axis=1)
                k_nope, v_mla = expand_kv(lat_all, p["w_kv_b"], p["g_knope"])
            h = rms_norm(x, p["g_pre_b"][j])
            q, gate = mla_query(h, p["w_in_b"][j], p["g_qa"][j], p["w_q_b"][j],
                                p["g_qn"][j], p["g_qp"][j], pos)
            if past is None:
                o = sweep_query_blocks(mla_attend, q, k_nope, kpe_all, v_mla)
            else:
                o = mla_attend(q, k_nope, kpe_all, v_mla, t0)
            x = x + gated_out(o, gate, p["w_o_b"][j])
    y = rms_norm(x, p["g_final"])
    return y, jnp.stack(new_k), jnp.stack(new_v), latent, kpe

def setup_inputs(seed: int = 0) -> dict:
    key = jax.random.key(seed)
    ks = iter(jax.random.split(key, 32))

    def nrm(shape, scale=1.0):
        return jax.random.normal(next(ks), shape, jnp.float32) * scale

    def gain(shape):
        return 1.0 + 0.1 * nrm(shape)

    d = D_MODEL
    return {
        "x_prompt": nrm((BATCH, SEQ, d)),
        "x_sample": nrm((DEC_BATCH, DEC_SEQ, d)),
        "cache_sb_k": nrm((N_A_LAYERS, DEC_BATCH, PAST_LEN, SB_HEADS, SB_HEAD_DIM)),
        "cache_sb_v": nrm((N_A_LAYERS, DEC_BATCH, PAST_LEN, SB_HEADS, SB_HEAD_DIM)),
        "cache_mla_latent": nrm((DEC_BATCH, PAST_LEN, KV_LORA)),
        "cache_mla_kpe": nrm((DEC_BATCH, PAST_LEN, MLA_ROPE)),
        "g_pre_a": gain((N_A_LAYERS, d)),
        "w_in_a": nrm((N_A_LAYERS, d, 4 * SB_WIDTH), d ** -0.5),
        "g_q_a": gain((N_A_LAYERS, SB_HEAD_DIM)),
        "g_k_a": gain((N_A_LAYERS, SB_HEAD_DIM)),
        "w_o_a": nrm((N_A_LAYERS, SB_WIDTH, d), SB_WIDTH ** -0.5),
        "g_kv": gain((d,)),
        "w_kv_a": nrm((d, KV_LORA + MLA_ROPE), d ** -0.5),
        "g_kv_a": gain((KV_LORA,)),
        "g_kpe": gain((MLA_ROPE,)),
        "w_kv_b": nrm((KV_LORA, MLA_HEADS * (MLA_NOPE + MLA_V)), KV_LORA ** -0.5),
        "g_knope": gain((MLA_NOPE,)),
        "g_pre_b": gain((N_B_LAYERS, d)),
        "w_in_b": nrm((N_B_LAYERS, d, Q_LORA + MLA_WIDTH), d ** -0.5),
        "g_qa": gain((N_B_LAYERS, Q_LORA)),
        "w_q_b": nrm((N_B_LAYERS, Q_LORA, MLA_HEADS * MLA_QK), Q_LORA ** -0.5),
        "g_qn": gain((N_B_LAYERS, MLA_NOPE)),
        "g_qp": gain((N_B_LAYERS, MLA_ROPE)),
        "w_o_b": nrm((N_B_LAYERS, MLA_WIDTH, d), MLA_WIDTH ** -0.5),
        "g_final": gain((d,)),
    }

def reference(x_prompt, x_sample, cache_sb_k, cache_sb_v, cache_mla_latent, cache_mla_kpe,
              g_pre_a, w_in_a, g_q_a, g_k_a, w_o_a,
              g_kv, w_kv_a, g_kv_a, g_kpe, w_kv_b, g_knope,
              g_pre_b, w_in_b, g_qa, w_q_b, g_qn, g_qp, w_o_b, g_final):
    p = dict(g_pre_a=g_pre_a, w_in_a=w_in_a, g_q_a=g_q_a, g_k_a=g_k_a, w_o_a=w_o_a,
             g_kv=g_kv, w_kv_a=w_kv_a, g_kv_a=g_kv_a, g_kpe=g_kpe, w_kv_b=w_kv_b, g_knope=g_knope,
             g_pre_b=g_pre_b, w_in_b=w_in_b, g_qa=g_qa, w_q_b=w_q_b, g_qn=g_qn, g_qp=g_qp,
             w_o_b=w_o_b, g_final=g_final)
    y_prompt, sb_k_p, sb_v_p, lat_p, kpe_p = trunk(x_prompt, 0, None, p)
    y_sample, sb_k_s, sb_v_s, lat_s, kpe_s = trunk(
        x_sample, PAST_LEN, (cache_sb_k, cache_sb_v, cache_mla_latent, cache_mla_kpe), p)
    return (y_prompt, y_sample, sb_k_p, sb_v_p, lat_p, kpe_p, sb_k_s, sb_v_s, lat_s, kpe_s)


_drawn_inputs = setup_inputs


def setup_inputs(seed=0):
    import zlib

    import numpy as np

    out = dict(_drawn_inputs(seed))
    spreads = {}
    factors = {'g_q_a': 3.416, 'g_knope': 8.0, 'g_pre_b': 5.516, 'g_qa': 8.0, 'g_qn': 8.0, 'g_qp': 8.0}
    for name, (base, spread) in spreads.items():
        noise = np.random.default_rng([zlib.crc32(name.encode()), seed]).standard_normal(out[name].shape)
        drawn = base * np.exp(spread * noise) if base else spread * noise
        out[name] = __import__('jax').numpy.asarray(drawn.astype(out[name].dtype))
    for name, factor in factors.items():
        out[name] = (out[name] * factor).astype(out[name].dtype)
    return out
```

```python
from contextlib import ExitStack

import numpy as np

import concourse.bass as bass
from concourse import mybir

F32 = mybir.dt.float32
F32R = mybir.dt.float32r
BF16 = mybir.dt.bfloat16
ALU = mybir.AluOpType
ACT = mybir.ActivationFunctionType
AX = mybir.AxisListType

P = 128
D = 1024
KD = D // P
SEQ, SMP, PAST = 512, 32, 128
NT = SEQ // P
TT = NT + 1
TOK = SEQ + SMP
HALF = TOK // 2
FLAT = KD * TOK + P - SMP
HD = 64
NP = D // P
KV = 512
KL = KV // P
QFLAT = KL * TOK + P - SMP
NH = 8
NOPE, ROPE, VD = 128, 64, 128
QK = NOPE + ROPE
LT = TT + 1
KEYS = TOK + PAST
SKEY = SMP + PAST
EPS = 1e-6
BIG = -1e30

G_OA, G_LAT, G_KPE, G_QA, G_GATE, G_D, G_OB = NP, NP + 2, NP + 3, NP + 4, NP + 5, NP + 7, NP + 15
PIECES = 4
COLS = {g: KD * 512 for g in range(G_OB + 2)}
COLS[G_KPE] = KD * ROPE
for _g in range(G_D, G_OB):
    COLS[_g] = KL * (QK + NOPE + VD)

UA = 1 + 2 * NT
UNIT_A = [None] + [(h, i) for h in range(2) for i in reversed(range(NT))]
CA = TT + 2
XA = TT + 1
STEP_A = [("S", 0), ("S", 1), ("C", 0), ("W", 0), ("T", 0), ("S", 2), ("C", 1), ("W", 1), ("T", 1), ("X", 0),
          ("O", 0), ("S", 3), ("C", 2), ("W", 2), ("T", 2), ("X", 1), ("S", 4), ("C", 3), ("W", 3), ("T", 3),
          ("X", 2), ("S", 5), ("C", 4), ("T", 4), ("X", 3), ("S", 6), ("G", 0), ("O", 1), ("T", 5), ("X", 4),
          ("S", 7), ("T", 6), ("Z", 0), ("S", 8), ("G", 1), ("T", 7), ("T", 8), ("O", 2)]
UD = 1 + NT
CD = TT + LT
STEP_D = [("S", 0), ("Q", 0), ("S", 1), ("Q", 1), ("W", 0), ("K", 0), ("T", 0), ("X", 0), ("K", 1), ("X", 1),
          ("O", 0), ("T", 1), ("S", 2), ("W", 1), ("Q", 2), ("Y", 0), ("K", 2), ("Y", 1), ("X", 2), ("T", 2),
          ("S", 3), ("Q", 3), ("W", 2), ("Y", 2), ("K", 3), ("X", 3), ("T", 3), ("S", 4), ("Q", 4), ("W", 3),
          ("Y", 3), ("K", 4), ("X", 4), ("T", 4), ("K", 5), ("Y", 4), ("O", 1), ("Y", 5)]
CHUNK_D = {s: n for n, s in enumerate([s for s in STEP_D if s[0] in "QK"])}
XPOSE_D = {s: n for n, s in enumerate([s for s in STEP_D if s[0] in "XY"])}
MEAN_D = [0]
for _s in CHUNK_D:
    MEAN_D.append(MEAN_D[-1] + (2 if _s[0] == "Q" else 1))
MEANS = MEAN_D[-1]
AHEAD = {"C", "G", "X", "Z", "Q", "K", "Y"}


def rope_tables():
    half = ROPE // 2
    inv = np.float32(10000.0) ** (-np.arange(half, dtype=np.float32) / np.float32(half))
    pos = np.zeros(TT * P, np.float32)
    pos[:SEQ] = np.arange(SEQ)
    pos[SEQ:TOK] = PAST + np.arange(SMP)
    ang = (pos[:, None] * inv[None, :].astype(np.float32)).astype(np.float32)
    cos, sin = np.cos(ang).astype(np.float32), np.sin(ang).astype(np.float32)
    return cos, np.concatenate([-sin, sin], 1)


def build(nc, a, out, scratch):
    x_p = a["x_prompt"][0].rearrange("(t p) d -> p t d", p=P)
    x_s = a["x_sample"][0]
    w_in = a["w_in_a"][0].rearrange("(k p) (f m) -> p k f m", p=P, f=4)
    w_oa = a["w_o_a"][0].rearrange("(k p) n -> p k n", p=P)
    w_ob = a["w_o_b"][0].rearrange("(k p) n -> p k n", p=P)
    w_kva = a["w_kv_a"].rearrange("(k p) n -> p k n", p=P)
    w_inb = a["w_in_b"][0].rearrange("(k p) n -> p k n", p=P)
    w_qb = a["w_q_b"][0].rearrange("(k p) n -> p k n", p=P)
    w_kvb = a["w_kv_b"].rearrange("(k p) n -> p k n", p=P)
    ck = a["cache_sb_k"][0, 0].rearrange("t h d -> t (h d)")
    cv = a["cache_sb_v"][0, 0].rearrange("t h d -> t (h d)")
    y_p, y_s, k_p, v_p, lat_p, kpe_p, k_s, v_s, lat_s, kpe_s = out
    ko_p = k_p[0, 0].rearrange("(t p) h d -> p t (h d)", p=P)
    vo_p = v_p[0, 0].rearrange("(t p) h d -> p t (h d)", p=P)
    ko_s = k_s[0, 0].rearrange("p h d -> p (h d)")
    vo_s = v_s[0, 0].rearrange("p h d -> p (h d)")

    with ExitStack() as ctx:
        base = (nc.sbuf_base + 63) // 64 * 64
        arena = nc.sbuf_usable_end - base
        at = [0]

        def place(name, shape, dt, off=None):
            size = int(np.prod(shape[1:])) * (2 if dt == BF16 else 4)
            size = (size + 31) // 32 * 32
            o = at[0] if off is None else off
            if off is None:
                at[0] += size
            assert o + size <= arena, (name, o + size, arena)
            return nc.alloc_sbuf_tensor_at(name, shape, dt, offset=base + o), o + size

        def keep(name, shape, dt=F32):
            return place(name, shape, dt)[0]

        def alias(name, shape, off, dt=F32):
            return place(name, shape, dt, off)

        ident = keep("ident", [P, P])
        ident_b = keep("ident_b", [P, P], BF16)
        causal = keep("causal", [P, P], BF16)
        causal_s = keep("causal_s", [P, SMP], BF16)
        chunk_mask = keep("chunk_mask", [P, P], BF16)
        g_qk = keep("g_qk", [P, 2, 2, HD])
        g_q = keep("g_q", [P, QK])
        g_kn = keep("g_kn", [P, NOPE])
        g_kp = keep("g_kp", [P, ROPE])
        g_col = keep("g_col", [P, 3, KD])
        cos_t = keep("cos_t", [P, TT, ROPE // 2])
        sin_t = keep("sin_t", [P, TT, ROPE])
        neg_half = keep("neg_half", [P, 4])
        lat_ss = keep("lat_ss", [P, 2 * TT, 2])
        lat_ms = keep("lat_ms", [P, 2 * TT, 2])
        lat_r = keep("lat_r", [P, 2 * TT, 2])
        sq_pe = keep("sq_pe", [P, ROPE])
        pe_tmp = keep("pe_tmp", [P, 3, ROPE])
        ssq = keep("ssq", [P, 2, 4])
        msq = keep("msq", [P, 2, 4])
        rstd = keep("rstd", [P, 2, 4])
        row_ss = keep("row_ss", [P, 3, TT])
        row_ms = keep("row_ms", [P, 3, TT])
        row_r = keep("row_r", [P, 3, TT])
        neg_max = keep("neg_max", [P, 2])
        p_sum = keep("p_sum", [P, 2])
        p_inv = keep("p_inv", [P, 2])
        raw = keep("raw", [P, KD * 512])
        whi = [keep(f"whi{s}", [P, KD * 512], F32R) for s in range(2)]
        wlo = [keep(f"wlo{s}", [P, KD * 512], F32R) for s in range(2)]
        o_ht = at[0]
        ht = [keep(f"ht{s}", [P, FLAT], F32R) for s in ("hi", "lo")]
        o_gt = at[0]
        gt = [keep(f"gt{s}", [P, FLAT], F32R) for s in ("hi", "lo")]
        o_s = at[0]
        x_in, _ = alias("x_in", [P, TT, D], o_gt)
        qkt, o = alias("qkt", [P, 2, 2, TOK], o_s)
        vtok, o = alias("vtok", [P, 2, TT, P], o)
        qkn, o = alias("qkn", [P, TT, 2, P], o)
        kc, o = alias("kc", [P, 2, P], o)
        vc, o = alias("vc", [P, 2, P], o)
        kct, o = alias("kct", [P, 2, P], o)
        sgate, o = alias("sgate", [P, 2, TOK], o)
        wt, o = alias("wt", [P, NT, SEQ], o)
        wts, o = alias("wts", [P, 2, 2 * SMP], o)
        stay, o = alias("stay", [P, 2, SEQ], o)
        left, o = alias("left", [P, 2, SEQ + 1], o)
        wgt, o = alias("wgt", [P, 2, SEQ], o)
        sigm, _ = alias("sigm", [P, HALF], o)
        sq, o = alias("sq", [P, 2 * P], o)
        qkr, o = alias("qkr", [P, 2 * P], o)
        gated, o = alias("gated", [P, TOK], o)
        dump_x, o = alias("dump_x", [P, D], o_s)
        g_rows, _ = alias("g_rows", [3 * KD, P], o)
        x2, o = alias("x2", [P, TT, D], o_s)
        xn, o = alias("xn", [P, TT, D], o)
        dump, _ = alias("dump", [P, D], o)
        lath, o = alias("lath", [P, KL * LT * P], o_s, F32R)
        latl, o = alias("latl", [P, KL * LT * P], o, F32R)
        kpet, o_d = alias("kpet", [P, KEYS], o)
        lat, o = alias("lat", [P, LT, KV], o_d)
        kpe, o = alias("kpe", [P, LT, P], o)
        qan, o = alias("qan", [P, KV], o)
        sigc, _ = alias("sigc", [P, HALF], o)
        sqc, o = alias("sqc", [P, KV], o)
        g_lat, o = alias("g_lat", [P, KV], max(o, o_s + 8 * TT * D))
        g_qar, o = alias("g_qar", [P, KV], o)
        qat0, o = alias("qat0", [P, QFLAT], o_gt, F32R)
        qat1, o = alias("qat1", [P, QFLAT], o, F32R)
        qat = [qat0, qat1]
        latt = [lath, latl]
        sg_flat, _ = alias("sg", [P, NH * TOK], o)
        sg = sg_flat[:, :].rearrange("p (h t) -> p h t", h=NH)
        q2t, o = alias("q2t", [P, 2, 2, TOK], o_ht)
        k2t, o = alias("k2t", [P, 2, KEYS], o)
        wt2, o = alias("wt2", [P, NT, SEQ], o)
        prob, o = alias("prob", [P, 2, SEQ], o)
        assert o <= o_gt
        v2, o = alias("v2", [P, 2, LT, P], o_d)
        qn2, o = alias("qn2", [P, 2, 2 * P], o)
        kn2, o = alias("kn2", [P, 2, P], o)
        wts2, o = alias("wts2", [P, 2, SMP], o)
        sqd, o = alias("sqd", [P, NOPE], o)
        x2e, o = alias("x2e", [P, TT, D], o_s)
        g_fin, o = alias("g_fin", [P, D], o)
        dump2, o = alias("dump2", [P, D], o)

        bank = [ctx.enter_context(nc.psum_tensor(f"bank{b}", [P, 512], F32)) for b in range(8)]
        PRJ, SCR, TRB, OUT, XB = bank[0:2], bank[2:4], bank[4:6], bank[6], bank[7]

        def sem(name):
            return ctx.enter_context(nc.semaphore(name))

        s_hi = sem("s_hi")
        s_lo = sem("s_lo")
        s_raw = sem("s_raw")
        s_kcd = [sem(f"s_kcd{i}") for i in range(2)]
        s_vcd = [sem(f"s_vcd{i}") for i in range(2)]
        s_x_in = [sem(f"s_x_in{i}") for i in range(TT)]
        s_const_d = sem("s_const_d")
        s_normed = sem("s_normed")
        s_kout = sem("s_kout")
        s_act_c = sem("s_act_c")
        s_vout = [sem(f"s_vout{i}") for i in range(2)]
        s_av = sem("s_av")
        s_glo = sem("s_glo")
        s_x2d = [sem(f"s_x2d{i}") for i in range(TT)]
        s_rows_g = sem("s_rows_g")
        s_x2sum = sem("s_x2sum")
        s_x2out = sem("s_x2out")
        s_ct = sem("s_ct")
        s_latc = sem("s_latc")
        s_zeros_c = sem("s_zeros_c")
        s_latn = sem("s_latn")
        s_kper = sem("s_kper")
        s_latout = sem("s_latout")
        s_proj2 = sem("s_proj2")
        s_proj = sem("s_proj")
        s_od2 = sem("s_od2")
        s_x2in = [sem(f"s_x2in{i}") for i in range(TT)]
        s_gfin = sem("s_gfin")
        s_yn = sem("s_yn")
        s_yout = sem("s_yout")
        s_xt_hi = sem("s_xt_hi")
        s_xt = sem("s_xt")
        s_xt_lo = sem("s_xt_lo")
        s_dve_c = sem("s_dve_c")
        s_xev = sem("s_xev")
        s_xpose = sem("s_xpose")
        s_stay = sem("s_stay")
        s_score = sem("s_score")
        s_wgt = sem("s_wgt")
        s_wtev = sem("s_wtev")
        s_tr = sem("s_tr")
        s_odone = sem("s_odone")
        s_gcol = sem("s_gcol")
        s_xn = sem("s_xn")
        s_masks = sem("s_masks")
        s_gcol_t = sem("s_gcol_t")
        s_pad = sem("s_pad")
        s_ghi = sem("s_ghi")
        s_zeros_b = sem("s_zeros_b")
        s_yprod = sem("s_yprod")
        s_ct_lo = sem("s_ct_lo")
        s_ct_hi = sem("s_ct_hi")
        s_lat_lo = sem("s_lat_lo")
        s_kpet_e = sem("s_kpet_e")
        s_latx = sem("s_latx")
        s_latm = sem("s_latm")
        s_lat_hi = sem("s_lat_hi")
        s_zeros_d = sem("s_zeros_d")
        s_act2 = sem("s_act2")
        s_dve2 = sem("s_dve2")
        s_nrm2 = sem("s_nrm2")
        s_xev2 = sem("s_xev2")
        s_xp2 = sem("s_xp2")
        s_expd = sem("s_expd")
        s_score2 = sem("s_score2")
        s_scaled = sem("s_scaled")
        s_wtev2 = sem("s_wtev2")
        s_tr2 = sem("s_tr2")
        s_av2 = sem("s_av2")
        s_zeros_e = sem("s_zeros_e")
        s_go_hi = sem("s_go_hi")
        s_go_lo = sem("s_go_lo")
        s_ysum = sem("s_ysum")
        s_row_ss = sem("s_row_ss")
        s_msq_d = sem("s_msq_d")
        s_sqd = sem("s_sqd")
        s_left = sem("s_left")
        s_lat_ss = sem("s_lat_ss")
        s_mean2 = sem("s_mean2")
        s_mean = sem("s_mean")
        s_negmax = sem("s_negmax")
        s_row_ms = sem("s_row_ms")
        s_row_r = sem("s_row_r")
        s_zeros_m = sem("s_zeros_m")
        s_rs = sem("s_rs")
        s_lat_ms = sem("s_lat_ms")
        s_lat_r = sem("s_lat_r")
        s_rs2 = sem("s_rs2")
        s_gscale = sem("s_gscale")
        s_rope = sem("s_rope")
        s_inv = sem("s_inv")

        def begun(v):
            return not isinstance(v, int) or v > 0

        def wcol(g, part, k, c0, n, per):
            t = (whi, wlo)[part][g % 2]
            return t[:, k * per + c0:k * per + c0 + n]

        def acol(t, k, tile, width=TOK):
            return t[:, k * width + tile * P:k * width + tile * P + P]

        def three(eng, dst, pairs, ready=None):
            n = len(pairs)
            for k, (st, mv) in enumerate(pairs):
                if ready:
                    ready(k)
                eng.matmul(dst, st[0], mv[0], start=(k == 0), stop=False)
                eng.matmul(dst, st[0], mv[1], start=False, stop=False)
                mm = eng.matmul(dst, st[1], mv[0], start=False, stop=(k == n - 1))
            return mm

        block = ctx.enter_context(nc.Block())

        @block.sync
        def _(sp):
            def load_group(g, pieces):
                if begun(PIECES * g):
                    sp.wait_ge(s_hi, PIECES * g)
                if begun(PIECES * g):
                    sp.wait_ge(s_lo, PIECES * g)
                for dst, src in pieces:
                    sp.dma_start(dst, src).then_inc(s_raw, 16)

            def raw_v(per, c0, n, k0=0, kn=KD):
                return raw[:, 0:kn * per].rearrange("p (k c) -> p k c", k=kn)[:, k0:, c0:c0 + n]

            def load_pair(g):
                load_group(g, [(raw_v(512, f * P, P), w_in[:, :, f, bass.ds(g * P, P)]) for f in range(4)])

            def load_cols(g, w, c0, n):
                v = raw_v(n, 0, n)
                load_group(g, [(v[:, 2 * j:2 * j + 2], w[:, 2 * j:2 * j + 2, c0:c0 + n]) for j in range(4)])

            def load_head(h):
                v = raw[:, 0:COLS[G_D]].rearrange("p (k c) -> p k c", k=KL)
                pieces = []
                for j in range(2):
                    ks = slice(2 * j, 2 * j + 2)
                    pieces.append((v[:, ks, 0:QK], w_qb[:, ks, bass.ds(h * QK, QK)]))
                    pieces.append((v[:, ks, QK:], w_kvb[:, ks, bass.ds(h * 256, 256)]))
                load_group(G_D + h, pieces)

            def load_late(g):
                if g < NP:
                    load_pair(g)
                elif g < G_LAT:
                    load_cols(g, w_oa, (g - G_OA) * 512, 512)
                elif g == G_LAT:
                    load_cols(g, w_kva, 0, KV)
                elif g == G_KPE:
                    load_cols(g, w_kva, KV, ROPE)
                elif g == G_QA:
                    load_cols(g, w_inb, 0, 512)
                elif g < G_D:
                    load_cols(g, w_inb, (g - G_GATE + 1) * 512, 512)
                elif g < G_OB:
                    load_head(g - G_D)
                elif g < G_OB + 2:
                    load_cols(g, w_ob, (g - G_OB) * 512, 512)

            def cache_pair(q, par):
                sp.dma_start(kc[:, par, :], ck[:, bass.ds(q * P, P)]).then_inc(s_kcd[par], 16)
                sp.dma_start(vc[:, par, :], cv[:, bass.ds(q * P, P)]).then_inc(s_vcd[par], 16)

            for t in range(NT):
                sp.dma_start(x_in[:, t, :], x_p[:, t, :]).then_inc(s_x_in[t], 16)
            sp.dma_start(x_in[0:SMP, NT, :], x_s).then_inc(s_x_in[NT], 16)
            load_pair(0)
            for t, (dst, src) in enumerate([
                    (g_qk[:, 0, 0, :], a["g_q_a"].to_broadcast([P, HD])),
                    (g_qk[:, 0, 1, :], a["g_q_a"].to_broadcast([P, HD])),
                    (g_qk[:, 1, 0, :], a["g_k_a"].to_broadcast([P, HD])),
                    (g_qk[:, 1, 1, :], a["g_k_a"].to_broadcast([P, HD])),
                    (g_q[:, 0:NOPE], a["g_qn"].to_broadcast([P, NOPE])),
                    (g_q[:, NOPE:], a["g_qp"].to_broadcast([P, ROPE])),
                    (g_kn[:, :], a["g_knope"].rearrange("(a n) -> a n", a=1).to_broadcast([P, NOPE])),
                    (g_kp[:, :], a["g_kpe"].rearrange("(a n) -> a n", a=1).to_broadcast([P, ROPE])),
                    (g_rows[0:KD, :], a["g_pre_a"][0].rearrange("(k p) -> k p", p=P)),
                    (g_rows[KD:2 * KD, :], a["g_kv"].rearrange("(k p) -> k p", p=P)),
                    (g_rows[2 * KD:3 * KD, :], a["g_pre_b"][0].rearrange("(k p) -> k p", p=P)),
                    (cos_t[:, :, :], a["rope_cos"].rearrange("(t p) d -> p t d", p=P)),
                    (sin_t[:, :, :], a["rope_sin"].rearrange("(t p) d -> p t d", p=P))]):
                sp.dma_start(dst, src).then_inc(s_const_d, 16)
            load_pair(1)
            cache_pair(0, 0)
            cache_pair(1, 1)

            def outputs(q, par):
                sp.wait_ge(s_normed, TT * (q + 1))
                cols = bass.ds(q * P, P)
                sp.dma_start(ko_p[:, :, cols], qkn[:, 0:NT, 1, :]).then_inc(s_kout, 16)
                sp.dma_start(ko_s[:, cols], qkn[0:SMP, NT, 1, :]).then_inc(s_kout, 16)
                sp.wait_ge(s_act_c, CA * q + TT)
                sp.dma_start(vo_p[:, :, cols], vtok[:, par, 0:NT, :]).then_inc(s_vout[par], 16)
                sp.dma_start(vo_s[:, cols], vtok[0:SMP, par, NT, :]).then_inc(s_vout[par], 16)

            def step(p, par, last=False):
                if isinstance(p, int) and p + 3 >= NP:
                    load_late(p + 3)
                else:
                    load_pair(p + 3)
                if not (isinstance(p, int) and (p + 2 >= NP or p < 0)):
                    sp.wait_ge(s_av, 3 * p + 1)
                    cache_pair(p + 2, par)
                if not last:
                    outputs(p + 1, 1 - par)

            step(-1, 1)
            step(0, 0)
            with sp.Fori(0, 2) as i:
                step(2 * i + 1, 1)
                step(2 * i + 2, 0)
            step(5, 1)
            step(6, 0)
            step(7, 1, last=True)

            sp.wait_ge(s_glo, NP)
            sp.wait_ge(s_kout, 32 * NP)
            sp.wait_ge(s_vout[0], 16 * NP)
            sp.wait_ge(s_vout[1], 16 * NP)
            for t in range(NT):
                sp.dma_start(x2[:, t, :], x_p[:, t, :]).then_inc(s_x2d[t], 16)
            sp.dma_start(x2[0:SMP, NT, :], x_s).then_inc(s_x2d[NT], 16)
            sp.dma_start(g_lat[:, :], a["g_kv_a"].rearrange("(a n) -> a n", a=1).to_broadcast([P, KV])).then_inc(s_rows_g, 16)
            sp.dma_start(g_qar[:, :], a["g_qa"].to_broadcast([P, KV])).then_inc(s_rows_g, 16)
            for t in range(TT):
                n = P if t < NT else SMP
                sp.wait_ge(s_x2sum, 2 * (t + 1))
                sp.dma_start(scratch[t * P:t * P + n, :], x2[0:n, t, :]).then_inc(s_x2out, 16)
            load_late(G_KPE)

            sp.wait_ge(s_ct, KD)
            sp.wait_ge(s_x2out, 16 * TT)
            sp.dma_start(lat[:, TT, :], a["cache_mla_latent"][0]).then_inc(s_latc, 16)
            sp.wait_ge(s_zeros_c, 1)
            sp.dma_start(kpe[:, TT, 0:ROPE], a["cache_mla_kpe"][0]).then_inc(s_latc, 16)
            load_late(G_QA)
            for t in range(TT):
                n = P if t < NT else SMP
                sp.wait_ge(s_latn, t + 1)
                sp.wait_ge(s_kper, t + 1)
                lo_, ko_ = (lat_p, kpe_p) if t < NT else (lat_s, kpe_s)
                r0 = t * P if t < NT else 0
                sp.dma_start(lo_[0, r0:r0 + n, :], lat[0:n, t, :]).then_inc(s_latout, 16)
                sp.dma_start(ko_[0, r0:r0 + n, :], kpe[0:n, t, 0:ROPE]).then_inc(s_latout, 16)
            for g in range(G_GATE, G_D + 2):
                load_late(g)

            load_head(2)
            with sp.Fori(0, NH - 3) as h:
                load_head(h + 3)
            load_late(G_OB)
            load_late(G_OB + 1)
            sp.wait_ge(s_proj2, CD * NH)
            sp.wait_ge(s_od2, 2 * NH)
            sp.wait_ge(s_latout, 32 * TT)
            for t in range(TT):
                n = P if t < NT else SMP
                sp.dma_start(x2e[0:n, t, :], scratch[t * P:t * P + n, :]).then_inc(s_x2in[t], 16)
            sp.dma_start(g_fin[:, :], a["g_final"].rearrange("(a n) -> a n", a=1).to_broadcast([P, D])).then_inc(s_gfin, 16)
            for t in range(TT):
                n = P if t < NT else SMP
                sp.wait_ge(s_yn, t + 1)
                dst = y_p[0, t * P:t * P + n, :] if t < NT else y_s[0]
                sp.dma_start(dst, x2e[0:n, t, :]).then_inc(s_yout, 16)
            sp.wait_ge(s_yout, 16 * TT)

        @block.tensor
        def _(pe):
            def weights(g):
                pe.wait_ge(s_hi, PIECES * (g + 1))
                pe.wait_ge(s_lo, PIECES * (g + 1))

            def piece(g, kn=KD):
                def ready(k):
                    if k * PIECES % kn == 0:
                        pe.wait_ge(s_hi, PIECES * g + k * PIECES // kn + 1)
                        pe.wait_ge(s_lo, PIECES * g + k * PIECES // kn + 1)
                return ready

            def proj_a(q, par, c):
                ready = piece(q) if c == 0 else None
                if c == 0 and isinstance(q, int) and q == 0:
                    def ready(k):
                        piece(0)(k)
                        pe.wait_ge(s_xt_hi, k + 1)
                        pe.wait_ge(s_xt_lo, k + 1)
                if begun(CA * q + c - 1):
                    pe.wait_ge(s_act_c, CA * q + c - 1)
                if begun(CA * q + c - 1):
                    pe.wait_ge(s_dve_c, CA * q + c - 1)
                b = PRJ[(par + c) % 2]
                mm = three(pe, b[:, 0:3 * P], [
                    ([acol(ht[0], k, c), acol(ht[1], k, c)],
                     [whi[par][:, k * 512:k * 512 + 3 * P], wlo[par][:, k * 512:k * 512 + 3 * P]]) for k in range(KD)], ready)
                mm.then_inc(s_proj, 1)

            def gate_a(q, par, j):
                c = TT + j
                pe.wait_ge(s_act_c, CA * q + c - 1)
                if begun(CA * q + c - 1):
                    pe.wait_ge(s_dve_c, CA * q + c - 1)
                b = PRJ[(par + c) % 2]
                mm = three(pe, b[:, 0:HALF], [
                    ([whi[par][:, k * 512 + 384:k * 512 + 512], wlo[par][:, k * 512 + 384:k * 512 + 512]],
                     [ht[m][:, k * TOK + j * HALF:k * TOK + (j + 1) * HALF] for m in range(2)]) for k in range(KD)])
                mm.then_inc(s_proj, 1)

            def xpose_a(q, par, t):
                pe.wait_ge(s_normed, TT * q + t + 1)
                if begun(XA * q + t):
                    pe.wait_ge(s_xev, XA * q + t)
                for m in range(2):
                    mm = pe.transpose(XB[:, m * P:(m + 1) * P], qkn[:, t, m, :], ident[:, :])
                mm.then_inc(s_xpose, 1)

            def xpose_cache(q, par):
                pe.wait_ge(s_kcd[par], 8 * (q - par) + 16)
                pe.wait_ge(s_xev, XA * q + TT)
                pe.transpose(XB[:, 0:P], kc[:, par, :], ident[:, :]).then_inc(s_xpose, 1)

            def score_a(p, par, u):
                ub = (par + u) % 2
                if begun(UA * p + u - 1):
                    pe.wait_ge(s_stay, UA * p + u - 1)
                if u == 0:
                    pe.wait_ge(s_xev, XA * (p + 1))
                b = SCR[ub]
                if u == 0:
                    pe.matmul(b[0:2 * SMP, PAST:SKEY], ident_b[:, 0:2 * SMP], causal_s[:, :],
                              start=True, stop=False, skip_group_check=True)
                    for h in range(2):
                        r = slice(h * HD, (h + 1) * HD)
                        o = slice(h * SMP, (h + 1) * SMP)
                        qs = qkt[r, par, 0, SEQ:TOK]
                        pe.matmul(b[o, PAST:SKEY], qs, qkt[r, par, 1, SEQ:TOK], start=False, stop=True,
                                  skip_group_check=True)
                        mm = pe.matmul(b[o, 0:PAST], qs, kct[r, par, :], start=False, stop=True,
                                       skip_group_check=True)
                    mm.then_inc(s_score, 1)
                    return
                h, i = UNIT_A[u]
                r = slice(h * HD, (h + 1) * HD)
                pe.matmul(b[:, 0:(i + 1) * P], qkt[r, par, 0, i * P:(i + 1) * P], qkt[r, par, 1, 0:(i + 1) * P],
                          start=True, stop=True)
                pe.matmul(b[:, i * P:(i + 1) * P], ident_b[:, :], causal[:, :], start=False, stop=True,
                          skip_group_check=True).then_inc(s_score, 1)

            def turn_a(p, par, u):
                ub = (par + u) % 2
                pe.wait_ge(s_wgt, UA * p + u + 1)
                if begun(UA * p + u - 1):
                    pe.wait_ge(s_wtev, UA * p + u - 1)
                n = 2 if u == 0 else UNIT_A[u][1] + 1
                for j in range(n):
                    mm = pe.transpose(TRB[ub][:, j * P:(j + 1) * P], wgt[:, ub, j * P:(j + 1) * P], ident[:, :])
                mm.then_inc(s_tr, 1)

            def out_a(p, par, o):
                if begun(3 * p + o):
                    pe.wait_ge(s_odone, 3 * p + o)
                pe.wait_ge(s_wtev, UA * p + (1 if o == 0 else 1 + NT * o))
                if o == 0:
                    pe.wait_ge(s_vcd[par], 8 * (p - par) + 16)
                    pe.wait_ge(s_act_c, CA * p + TT)
                    for h in range(2):
                        r = slice(h * HD, (h + 1) * HD)
                        c = slice(h * SMP, (h + 1) * SMP)
                        pe.matmul(OUT[r, 0:SMP], vc[:, par, r], wts[:, 0, c], start=True, stop=False)
                        mm = pe.matmul(OUT[r, 0:SMP], vtok[0:SMP, par, NT, r], wts[0:SMP, 1, c], start=False, stop=True)
                    mm.then_inc(s_av, 1)
                    return
                r = slice((o - 1) * HD, o * HD)
                for j in range(NT):
                    mm = pe.matmul(OUT[r, j * P:SEQ], vtok[:, par, j, r], wt[:, j, j * P:SEQ],
                                   start=(j == 0), stop=(j == NT - 1))
                mm.then_inc(s_av, 1)

            def step_a(p, par, att=True, ahead=True):
                for what, n in STEP_A:
                    if what in AHEAD:
                        if not ahead:
                            continue
                        q, qpar = p + 1, 1 - par
                        if what == "C":
                            proj_a(q, qpar, n)
                        elif what == "G":
                            gate_a(q, qpar, n)
                        elif what == "X":
                            xpose_a(q, qpar, n)
                        elif what == "Z":
                            xpose_cache(q, qpar)
                    elif att:
                        if what == "S":
                            score_a(p, par, n)
                        elif what == "T":
                            turn_a(p, par, n)
                        elif what == "O":
                            out_a(p, par, n)

            def turn_x(K):
                b, bs = (bank[4 + K % 2], bank[6 + K % 2])
                if begun(K - 1):
                    pe.wait_ge(s_xt_lo, K - 1)
                if K == 1:
                    pe.wait_ge(s_gcol, 1)
                for t in range(NT):
                    if K == 0:
                        pe.wait_ge(s_xn, t + 1)
                    pe.transpose(b[:, t * P:(t + 1) * P], x_in[:, t, K * P:(K + 1) * P], ident[:, :])
                if K == 0:
                    pe.wait_ge(s_xn, TT)
                pe.transpose(bs[:, 0:SMP], x_in[0:SMP, NT, K * P:(K + 1) * P], ident[0:SMP, 0:SMP]).then_inc(s_xt, 1)

            pe.wait_ge(s_masks, 2)
            pe.wait_ge(s_const_d, 16 * 13)
            pe.transpose(XB[:, 0:3 * KD], g_rows[:, :], ident[0:3 * KD, 0:3 * KD]).then_inc(s_gcol_t, 1)
            for K in range(KD):
                turn_x(K)
            pe.wait_ge(s_pad, 4)

            pe.wait_ge(s_gcol, 1)
            step_a(-1, 1, att=False)
            pe.wait_ge(s_masks, 7)
            step_a(0, 0)
            with pe.Fori(0, 3) as i:
                step_a(2 * i + 1, 1)
                step_a(2 * i + 2, 0)
            step_a(7, 1, ahead=False)

            weights(G_OA)
            weights(G_OA + 1)
            pe.wait_ge(s_ghi, NP)
            pe.wait_ge(s_glo, NP)
            pe.wait_ge(s_zeros_b, 2)
            for t in range(TT):
                for nh in range(2):
                    n = 2 * t + nh
                    if begun(n - 3):
                        pe.wait_ge(s_x2sum, n - 3)
                    g = G_OA + nh
                    three(pe, bank[n % 4][:, :], [
                        ([acol(gt[0], k, t), acol(gt[1], k, t)],
                         [wcol(g, m, k, 0, 512, 512) for m in range(2)]) for k in range(KD)]).then_inc(s_yprod, 1)

            for K in range(KD):
                b, bs = bank[4 + K % 2], bank[6 + K % 2]
                if begun(K - 1):
                    pe.wait_ge(s_ct_lo, K - 1)
                if K == 0:
                    pe.wait_ge(s_xn, 2 * TT)
                for t in range(NT):
                    pe.transpose(b[:, t * P:(t + 1) * P], xn[:, t, K * P:(K + 1) * P], ident[:, :])
                pe.transpose(bs[:, 0:SMP], xn[0:SMP, NT, K * P:(K + 1) * P], ident[0:SMP, 0:SMP]).then_inc(s_ct, 1)
            pe.wait_ge(s_ct_hi, KD)
            pe.wait_ge(s_ct_lo, KD)

            def lat_turn(t):
                if begun(t):
                    pe.wait_ge(s_lat_lo, t)
                if begun(t):
                    pe.wait_ge(s_kpet_e, t)
                if t < TT:
                    pe.wait_ge(s_latn, t + 1)
                    pe.wait_ge(s_kper, t + 1)
                else:
                    pe.wait_ge(s_latc, 32)
                for k in range(KL):
                    pe.transpose(bank[4][:, k * P:(k + 1) * P], lat[:, t, k * P:(k + 1) * P], ident[:, :])
                pe.transpose(bank[5][:, 0:P], kpe[:, t, :], ident[:, :]).then_inc(s_latx, 1)

            for t in range(TT):
                if begun(t - 1):
                    pe.wait_ge(s_latn, t - 1)
                st = [[acol(gt[m], k, t) for m in range(2)] for k in range(KD)]
                three(pe, bank[t % 2][:, :], [(st[k], [wcol(G_LAT, m, k, 0, 512, 512) for m in range(2)]) for k in range(KD)],
                      piece(G_LAT) if t == 0 else None)
                if t == 0:
                    weights(G_KPE)
                three(pe, bank[2 + t % 2][:, 0:ROPE],
                      [(st[k], [wcol(G_KPE, m, k, 0, ROPE, ROPE) for m in range(2)]) for k in range(KD)]).then_inc(s_latm, 1)
                if t:
                    lat_turn(t - 1)
            lat_turn(TT - 1)
            lat_turn(TT)

            def qa_turn(t):
                pe.wait_ge(s_lat_lo, LT + t)
                pe.wait_ge(s_latn, TT + t + 1)
                for k in range(KL):
                    mm = pe.transpose(bank[4][:, k * P:(k + 1) * P], qan[:, k * P:(k + 1) * P], ident[:, :])
                mm.then_inc(s_latx, 1)

            for t in range(TT):
                n = TT + t
                pe.wait_ge(s_latn, n - 1)
                three(pe, bank[n % 2][:, :], [
                    ([acol(ht[m], k, t) for m in range(2)], [wcol(G_QA, m, k, 0, 512, 512) for m in range(2)])
                    for k in range(KD)], piece(G_QA) if t == 0 else None).then_inc(s_latm, 1)
                if t:
                    qa_turn(t - 1)
            for m8 in range(NH):
                g, mm4 = G_GATE + m8 // 4, m8 % 4
                if mm4 == 0:
                    weights(g)
                for j in range(2):
                    n = 2 * m8 + j
                    pe.wait_ge(s_dve_c, CA * NP + n - 1)
                    three(pe, bank[2 + n % 2][:, 0:HALF], [
                        ([wcol(g, m, k, mm4 * P, P, 512) for m in range(2)],
                         [ht[m][:, k * TOK + j * HALF:k * TOK + (j + 1) * HALF] for m in range(2)])
                        for k in range(KD)]).then_inc(s_proj, 1)
                    if n == 0:
                        qa_turn(TT - 1)
            pe.wait_ge(s_lat_hi, LT + TT)
            pe.wait_ge(s_lat_lo, LT + TT)
            pe.wait_ge(s_kpet_e, LT)
            pe.wait_ge(s_zeros_d, 4)

            def chunk_free(q, what, n):
                c = CHUNK_D[what, n]
                if begun(CD * q + c - 1):
                    pe.wait_ge(s_act2, CD * q + c - 1)
                if begun(CD * q + c - 1):
                    pe.wait_ge(s_dve2, CD * q + c - 1)
                return c

            def query_d(q, par, t):
                g = (G_D + par) % 2
                c = chunk_free(q, "Q", t)
                if c == 0:
                    if isinstance(q, int) and q == 0:
                        pe.wait_ge(s_dve_c, CA * NP + 2 * NH)
                three(pe, PRJ[(par + c) % 2][:, 0:QK], [
                    ([acol(qat[m], k, t) for m in range(2)],
                     [(whi, wlo)[m][g][:, k * 448:k * 448 + QK] for m in range(2)]) for k in range(KL)],
                    piece(q + G_D, KL) if c == 0 else None).then_inc(s_proj2, 1)

            def keyval_d(q, par, t):
                g = (G_D + par) % 2
                c = chunk_free(q, "K", t)
                three(pe, PRJ[(par + c) % 2][:, 0:256], [
                    ([latt[m][:, (k * LT + t) * P:(k * LT + t + 1) * P] for m in range(2)],
                     [(whi, wlo)[m][g][:, k * 448 + QK:(k + 1) * 448] for m in range(2)]) for k in range(KL)]).then_inc(s_proj2, 1)

            def turn_qk(q, par, what, t):
                src, n = (qn2, 2) if what == "X" else (kn2, 1)
                x = XPOSE_D[what, t]
                if what == "X":
                    pe.wait_ge(s_nrm2, TT * q + t + 1)
                else:
                    pe.wait_ge(s_dve2, CD * q + CHUNK_D["K", t] + 1)
                if begun(CD * q + x):
                    pe.wait_ge(s_xev2, CD * q + x)
                for m in range(n):
                    mm = pe.transpose(XB[:, m * P:(m + 1) * P], src[:, t % 2, m * P:(m + 1) * P], ident[:, :])
                mm.then_inc(s_xp2, 1)

            def score_d(h, par, u):
                ub = (par + u) % 2
                if begun(UD * h + u - 1):
                    pe.wait_ge(s_expd, UD * h + u - 1)
                if u == 0:
                    pe.wait_ge(s_xev2, CD * (h + 1))
                b = SCR[ub]
                if u == 0:
                    for m, rhs in ((0, k2t[:, par, SEQ:KEYS]), (1, kpet[:, SEQ:KEYS])):
                        mm = pe.matmul(b[0:SMP, 0:SKEY], q2t[:, par, m, SEQ:TOK], rhs, start=(m == 0), stop=(m == 1))
                    mm.then_inc(s_score2, 1)
                    return
                i = NT - u
                for m, rhs in ((0, k2t[:, par, 0:(i + 1) * P]), (1, kpet[:, 0:(i + 1) * P])):
                    pe.matmul(b[:, 0:(i + 1) * P], q2t[:, par, m, i * P:(i + 1) * P], rhs, start=(m == 0), stop=(m == 1))
                pe.matmul(b[:, i * P:(i + 1) * P], ident_b[:, :], chunk_mask[:, :], start=False, stop=True,
                          skip_group_check=True).then_inc(s_score2, 1)

            def turn_d(h, par, u):
                ub = (par + u) % 2
                pe.wait_ge(s_scaled, UD * h + u + 1)
                if begun(UD * h + u - 1):
                    pe.wait_ge(s_wtev2, UD * h + u - 1)
                offs = [0, SMP] if u == 0 else [j * P for j in range(NT - u + 1)]
                for j, o in enumerate(offs):
                    mm = pe.transpose(TRB[ub][:, j * P:(j + 1) * P], prob[:, ub, o:o + P], ident[:, :])
                mm.then_inc(s_tr2, 1)

            def out_d(h, par, o):
                if begun(2 * h + o):
                    pe.wait_ge(s_od2, 2 * h + o)
                pe.wait_ge(s_wtev2, UD * h + (1 if o == 0 else UD))
                if o == 0:
                    pe.wait_ge(s_dve2, CD * (h + 1))
                    pe.matmul(OUT[:, 0:SMP], v2[0:SMP, par, NT, :], wts2[0:SMP, 0, :], start=True, stop=False)
                    pe.matmul(OUT[:, 0:SMP], v2[:, par, TT, :], wts2[:, 1, :], start=False, stop=True).then_inc(s_av2, 1)
                    return
                for j in range(NT):
                    mm = pe.matmul(OUT[:, j * P:SEQ], v2[:, par, j, :], wt2[:, j, j * P:SEQ],
                                   start=(j == 0), stop=(j == NT - 1))
                mm.then_inc(s_av2, 1)

            def step_d(h, par, att=True, ahead=True):
                for what, n in STEP_D:
                    if what in AHEAD:
                        if not ahead:
                            continue
                        q, qpar = h + 1, 1 - par
                        if what == "Q":
                            query_d(q, qpar, n)
                        elif what == "K":
                            keyval_d(q, qpar, n)
                        else:
                            turn_qk(q, qpar, what, n)
                    elif att:
                        if what == "S":
                            score_d(h, par, n)
                        elif what == "T":
                            turn_d(h, par, n)
                        elif what == "O":
                            out_d(h, par, n)

            step_d(-1, 1, att=False)
            step_d(0, 0)
            with pe.Fori(0, 3) as i:
                step_d(2 * i + 1, 1)
                step_d(2 * i + 2, 0)
            step_d(7, 1, ahead=False)

            weights(G_OB)
            weights(G_OB + 1)
            pe.wait_ge(s_zeros_e, 2)

            def split_out(k):
                pe.wait_ge(s_go_hi, k + 1)
                pe.wait_ge(s_go_lo, k + 1)

            for t in range(TT):
                for nh in range(2):
                    n = 2 * t + nh
                    if begun(n - 3):
                        pe.wait_ge(s_ysum, n - 3)
                    g = G_OB + nh
                    three(pe, bank[n % 4][:, :], [
                        ([acol(ht[0], k, t), acol(ht[1], k, t)],
                         [wcol(g, m, k, 0, 512, 512) for m in range(2)]) for k in range(KD)],
                        split_out if n == 0 else None).then_inc(s_yprod, 1)

        def last_reader(g):
            if not isinstance(g, int) or g < G_LAT:
                return s_proj, CA * (g - 1)
            if g <= G_KPE:
                return s_yprod, 2 * TT - 1 + g - G_LAT
            if g <= G_GATE:
                return s_latm, TT
            if g == G_GATE + 1:
                return s_latm, 2 * TT
            return s_proj, CA * NP + NH * (g - G_D + 1)

        def last_reader_d(h):
            if isinstance(h, int) and h < 0:
                return last_reader(G_D + 1)
            return s_proj2, CD * (h + 1)

        OUT_A = [(slice(0, P), SEQ, SMP), (slice(0, HD), 0, SEQ), (slice(HD, P), 0, SEQ)]

        def gt_pair(t, p):
            return t[:, bass.ds(p * TOK, TOK)]

        def turned(t, tile, n, k=KL, width=LT * P):
            return t[:, 0:k * width].rearrange("p (k c) -> p k c", k=k)[:, :, tile * P:tile * P + n]

        @block.scalar
        def _(act):
            def split_piece(g, j, slot, cols):
                n = cols // PIECES
                if j == 0:
                    act.wait_ge(s_raw, 64 * (g + 1))
                c = slice(j * n, (j + 1) * n)
                nc.scalar.activation(whi[slot][:, c], raw[:, c], ACT.Copy).then_inc(s_hi, 1)

            def split_group(g):
                if g > 1:
                    sem, n = last_reader(g)
                    act.wait_ge(sem, n)
                for j in range(PIECES):
                    split_piece(g, j, g % 2, COLS[g])

            for t in range(TT):
                n = P if t < NT else SMP
                act.wait_ge(s_x_in[t], 16)
                if begun(t):
                    act.wait_ge(s_row_ss, t)
                nc.scalar.activation(dump_x[0:n, :], x_in[0:n, t, :], ACT.Square,
                                     accum_out=row_ss[0:n, 0, t:t + 1]).then_inc(s_row_ss, 1)
            act.wait_ge(s_gcol_t, 1)
            nc.scalar.activation(g_col[:, :, :].rearrange("p m k -> p (m k)"), XB[:, 0:3 * KD],
                                 ACT.Copy).then_inc(s_gcol, 1)
            act.wait_ge(s_gcol, 1)
            split_group(0)
            for K in range(KD):
                act.wait_ge(s_xt, K + 1)
                gain = g_col[:, 0, K:K + 1]
                nc.scalar.activation(ht[0][:, K * TOK:K * TOK + SEQ], bank[4 + K % 2][:, :], ACT.Copy, scale=gain)
                nc.scalar.activation(ht[0][:, K * TOK + SEQ:(K + 1) * TOK], bank[6 + K % 2][:, 0:SMP], ACT.Copy,
                                     scale=gain).then_inc(s_xt_hi, 1)

            def chunk_a(q, par, c):
                b = PRJ[(par + c) % 2]
                act.wait_ge(s_proj, CA * q + c + 1)
                if begun(TT * q + c):
                    act.wait_ge(s_msq_d, TT * q + c)
                if c == 0:
                    if begun(CA * q):
                        act.wait_ge(s_dve_c, CA * q)
                nc.scalar.activation(sq[:, :], b[:, 0:2 * P], ACT.Square).then_inc(s_sqd, 1)
                if c == 0:
                    if begun(3 * (q - 1)):
                        act.wait_ge(s_av, 3 * (q - 1))
                    if begun(16 * (q - par)):
                        act.wait_ge(s_vout[par], 16 * (q - par))
                nc.scalar.activation(vtok[:, par, c, :], b[:, 2 * P:3 * P], ACT.Copy).then_inc(s_act_c, 1)

            def gate_a(q, par, j):
                c = TT + j
                act.wait_ge(s_proj, CA * q + c + 1)
                act.wait_ge(s_dve_c, CA * q + c)
                act.wait_ge(s_normed, TT * (q + 1))
                nc.scalar.activation(sigm[:, :], PRJ[(par + c) % 2][:, 0:HALF], ACT.Sigmoid).then_inc(s_act_c, 1)

            def xev_a(q, par, t):
                n = P if t < NT else SMP
                act.wait_ge(s_xpose, XA * q + t + 1)
                nc.scalar.activation(qkt[:, par, :, t * P:t * P + n],
                                     XB[:, 0:2 * P].rearrange("p (m c) -> p m c", m=2)[:, :, 0:n],
                                     ACT.Copy).then_inc(s_xev, 1)

            def zev_a(q, par):
                act.wait_ge(s_xpose, XA * (q + 1))
                nc.scalar.activation(kct[:, par, :], XB[:, 0:P], ACT.Copy).then_inc(s_xev, 1)

            def stay_a(p, par, u):
                ub = (par + u) % 2
                act.wait_ge(s_score, UA * p + u + 1)
                if begun(UA * p + u - 1):
                    act.wait_ge(s_left, UA * p + u - 1)
                r, n = (2 * SMP, SKEY) if u == 0 else (P, (UNIT_A[u][1] + 1) * P)
                nc.scalar.activation(stay[0:r, ub, SEQ - n:SEQ], SCR[ub][0:r, 0:n], ACT.Sigmoid,
                                     scale=-1.0).then_inc(s_stay, 1)

            def wtev_a(p, par, u):
                ub = (par + u) % 2
                act.wait_ge(s_tr, UA * p + u + 1)
                if u == 0:
                    if begun(3 * p - 2):
                        act.wait_ge(s_av, 3 * p - 2)
                    nc.scalar.activation(wts[:, :, :],
                                         TRB[ub][:, 0:2 * P].rearrange("p (j c) -> p j c", j=2)[:, :, 0:2 * SMP],
                                         ACT.Copy).then_inc(s_wtev, 1)
                    return
                h, i = UNIT_A[u]
                if i == NT - 1:
                    if begun(3 * p + 2 * h):
                        act.wait_ge(s_av, 3 * p + 2 * h)
                nc.scalar.activation(wt[:, 0:i + 1, i * P:(i + 1) * P],
                                     TRB[ub][:, 0:(i + 1) * P].rearrange("p (j c) -> p j c", j=i + 1),
                                     ACT.Copy).then_inc(s_wtev, 1)

            def out_hi(p):
                act.wait_ge(s_odone, 3 * (p + 1))
                nc.scalar.activation(gt_pair(gt[0], p), gated[:, :], ACT.Copy).then_inc(s_ghi, 1)

            def step_a(p, par, att=True, ahead=True):
                for what, n in STEP_A:
                    if what in AHEAD:
                        if not ahead:
                            continue
                        q, qpar = p + 1, 1 - par
                        if what == "C":
                            chunk_a(q, qpar, n)
                        elif what == "G":
                            gate_a(q, qpar, n)
                        elif what == "X":
                            xev_a(q, qpar, n)
                        elif what == "Z":
                            zev_a(q, qpar)
                    elif what == "W":
                        if n == 0 and not (isinstance(p, int) and p < 0):
                            sem, count = last_reader(p + 2)
                            act.wait_ge(sem, count)
                        split_piece(p + 2, n, par, KD * 512)
                    elif att:
                        if what == "S":
                            stay_a(p, par, n)
                        elif what == "T":
                            wtev_a(p, par, n)
                        elif what == "O" and n == 2:
                            out_hi(p)

            step_a(-1, 1, att=False)
            step_a(0, 0)
            with act.Fori(0, 3) as i:
                step_a(2 * i + 1, 1)
                step_a(2 * i + 2, 0)
            step_a(7, 1, ahead=False)

            for t in range(TT):
                n = P if t < NT else SMP
                if t == NT:
                    split_group(G_LAT)
                act.wait_ge(s_x2sum, 2 * (t + 1))
                act.wait_ge(s_row_ss, TT + t)
                nc.scalar.activation(dump[0:n, :], x2[0:n, t, :], ACT.Square,
                                     accum_out=row_ss[0:n, 1, t:t + 1]).then_inc(s_row_ss, 1)

            for K in range(KD):
                act.wait_ge(s_ct, K + 1)
                for m, dst in ((1, gt[0]), (2, ht[0])):
                    gain = g_col[:, m, K:K + 1]
                    nc.scalar.activation(dst[:, K * TOK:K * TOK + SEQ], bank[4 + K % 2][:, :], ACT.Copy, scale=gain)
                    last = nc.scalar.activation(dst[:, K * TOK + SEQ:(K + 1) * TOK], bank[6 + K % 2][:, 0:SMP],
                                                ACT.Copy, scale=gain)
                last.then_inc(s_ct_hi, 1)
            split_group(G_KPE)

            def lat_hi(t):
                act.wait_ge(s_latx, t + 1)
                nc.scalar.activation(turned(latt[0], t, P), bank[4][:, :].rearrange("p (k c) -> p k c", k=KL),
                                     ACT.Copy).then_inc(s_lat_hi, 1)
                c0, n = [(t * P, P), (SEQ, SMP), (TOK, P)][max(0, t - NT + 1)]
                nc.scalar.activation(kpet[:, c0:c0 + n], bank[5][:, 0:n], ACT.Copy).then_inc(s_kpet_e, 1)

            def qa_hi(t):
                n = P if t < NT else SMP
                act.wait_ge(s_latx, LT + t + 1)
                nc.scalar.activation(turned(qat[0], t, n, width=TOK),
                                     bank[4][:, :].rearrange("p (k c) -> p k c", k=KL)[:, :, 0:n],
                                     ACT.Copy).then_inc(s_lat_hi, 1)

            for t in range(TT):
                act.wait_ge(s_latm, t + 1)
                if begun(t):
                    act.wait_ge(s_lat_ss, t)
                nc.scalar.activation(sqc[:, :], bank[t % 2][:, :], ACT.Square, accum_out=lat_ss[:, t, 0:1])
                nc.scalar.activation(sq_pe[:, :], bank[2 + t % 2][:, 0:ROPE], ACT.Square,
                                     accum_out=lat_ss[:, t, 1:2]).then_inc(s_lat_ss, 1)
                if t:
                    lat_hi(t - 1)
            split_group(G_QA)
            lat_hi(TT - 1)
            lat_hi(TT)
            for t in range(TT):
                act.wait_ge(s_latm, TT + t + 1)
                act.wait_ge(s_lat_ss, TT + t)
                nc.scalar.activation(sqc[:, :], bank[(TT + t) % 2][:, :], ACT.Square,
                                     accum_out=lat_ss[:, TT + t, 0:1]).then_inc(s_lat_ss, 1)
                if t:
                    qa_hi(t - 1)
                if t == 2:
                    split_group(G_GATE)
            split_group(G_GATE + 1)
            for n in range(2 * NH):
                act.wait_ge(s_proj, CA * NP + n + 1)
                act.wait_ge(s_dve_c, CA * NP + n)
                act.wait_ge(s_lat_ss, 2 * TT)
                nc.scalar.activation(sigc[:, :], bank[2 + n % 2][:, 0:HALF], ACT.Sigmoid).then_inc(s_act_c, 1)
                if n == 0:
                    qa_hi(TT - 1)
                if n == NH:
                    split_group(G_D)

            def chunk_d(q, par, what, t):
                c = CHUNK_D[what, t]
                b, sl = PRJ[(par + c) % 2], (par + c) % 2
                act.wait_ge(s_proj2, CD * q + c + 1)
                if begun(CD * q + c):
                    act.wait_ge(s_act2, CD * q + c)
                if begun(MEANS * q + MEAN_D[c] - 1):
                    act.wait_ge(s_mean2, MEANS * q + MEAN_D[c] - 1)
                mm = nc.scalar.activation(sqd[:, 0:NOPE], b[:, 0:NOPE], ACT.Square, accum_out=ssq[:, sl, 0:1])
                if what == "Q":
                    mm = nc.scalar.activation(sq_pe[:, :], b[:, NOPE:QK], ACT.Square, accum_out=ssq[:, sl, 1:2])
                mm.then_inc(s_act2, 1)

            def turn_d(q, par, what, t):
                x = XPOSE_D[what, t]
                act.wait_ge(s_xp2, CD * q + x + 1)
                if what == "X":
                    n = P if t < NT else SMP
                    nc.scalar.activation(q2t[:, par, :, t * P:t * P + n],
                                         XB[:, 0:2 * P].rearrange("p (m c) -> p m c", m=2)[:, :, 0:n],
                                         ACT.Copy).then_inc(s_xev2, 1)
                else:
                    c0, n = [(t * P, P), (SEQ, SMP), (TOK, P)][max(0, t - NT + 1)]
                    nc.scalar.activation(k2t[:, par, c0:c0 + n], XB[:, 0:n], ACT.Copy).then_inc(s_xev2, 1)

            def exp_d(h, par, u):
                ub = (par + u) % 2
                act.wait_ge(s_negmax, UD * h + u + 1)
                if begun(UD * h + u - 1):
                    act.wait_ge(s_tr2, UD * h + u - 1)
                r, n = (SMP, SKEY) if u == 0 else (P, (NT - u + 1) * P)
                nc.scalar.activation(prob[0:r, ub, 0:n], SCR[ub][0:r, 0:n], ACT.Exp, bias=neg_max[0:r, ub:ub + 1],
                                     accum_out=p_sum[0:r, ub:ub + 1]).then_inc(s_expd, 1)

            def wtev_d(h, par, u):
                ub = (par + u) % 2
                act.wait_ge(s_tr2, UD * h + u + 1)
                if u == 0:
                    if begun(2 * h - 1):
                        act.wait_ge(s_av2, 2 * h - 1)
                    nc.scalar.activation(wts2[:, :, :],
                                         TRB[ub][:, 0:2 * P].rearrange("p (j c) -> p j c", j=2)[:, :, 0:SMP],
                                         ACT.Copy).then_inc(s_wtev2, 1)
                    return
                i = NT - u
                if i == NT - 1:
                    if begun(2 * h):
                        act.wait_ge(s_av2, 2 * h)
                nc.scalar.activation(wt2[:, 0:i + 1, i * P:(i + 1) * P],
                                     TRB[ub][:, 0:(i + 1) * P].rearrange("p (j c) -> p j c", j=i + 1),
                                     ACT.Copy).then_inc(s_wtev2, 1)

            def step_d(h, par, att=True, ahead=True):
                for what, n in STEP_D:
                    if what in AHEAD:
                        if not ahead:
                            continue
                        q, qpar = h + 1, 1 - par
                        if what in "QK":
                            chunk_d(q, qpar, what, n)
                        else:
                            turn_d(q, qpar, what, n)
                    elif what == "W":
                        g, cols = h + G_D + 2, COLS[G_D]
                        if isinstance(h, int) and g >= G_OB:
                            cols = COLS[g]
                        if n == 0:
                            sem, count = last_reader_d(h)
                            act.wait_ge(sem, count)
                        split_piece(g, n, (G_D + par) % 2, cols)
                    elif att:
                        if what == "S":
                            exp_d(h, par, n)
                        elif what == "T":
                            wtev_d(h, par, n)

            step_d(-1, 1, att=False)
            step_d(0, 0)
            with act.Fori(0, 2) as i:
                step_d(2 * i + 1, 1)
                step_d(2 * i + 2, 0)
            step_d(5, 1)
            step_d(6, 0)
            step_d(7, 1, ahead=False)

            act.wait_ge(s_od2, 2 * NH)
            for K in range(KD):
                nc.scalar.activation(ht[0][:, K * TOK:(K + 1) * TOK], sg[:, K, :], ACT.Copy).then_inc(s_go_hi, 1)
            for t in range(TT):
                n = P if t < NT else SMP
                act.wait_ge(s_ysum, 2 * (t + 1))
                act.wait_ge(s_row_ss, 2 * TT + t)
                nc.scalar.activation(dump2[0:n, :], x2e[0:n, t, :], ACT.Square,
                                     accum_out=row_ss[0:n, 2, t:t + 1]).then_inc(s_row_ss, 1)

        @block.gpsimd
        def _(pool):
            def split_piece(g, j, slot, cols):
                n = cols // PIECES
                c = slice(j * n, (j + 1) * n)
                pool.wait_ge(s_hi, PIECES * g + j + 1)
                nc.gpsimd.tensor_tensor(wlo[slot][:, c], raw[:, c], whi[slot][:, c].bitcast(F32),
                                        ALU.subtract).then_inc(s_lo, 1)

            def split_group(g):
                if g > 1:
                    sem, n = last_reader(g)
                    pool.wait_ge(sem, n)
                for j in range(PIECES):
                    split_piece(g, j, g % 2, COLS[g])

            def rms_rows(phase, t):
                n = P if t < NT else SMP
                k = TT * phase + t
                pool.wait_ge(s_row_ss, k + 1)
                nc.gpsimd.tensor_scalar(row_ms[0:n, phase, t:t + 1], row_ss[0:n, phase, t:t + 1], 1.0 / D, EPS,
                                        ALU.mult, ALU.add).then_inc(s_row_ms, 1)
                pool.wait_ge(s_row_ms, k + 1)
                nc.gpsimd.tensor_tensor(row_r[0:n, phase, t:t + 1], row_ms[0:n, phase, t:t + 1],
                                        neg_half[0:n, 0:1], ALU.pow).then_inc(s_row_r, 1)

            nc.gpsimd.memset(neg_half[:, :], -0.5).then_inc(s_masks, 1)
            nc.gpsimd.memset(ident[:, :], 0.0).then_inc(s_pad, 1)
            pool.wait_ge(s_pad, 1)
            nc.gpsimd.affine_select(out=ident[:, :], in_=ident[:, :], compare_op=ALU.not_equal, fill=1.0,
                                    base=0, pattern=[[-1, P]], channel_multiplier=1).then_inc(s_masks, 1)
            nc.gpsimd.memset(ht[0][:, KD * TOK:FLAT].bitcast(F32), 0.0).then_inc(s_pad, 1)
            nc.gpsimd.memset(ht[1][:, KD * TOK:FLAT].bitcast(F32), 0.0).then_inc(s_pad, 1)
            nc.gpsimd.memset(wgt[:, :, :], 0.0).then_inc(s_pad, 1)
            for t in range(TT):
                rms_rows(0, t)
            pool.wait_ge(s_masks, 2)
            nc.gpsimd.tensor_copy(ident_b[:, :], ident[:, :]).then_inc(s_masks, 1)
            nc.gpsimd.memset(causal[:, :], 0.0).then_inc(s_zeros_m, 1)
            nc.gpsimd.memset(causal_s[:, :], 0.0).then_inc(s_zeros_m, 1)
            nc.gpsimd.memset(chunk_mask[:, :], 0.0).then_inc(s_zeros_m, 1)
            pool.wait_ge(s_zeros_m, 3)
            nc.gpsimd.affine_select(out=causal[:, :], in_=causal[:, :], compare_op=ALU.is_gt, fill=BIG,
                                    base=0, pattern=[[-1, P]], channel_multiplier=1).then_inc(s_masks, 1)
            for h in range(2):
                r = slice(h * SMP, (h + 1) * SMP)
                pool.wait_ge(s_masks, 4 + h)
                nc.gpsimd.affine_select(out=causal_s[r, :], in_=causal_s[r, :], compare_op=ALU.is_gt, fill=BIG,
                                        base=0, pattern=[[-1, SMP]], channel_multiplier=1).then_inc(s_masks, 1)
            pool.wait_ge(s_masks, 6)
            nc.gpsimd.memset(chunk_mask[0:HD, HD:P], BIG).then_inc(s_masks, 1)
            split_group(0)

            def rms_a(q, par, c):
                sl = (par + c) % 2
                pool.wait_ge(s_mean, TT * q + c + 1)
                nc.gpsimd.tensor_tensor(rstd[:, sl, :], msq[:, sl, :], neg_half[:, :], ALU.pow).then_inc(s_rs, 1)

            def out_lo(p):
                pool.wait_ge(s_ghi, p + 1)
                nc.gpsimd.tensor_tensor(gt_pair(gt[1], p), gated[:, :], gt_pair(gt[0], p).bitcast(F32),
                                        ALU.subtract).then_inc(s_glo, 1)

            def step_a(p, par, att=True, ahead=True):
                for what, n in STEP_A:
                    if what == "C" and ahead:
                        rms_a(p + 1, 1 - par, n)
                    elif what == "W":
                        if n == 0 and not (isinstance(p, int) and p < 0):
                            sem, count = last_reader(p + 2)
                            pool.wait_ge(sem, count)
                        split_piece(p + 2, n, par, KD * 512)
                    elif (what, n) == ("O", 2) and att:
                        out_lo(p)

            step_a(-1, 1, att=False)
            step_a(0, 0)
            with pool.Fori(0, 3) as i:
                step_a(2 * i + 1, 1)
                step_a(2 * i + 2, 0)
            step_a(7, 1, ahead=False)

            nc.gpsimd.memset(gt[0][:, KD * TOK:FLAT].bitcast(F32), 0.0).then_inc(s_zeros_b, 1)
            nc.gpsimd.memset(gt[1][:, KD * TOK:FLAT].bitcast(F32), 0.0).then_inc(s_zeros_b, 1)
            for t in range(TT):
                if t == NT:
                    split_group(G_LAT)
                rms_rows(1, t)

            pool.wait_ge(s_ct, KD)
            nc.gpsimd.memset(kpe[:, :, ROPE:P], 0.0).then_inc(s_zeros_c, 1)
            split_group(G_KPE)

            def rms_lat(n):
                pool.wait_ge(s_lat_ss, n + 1)
                nc.gpsimd.tensor_scalar(lat_ms[:, n, 0:1], lat_ss[:, n, 0:1], 1.0 / KV, EPS,
                                        ALU.mult, ALU.add).then_inc(s_lat_ms, 1)
                w = 1
                if n < TT:
                    nc.gpsimd.tensor_scalar(lat_ms[:, n, 1:2], lat_ss[:, n, 1:2], 1.0 / ROPE, EPS,
                                            ALU.mult, ALU.add).then_inc(s_lat_ms, 1)
                    w = 2
                pool.wait_ge(s_lat_ms, 2 * (n + 1) if n < TT else TT + n + 1)
                nc.gpsimd.tensor_tensor(lat_r[:, n, 0:w], lat_ms[:, n, 0:w], neg_half[:, 0:w],
                                        ALU.pow).then_inc(s_lat_r, 1)

            for t in range(TT):
                rms_lat(t)
            split_group(G_QA)
            for m in range(2):
                pool.wait_ge(s_latm, TT)
                nc.gpsimd.memset(qat[m][:, KL * TOK:QFLAT].bitcast(F32), 0.0).then_inc(s_zeros_d, 1)
            for t in range(TT):
                rms_lat(TT + t)
                if t == 2:
                    split_group(G_GATE)
            split_group(G_GATE + 1)
            split_group(G_D)

            pool.wait_ge(s_proj, CA * NP + 2 * NH)
            nc.gpsimd.memset(prob[:, :, :], 0.0).then_inc(s_zeros_d, 1)
            pool.wait_ge(s_latout, 32 * TT)
            pool.wait_ge(s_kpet_e, LT)
            nc.gpsimd.memset(qn2[:, :, QK:2 * P], 0.0).then_inc(s_zeros_d, 1)

            def rms_d(q, par, what, t):
                c = CHUNK_D[what, t]
                sl = (par + c) % 2
                w = 2 if what == "Q" else 1
                pool.wait_ge(s_mean2, MEANS * q + MEAN_D[c + 1])
                nc.gpsimd.tensor_tensor(rstd[:, sl, 0:w], msq[:, sl, 0:w], neg_half[:, 0:w],
                                        ALU.pow).then_inc(s_rs2, 1)

            def step_d(h, par, ahead=True):
                for what, n in STEP_D:
                    if what in "QK" and ahead:
                        rms_d(h + 1, 1 - par, what, n)
                    elif what == "W":
                        g, cols = h + G_D + 2, COLS[G_D]
                        if isinstance(h, int) and g >= G_OB:
                            cols = COLS[g]
                        if n == 0:
                            sem, count = last_reader_d(h)
                            pool.wait_ge(sem, count)
                        split_piece(g, n, (G_D + par) % 2, cols)

            step_d(-1, 1)
            step_d(0, 0)
            with pool.Fori(0, 2) as i:
                step_d(2 * i + 1, 1)
                step_d(2 * i + 2, 0)
            step_d(5, 1)
            step_d(6, 0)
            step_d(7, 1, ahead=False)

            for m in range(2):
                pool.wait_ge(s_od2, 2 * NH)
                nc.gpsimd.memset(ht[m][:, KD * TOK:FLAT].bitcast(F32), 0.0).then_inc(s_zeros_e, 1)
            for K in range(KD):
                c = slice(K * TOK, (K + 1) * TOK)
                pool.wait_ge(s_go_hi, K + 1)
                nc.gpsimd.tensor_tensor(ht[1][:, c], sg[:, K, :], ht[0][:, c].bitcast(F32),
                                        ALU.subtract).then_inc(s_go_lo, 1)
            for t in range(TT):
                rms_rows(2, t)

        @block.vector
        def _(dve):
            v = nc.vector
            for t in range(TT):
                n = P if t < NT else SMP
                dve.wait_ge(s_row_r, t + 1)
                v.tensor_scalar(x_in[0:n, t, :], x_in[0:n, t, :], row_r[0:n, 0, t:t + 1], None,
                                ALU.mult).then_inc(s_xn, 1)
            dve.wait_ge(s_const_d, 16 * 13)
            v.tensor_scalar(g_qk[:, 0, :, :], g_qk[:, 0, :, :], HD ** -0.5, None, ALU.mult).then_inc(s_gscale, 1)
            v.tensor_scalar(g_q[:, :], g_q[:, :], QK ** -0.5, None, ALU.mult).then_inc(s_gscale, 1)
            v.memset(left[:, :, SEQ:SEQ + 1], 1.0).then_inc(s_gscale, 1)

            def low(dst, b, bs, K, gain, hi):
                c, e = slice(K * TOK, K * TOK + SEQ), slice(K * TOK + SEQ, (K + 1) * TOK)
                v.scalar_tensor_tensor(out=dst[:, c], in0=b[:, :], scalar=gain, in1=hi[:, c].bitcast(F32),
                                       op0=ALU.mult, op1=ALU.subtract)
                return v.scalar_tensor_tensor(out=dst[:, e], in0=bs[:, 0:SMP], scalar=gain, in1=hi[:, e].bitcast(F32),
                                              op0=ALU.mult, op1=ALU.subtract)

            dve.wait_ge(s_gcol, 1)
            for K in range(KD):
                dve.wait_ge(s_xt_hi, K + 1)
                low(ht[1], bank[4 + K % 2], bank[6 + K % 2], K, g_col[:, 0, K:K + 1], ht[0]).then_inc(s_xt_lo, 1)
            dve.wait_ge(s_gscale, 3)

            def chunk_a(q, par, c):
                sl = (par + c) % 2
                b = PRJ[sl]
                dve.wait_ge(s_sqd, TT * q + c + 1)
                if begun(TT * q + c - 1):
                    dve.wait_ge(s_rs, TT * q + c - 1)
                v.tensor_reduce(ssq[:, sl, :], sq[:, :].rearrange("p (a d) -> p a d", a=4), AX.X,
                                ALU.add).then_inc(s_msq_d, 1)
                dve.wait_ge(s_msq_d, TT * q + c + 1)
                v.tensor_scalar(msq[:, sl, :], ssq[:, sl, :], 1.0 / HD, EPS, ALU.mult, ALU.add).then_inc(s_mean, 1)
                dve.wait_ge(s_rs, TT * q + c + 1)
                dve.wait_ge(s_act_c, CA * q + c + 1)
                v.tensor_tensor(qkr[:, :].rearrange("p (a d) -> p a d", a=4),
                                b[:, 0:2 * P].rearrange("p (a d) -> p a d", a=4),
                                rstd[:, sl, :].unsqueeze(2).to_broadcast([P, 4, HD]), ALU.mult).then_inc(s_dve_c, 1)
                dve.wait_ge(s_dve_c, CA * q + c + 1)
                if c == 0:
                    if begun(XA * q):
                        dve.wait_ge(s_xpose, XA * q)
                    if begun(32 * q):
                        dve.wait_ge(s_kout, 32 * q)
                v.tensor_tensor(qkn[:, c, :, :].rearrange("p m d -> p (m d)"), qkr[:, :],
                                g_qk[:, :, :, :].rearrange("p m h d -> p (m h d)"), ALU.mult).then_inc(s_normed, 1)

            def gate_a(q, par, j):
                c = TT + j
                dve.wait_ge(s_act_c, CA * q + c + 1)
                v.tensor_tensor(sgate[:, par, j * HALF:(j + 1) * HALF], PRJ[(par + c) % 2][:, 0:HALF], sigm[:, :],
                                ALU.mult).then_inc(s_dve_c, 1)

            def weight_a(p, par, u):
                ub = (par + u) % 2
                dve.wait_ge(s_stay, UA * p + u + 1)
                r, n = (2 * SMP, SKEY) if u == 0 else (P, (UNIT_A[u][1] + 1) * P)
                back = stay[0:r, ub, SEQ - n:SEQ][:, ::-1]
                v.tensor_tensor_scan(out=left[0:r, ub, SEQ - n:SEQ][:, ::-1], data0=back, data1=back, initial=1.0,
                                     op0=ALU.mult, op1=ALU.bypass).then_inc(s_left, 1)
                dve.wait_ge(s_left, UA * p + u + 1)
                if begun(UA * p + u - 1):
                    dve.wait_ge(s_tr, UA * p + u - 1)
                v.tensor_tensor(wgt[0:r, ub, 0:n], left[0:r, ub, SEQ - n + 1:SEQ + 1], left[0:r, ub, SEQ - n:SEQ],
                                ALU.subtract).then_inc(s_wgt, 1)

            def gate_out(p, par, o):
                dve.wait_ge(s_av, 3 * p + o + 1)
                if o == 0:
                    if begun(p):
                        dve.wait_ge(s_ghi, p)
                    if begun(p):
                        dve.wait_ge(s_glo, p)
                r, c0, n = OUT_A[o]
                v.tensor_tensor(gated[r, c0:c0 + n], OUT[r, 0:n], sgate[r, par, c0:c0 + n], ALU.mult).then_inc(s_odone, 1)

            def step_a(p, par, att=True, ahead=True):
                for what, n in STEP_A:
                    if what == "C" and ahead:
                        chunk_a(p + 1, 1 - par, n)
                    elif what == "G" and ahead:
                        gate_a(p + 1, 1 - par, n)
                    elif what == "S" and att:
                        weight_a(p, par, n)
                    elif what == "O" and att:
                        gate_out(p, par, n)

            step_a(-1, 1, att=False)
            step_a(0, 0)
            with dve.Fori(0, 3) as i:
                step_a(2 * i + 1, 1)
                step_a(2 * i + 2, 0)
            step_a(7, 1, ahead=False)

            def norm_rows(t):
                n = P if t < NT else SMP
                dve.wait_ge(s_row_r, TT + t + 1)
                v.tensor_scalar(xn[0:n, t, :], x2[0:n, t, :], row_r[0:n, 1, t:t + 1], None,
                                ALU.mult).then_inc(s_xn, 1)

            for t in range(TT):
                n = P if t < NT else SMP
                dve.wait_ge(s_x2d[t], 16)
                for nh in range(2):
                    c = slice(nh * 512, (nh + 1) * 512)
                    m = 2 * t + nh
                    dve.wait_ge(s_yprod, m + 1)
                    v.tensor_tensor(x2[0:n, t, c], bank[m % 4][0:n, :], x2[0:n, t, c], ALU.add).then_inc(s_x2sum, 1)
                if t:
                    norm_rows(t - 1)
            norm_rows(TT - 1)

            for K in range(KD):
                dve.wait_ge(s_ct_hi, K + 1)
                for m, (dst, hi) in ((1, (gt[1], gt[0])), (2, (ht[1], ht[0]))):
                    last = low(dst, bank[4 + K % 2], bank[6 + K % 2], K, g_col[:, m, K:K + 1], hi)
                last.then_inc(s_ct_lo, 1)

            def rotary_norm(src, r, gain):
                v.scalar_tensor_tensor(out=pe_tmp[:, 0, :], in0=src, scalar=r, in1=gain, op0=ALU.mult,
                                       op1=ALU.mult).then_inc(s_rope, 1)

            def rotate(dst, t, n):
                dve.wait_ge(s_rope, 3 * n + 1)
                v.tensor_tensor(pe_tmp[:, 1, :].rearrange("p (h d) -> p h d", h=2),
                                pe_tmp[:, 0, :].rearrange("p (h d) -> p h d", h=2),
                                cos_t[:, t, :].unsqueeze(1).to_broadcast([P, 2, ROPE // 2]),
                                ALU.mult).then_inc(s_rope, 1)
                swapped = pe_tmp[:, 0, :].rearrange("p (h d) -> p h d", h=2)[:, ::-1, :]
                v.tensor_tensor(pe_tmp[:, 2, :].rearrange("p (h d) -> p h d", h=2), swapped,
                                sin_t[:, t, :].rearrange("p (h d) -> p h d", h=2), ALU.mult).then_inc(s_rope, 1)
                dve.wait_ge(s_rope, 3 * n + 3)
                return v.tensor_tensor(dst, pe_tmp[:, 1, :], pe_tmp[:, 2, :], ALU.add)

            def lat_lo(t):
                dve.wait_ge(s_lat_hi, t + 1)
                v.tensor_tensor(turned(latt[1], t, P), bank[4][:, :].rearrange("p (k c) -> p k c", k=KL),
                                turned(latt[0], t, P).bitcast(F32), ALU.subtract).then_inc(s_lat_lo, 1)

            def qa_lo(t):
                n = P if t < NT else SMP
                dve.wait_ge(s_lat_hi, LT + t + 1)
                v.tensor_tensor(turned(qat[1], t, n, width=TOK),
                                bank[4][:, :].rearrange("p (k c) -> p k c", k=KL)[:, :, 0:n],
                                turned(qat[0], t, n, width=TOK).bitcast(F32), ALU.subtract).then_inc(s_lat_lo, 1)

            dve.wait_ge(s_rows_g, 32)
            for t in range(TT):
                dve.wait_ge(s_lat_r, t + 1)
                rotary_norm(bank[2 + t % 2][:, 0:ROPE], lat_r[:, t, 1:2], g_kp[:, :])
                v.scalar_tensor_tensor(out=lat[:, t, :], in0=bank[t % 2][:, :], scalar=lat_r[:, t, 0:1],
                                       in1=g_lat[:, :], op0=ALU.mult, op1=ALU.mult).then_inc(s_latn, 1)
                rotate(kpe[:, t, 0:ROPE], t, t).then_inc(s_kper, 1)
                if t:
                    lat_lo(t - 1)
            lat_lo(TT - 1)
            lat_lo(TT)
            for t in range(TT):
                dve.wait_ge(s_lat_r, TT + t + 1)
                dve.wait_ge(s_latx, LT + t)
                v.scalar_tensor_tensor(out=qan[:, :], in0=bank[(TT + t) % 2][:, :], scalar=lat_r[:, TT + t, 0:1],
                                       in1=g_qar[:, :], op0=ALU.mult, op1=ALU.mult).then_inc(s_latn, 1)
                if t:
                    qa_lo(t - 1)
            for n in range(2 * NH):
                dve.wait_ge(s_act_c, CA * NP + n + 1)
                v.tensor_tensor(sg[:, n // 2, (n % 2) * HALF:(n % 2 + 1) * HALF], bank[2 + n % 2][:, 0:HALF], sigc[:, :],
                                ALU.mult).then_inc(s_dve_c, 1)
                if n == 0:
                    qa_lo(TT - 1)

            dve.wait_ge(s_zeros_d, 4)

            def chunk_d(q, par, what, t):
                c = CHUNK_D[what, t]
                sl = (par + c) % 2
                b = PRJ[sl]
                dve.wait_ge(s_act2, CD * q + c + 1)
                v.tensor_scalar(msq[:, sl, 0:1], ssq[:, sl, 0:1], 1.0 / NOPE, EPS,
                                ALU.mult, ALU.add).then_inc(s_mean2, 1)
                if what == "Q":
                    v.tensor_scalar(msq[:, sl, 1:2], ssq[:, sl, 1:2], 1.0 / ROPE, EPS,
                                    ALU.mult, ALU.add).then_inc(s_mean2, 1)
                dve.wait_ge(s_rs2, CD * q + c + 1)
                if what == "Q":
                    if begun(CD * q + (XPOSE_D["X", t - 2] + 1 if t > 1 else 0)):
                        dve.wait_ge(s_xp2, CD * q + (XPOSE_D["X", t - 2] + 1 if t > 1 else 0))
                    rotary_norm(b[:, NOPE:QK], rstd[:, sl, 1:2], g_q[:, NOPE:QK])
                    v.scalar_tensor_tensor(out=qn2[:, t % 2, 0:NOPE], in0=b[:, 0:NOPE], scalar=rstd[:, sl, 0:1],
                                           in1=g_q[:, 0:NOPE], op0=ALU.mult, op1=ALU.mult).then_inc(s_dve2, 1)
                    rotate(qn2[:, t % 2, NOPE:QK], t, TT * (q + 1) + t).then_inc(s_nrm2, 1)
                else:
                    if begun(CD * q + (XPOSE_D["Y", t - 2] + 1 if t > 1 else 0)):
                        dve.wait_ge(s_xp2, CD * q + (XPOSE_D["Y", t - 2] + 1 if t > 1 else 0))
                    if t == 0:
                        if begun(2 * (q - 1)):
                            dve.wait_ge(s_av2, 2 * (q - 1))
                    v.tensor_copy(v2[:, par, t, :], b[:, NOPE:256])
                    v.scalar_tensor_tensor(out=kn2[:, t % 2, :], in0=b[:, 0:NOPE], scalar=rstd[:, sl, 0:1],
                                           in1=g_kn[:, :], op0=ALU.mult, op1=ALU.mult).then_inc(s_dve2, 1)

            def soft_d(h, par, u):
                ub = (par + u) % 2
                r, n = (SMP, SKEY) if u == 0 else (P, (NT - u + 1) * P)
                dve.wait_ge(s_score2, UD * h + u + 1)
                v.tensor_reduce(neg_max[0:r, ub:ub + 1], SCR[ub][0:r, 0:n], AX.X, ALU.max,
                                negate=True).then_inc(s_negmax, 1)
                dve.wait_ge(s_expd, UD * h + u + 1)
                v.reciprocal(p_inv[0:r, ub:ub + 1], p_sum[0:r, ub:ub + 1]).then_inc(s_inv, 1)
                dve.wait_ge(s_inv, UD * h + u + 1)
                v.tensor_scalar(prob[0:r, ub, 0:n], prob[0:r, ub, 0:n], p_inv[0:r, ub:ub + 1], None,
                                ALU.mult).then_inc(s_scaled, 1)

            def gate_out_d(h, o):
                dve.wait_ge(s_av2, 2 * h + o + 1)
                c0, n = ((SEQ, SMP), (0, SEQ))[o]
                at_h = sg_flat[:, bass.ds(h * TOK + c0, n)]
                v.tensor_tensor(at_h, OUT[:, 0:n], at_h, ALU.mult).then_inc(s_od2, 1)

            def step_d(h, par, att=True, ahead=True):
                for what, n in STEP_D:
                    if what in "QK" and ahead:
                        chunk_d(h + 1, 1 - par, what, n)
                    elif what == "S" and att:
                        soft_d(h, par, n)
                    elif what == "O" and att:
                        gate_out_d(h, n)

            step_d(-1, 1, att=False)
            step_d(0, 0)
            with dve.Fori(0, 3) as i:
                step_d(2 * i + 1, 1)
                step_d(2 * i + 2, 0)
            step_d(7, 1, ahead=False)

            def norm_y(t):
                n = P if t < NT else SMP
                dve.wait_ge(s_row_r, 2 * TT + t + 1)
                v.scalar_tensor_tensor(out=x2e[0:n, t, :], in0=x2e[0:n, t, :], scalar=row_r[0:n, 2, t:t + 1],
                                       in1=g_fin[0:n, :], op0=ALU.mult, op1=ALU.mult).then_inc(s_yn, 1)

            dve.wait_ge(s_gfin, 16)
            for t in range(TT):
                n = P if t < NT else SMP
                dve.wait_ge(s_x2in[t], 16)
                for nh in range(2):
                    c = slice(nh * 512, (nh + 1) * 512)
                    m = 2 * t + nh
                    dve.wait_ge(s_yprod, 2 * TT + m + 1)
                    v.tensor_tensor(x2e[0:n, t, c], bank[m % 4][0:n, :], x2e[0:n, t, c], ALU.add).then_inc(s_ysum, 1)
                if t:
                    norm_y(t - 1)
            norm_y(TT - 1)


_INS = ["x_prompt", "x_sample", "cache_sb_k", "cache_sb_v", "cache_mla_latent", "cache_mla_kpe", "g_pre_a",
        "w_in_a", "g_q_a", "g_k_a", "w_o_a", "g_kv", "w_kv_a", "g_kv_a", "g_kpe", "w_kv_b", "g_knope", "g_pre_b",
        "w_in_b", "g_qa", "w_q_b", "g_qn", "g_qp", "w_o_b", "g_final"]
_OUTS = [(1, SEQ, D), (1, SMP, D), (1, 1, SEQ, 16, HD), (1, 1, SEQ, 16, HD), (1, SEQ, KV), (1, SEQ, ROPE),
         (1, 1, SMP, 16, HD), (1, 1, SMP, 16, HD), (1, SMP, KV), (1, SMP, ROPE)]


def kernel(**inputs):
    import concourse.bacc as bacc
    from concourse.bass_utils import run_bass_kernel_spmd

    nc = bacc.Bacc("TRN2", target_bir_lowering=False, num_devices=1)
    cos, sin = rope_tables()
    arrays = {f"in_{n}": np.ascontiguousarray(inputs[n]) for n in _INS}
    arrays["in_rope_cos"], arrays["in_rope_sin"] = cos, sin
    a = {n[3:]: nc.dram_tensor(n, v.shape, F32, kind="ExternalInput").ap() for n, v in arrays.items()}
    out = [nc.dram_tensor(f"out_{i}", sh, F32, kind="ExternalOutput").ap() for i, sh in enumerate(_OUTS)]
    scratch = nc.dram_tensor("x2_scratch", (TT * P, D), F32, kind="Internal").ap()
    build(nc, a, out, scratch)
    r = run_bass_kernel_spmd(nc, [arrays], core_ids=[0])
    return tuple(r.results[0][f"out_{i}"] for i in range(len(_OUTS)))
```

```python
from contextlib import ExitStack

import numpy as np

import concourse.bass as bass
from concourse import mybir

F32 = mybir.dt.float32
F32R = mybir.dt.float32r
BF16 = mybir.dt.bfloat16
ALU = mybir.AluOpType
ACT = mybir.ActivationFunctionType
AX = mybir.AxisListType

P = 128
D = 1024
KD = D // P
SEQ, SMP, PAST = 512, 32, 128
NT = SEQ // P
TT = NT + 1
TOK = SEQ + SMP
HALF = TOK // 2
FLAT = KD * TOK + P - SMP
HD = 64
NP = D // P
KV = 512
KL = KV // P
QFLAT = KL * TOK + P - SMP
NH = 8
MP = NH // 2
NOPE, ROPE, VD = 128, 64, 128
QK = NOPE + ROPE
WQ, WK = 2 * QK, 2 * (NOPE + VD)
WD = WQ + WK
LT = TT + 1
KEYS = TOK + PAST
SKEY = SMP + PAST
EPS = 1e-6
BIG = -1e30

G_OA, G_LAT, G_KPE, G_QA, G_GATE, G_D, G_OB = NP, NP + 2, NP + 3, NP + 4, NP + 5, NP + 7, NP + 7 + MP
LA = 320
LB = KV + ROPE - LA
PIECES = 4
COLS = {g: KD * 512 for g in range(G_OB + 2)}
COLS[G_LAT], COLS[G_KPE] = KD * LA, KD * LB
for _g in range(G_D, G_OB):
    COLS[_g] = KL * WD

UA = 1 + 2 * NT
UNIT_A = [None] + [(h, i) for h in range(2) for i in reversed(range(NT))]
CA = TT + 2
XA = TT + 1
STEP_A = [("S", 0), ("S", 1), ("C", 0), ("W", 0), ("T", 0), ("S", 2), ("C", 1), ("W", 1), ("T", 1), ("X", 0),
          ("O", 0), ("S", 3), ("C", 2), ("W", 2), ("T", 2), ("X", 1), ("S", 4), ("C", 3), ("W", 3), ("T", 3),
          ("X", 2), ("S", 5), ("C", 4), ("T", 4), ("X", 3), ("S", 6), ("G", 0), ("O", 1), ("T", 5), ("X", 4),
          ("S", 7), ("T", 6), ("Z", 0), ("S", 8), ("G", 1), ("T", 7), ("T", 8), ("O", 2)]
ORDER = [NT] + list(range(NT))
CD = TT + LT
CHUNKS = [(w, t) for t in range(LT) for w in "QK" if (w, t) != ("Q", TT)]
CHUNK_D = {s: n for n, s in enumerate(CHUNKS)}
TURN = {"Q": "X", "K": "Y"}
STEP_D = []
for _j, (_w, _t) in enumerate(CHUNKS):
    STEP_D.append((_w, _t))
    if _j == 0:
        STEP_D.append(("P", TT))
    if 1 <= _j <= UA:
        STEP_D.append(("S", _j - 1))
    STEP_D.append(("N", _j))
    if _j in (3, 5, 7, 9):
        STEP_D.append(("W", (_j - 3) // 2))
    if 1 <= _j <= UA:
        STEP_D.append(("R", _j - 1))
    if _j == 3:
        STEP_D.append(("O", 0))
    if _j == 3 + NT:
        STEP_D.append(("O", 1))
    if _j >= 2:
        STEP_D.append(("T", _j - 2))
    if _j:
        STEP_D.append((TURN[CHUNKS[_j - 1][0]], CHUNKS[_j - 1][1]))
STEP_D.append(("O", 2))
AHEAD = {"C", "G", "X", "Z", "Q", "K", "Y", "N"}


def rope_tables():
    half = ROPE // 2
    inv = np.float32(10000.0) ** (-np.arange(half, dtype=np.float32) / np.float32(half))
    pos = np.zeros(TT * P, np.float32)
    pos[:SEQ] = np.arange(SEQ)
    pos[SEQ:TOK] = PAST + np.arange(SMP)
    ang = (pos[:, None] * inv[None, :].astype(np.float32)).astype(np.float32)
    cos, sin = np.cos(ang).astype(np.float32), np.sin(ang).astype(np.float32)
    return cos, np.concatenate([-sin, sin], 1)


def build(nc, a, out, scratch):
    x_p = a["x_prompt"][0].rearrange("(t p) d -> p t d", p=P)
    x_s = a["x_sample"][0]
    w_in = a["w_in_a"][0].rearrange("(k p) (f m) -> p k f m", p=P, f=4)
    w_oa = a["w_o_a"][0].rearrange("(k p) n -> p k n", p=P)
    w_ob = a["w_o_b"][0].rearrange("(k p) n -> p k n", p=P)
    w_kva = a["w_kv_a"].rearrange("(k p) n -> p k n", p=P)
    w_inb = a["w_in_b"][0].rearrange("(k p) n -> p k n", p=P)
    w_qb = a["w_q_b"][0].rearrange("(k p) n -> p k n", p=P)
    w_kvb = a["w_kv_b"].rearrange("(k p) n -> p k n", p=P)
    ck = a["cache_sb_k"][0, 0].rearrange("t h d -> t (h d)")
    cv = a["cache_sb_v"][0, 0].rearrange("t h d -> t (h d)")
    y_p, y_s, k_p, v_p, lat_p, kpe_p, k_s, v_s, lat_s, kpe_s = out
    ko_p = k_p[0, 0].rearrange("(t p) h d -> p t (h d)", p=P)
    vo_p = v_p[0, 0].rearrange("(t p) h d -> p t (h d)", p=P)
    ko_s = k_s[0, 0].rearrange("p h d -> p (h d)")
    vo_s = v_s[0, 0].rearrange("p h d -> p (h d)")

    with ExitStack() as ctx:
        base = (nc.sbuf_base + 63) // 64 * 64
        arena = nc.sbuf_usable_end - base
        at = [0]

        def place(name, shape, dt, off=None):
            size = int(np.prod(shape[1:])) * (2 if dt == BF16 else 4)
            size = (size + 31) // 32 * 32
            o = at[0] if off is None else off
            if off is None:
                at[0] += size
            assert o + size <= arena, (name, o + size, arena)
            return nc.alloc_sbuf_tensor_at(name, shape, dt, offset=base + o), o + size

        def keep(name, shape, dt=F32):
            return place(name, shape, dt)[0]

        def alias(name, shape, off, dt=F32):
            return place(name, shape, dt, off)

        ident = keep("ident", [P, P])
        ident_b = keep("ident_b", [P, P], BF16)
        causal = keep("causal", [P, P], BF16)
        causal_s = keep("causal_s", [P, SMP], BF16)
        chunk_mask = keep("chunk_mask", [P, P], BF16)
        g_qk = keep("g_qk", [P, 2, 2, HD])
        g_q = keep("g_q", [P, QK])
        g_kn = keep("g_kn", [P, NOPE])
        g_kp = keep("g_kp", [P, ROPE])
        g_col = keep("g_col", [P, 3, KD])
        cos_t = keep("cos_t", [P, TT, ROPE // 2])
        sin_t = keep("sin_t", [P, TT, ROPE])
        neg_half = keep("neg_half", [P, 4])
        lat_ss = keep("lat_ss", [P, 2 * TT, 3])
        lat_ms = keep("lat_ms", [P, 2 * TT, 2])
        lat_r = keep("lat_r", [P, 2 * TT, 2])
        sq_pe = keep("sq_pe", [P, ROPE])
        pe_tmp = keep("pe_tmp", [P, 3, ROPE])
        ssq = keep("ssq", [P, 2, 4])
        msq = keep("msq", [P, 2, 4])
        rstd = keep("rstd", [P, 2, 4])
        row_ss = keep("row_ss", [P, 3, TT])
        row_ms = keep("row_ms", [P, 3, TT])
        row_r = keep("row_r", [P, 3, TT])
        neg_max = keep("neg_max", [P, 2])
        p_sum = keep("p_sum", [P, 2])
        p_inv = keep("p_inv", [P, 2])
        raw = keep("raw", [P, KD * 512])
        whi = [keep(f"whi{s}", [P, KD * 512], F32R) for s in range(2)]
        wlo = [keep(f"wlo{s}", [P, KD * 512], F32R) for s in range(2)]
        o_ht = at[0]
        ht = [keep(f"ht{s}", [P, FLAT], F32R) for s in ("hi", "lo")]
        o_gt = at[0]
        gt = [keep(f"gt{s}", [P, FLAT], F32R) for s in ("hi", "lo")]
        o_s = at[0]
        x_in, _ = alias("x_in", [P, TT, D], o_gt)
        qkt, o = alias("qkt", [P, 2, 2, TOK], o_s)
        vtok, o = alias("vtok", [P, 2, TT, P], o)
        qkn, o = alias("qkn", [P, TT, 2, P], o)
        kc, o = alias("kc", [P, 2, P], o)
        vc, o = alias("vc", [P, 2, P], o)
        kct, o = alias("kct", [P, 2, P], o)
        sgate, o = alias("sgate", [P, 2, TOK], o)
        wt, o = alias("wt", [P, NT, SEQ], o)
        wts, o = alias("wts", [P, 2, 2 * SMP], o)
        stay, o = alias("stay", [P, 2, SEQ], o)
        left, o = alias("left", [P, 2, SEQ + 1], o)
        wgt, o = alias("wgt", [P, 2, SEQ], o)
        sigm, _ = alias("sigm", [P, HALF], o)
        sq, o = alias("sq", [P, 2 * P], o)
        qkr, o = alias("qkr", [P, 2 * P], o)
        gated, o = alias("gated", [P, TOK], o)
        dump_x, o = alias("dump_x", [P, D], o_s)
        g_rows, _ = alias("g_rows", [3 * KD, P], o)
        x2, o = alias("x2", [P, TT, D], o_s)
        xn, o = alias("xn", [P, TT, D], o)
        dump, _ = alias("dump", [P, D], o)
        lath, o = alias("lath", [P, KL * LT * P], o_s, F32R)
        latl, o = alias("latl", [P, KL * LT * P], o, F32R)
        kpet, o_d = alias("kpet", [P, KEYS], o)
        lat, o = alias("lat", [P, LT, KV], o_d)
        kpe, o = alias("kpe", [P, LT, P], o)
        qan, o = alias("qan", [P, KV], o)
        sigc, _ = alias("sigc", [P, HALF], o)
        sqc, o = alias("sqc", [P, KV], o)
        g_lat, o = alias("g_lat", [P, KV], max(o, o_s + 8 * TT * D))
        g_qar, o = alias("g_qar", [P, KV], o)
        qat0, o = alias("qat0", [P, QFLAT], o_gt, F32R)
        qat1, o = alias("qat1", [P, QFLAT], o, F32R)
        qat = [qat0, qat1]
        latt = [lath, latl]
        sg_flat, _ = alias("sg", [P, NH * TOK], o)
        sg = sg_flat[:, :].rearrange("p (h t) -> p h t", h=NH)
        q2t, o = alias("q2t", [P, 2, 3, TOK], o_ht)
        k2t, o = alias("k2t", [P, 2, 2, KEYS], o)
        wt2, o = alias("wt2", [P, NT, SEQ], o)
        sqd, o = alias("sqd", [P, WQ], o)
        pe_tmp2, o = alias("pe_tmp2", [P, 3, 2 * ROPE], o)
        assert o <= o_gt
        v2, o = alias("v2", [P, 2, 2, LT, P], o_d)
        qn2, o = alias("qn2", [P, 2, WQ], o)
        kn2, o = alias("kn2", [P, 2, 2 * NOPE], o)
        wts2, o = alias("wts2", [P, 2, 2 * SMP], o)
        prob, o = alias("prob", [P, 2, SEQ], o)
        x2e, o = alias("x2e", [P, TT, D], o_s)
        g_fin, o = alias("g_fin", [P, D], o)
        dump2, o = alias("dump2", [P, D], o)

        bank = [ctx.enter_context(nc.psum_tensor(f"bank{b}", [P, 512], F32)) for b in range(8)]
        LAB, QAB = [bank[2], bank[0], bank[1]], [bank[1], bank[0]]
        PRJ, SCR, TRB, OUT, XB = bank[0:2], bank[2:4], bank[4:6], bank[6], bank[7]

        def sem(name):
            return ctx.enter_context(nc.semaphore(name))

        s_hi = sem("s_hi")
        s_lo = sem("s_lo")
        s_raw = [sem(f"s_raw{j}") for j in range(PIECES)]
        s_kcd = [sem(f"s_kcd{i}") for i in range(2)]
        s_vcd = [sem(f"s_vcd{i}") for i in range(2)]
        s_x_in = [sem(f"s_x_in{i}") for i in range(TT)]
        s_const_d = sem("s_const_d")
        s_normed = sem("s_normed")
        s_kout = sem("s_kout")
        s_act_c = sem("s_act_c")
        s_vout = [sem(f"s_vout{i}") for i in range(2)]
        s_av = sem("s_av")
        s_glo = sem("s_glo")
        s_x2d = [sem(f"s_x2d{i}") for i in range(TT)]
        s_rows_g = sem("s_rows_g")
        s_x2sum = sem("s_x2sum")
        s_x2out = sem("s_x2out")
        s_ct = sem("s_ct")
        s_latc = sem("s_latc")
        s_latn = sem("s_latn")
        s_kper = sem("s_kper")
        s_latout = sem("s_latout")
        s_proj2 = sem("s_proj2")
        s_proj = sem("s_proj")
        s_od2 = sem("s_od2")
        s_x2in = [sem(f"s_x2in{i}") for i in range(TT)]
        s_gfin = sem("s_gfin")
        s_yn = sem("s_yn")
        s_yout = sem("s_yout")
        s_xt_hi = sem("s_xt_hi")
        s_xt = sem("s_xt")
        s_xt_lo = sem("s_xt_lo")
        s_dve_c = sem("s_dve_c")
        s_xev = sem("s_xev")
        s_xpose = sem("s_xpose")
        s_stay = sem("s_stay")
        s_score = sem("s_score")
        s_wgt = sem("s_wgt")
        s_wtev = sem("s_wtev")
        s_tr = sem("s_tr")
        s_odone = sem("s_odone")
        s_gcol = sem("s_gcol")
        s_xn = sem("s_xn")
        s_masks = sem("s_masks")
        s_gcol_t = sem("s_gcol_t")
        s_pad = sem("s_pad")
        s_ghi = sem("s_ghi")
        s_zeros_b = sem("s_zeros_b")
        s_yprod = sem("s_yprod")
        s_ct_lo = sem("s_ct_lo")
        s_ct_hi = sem("s_ct_hi")
        s_lat_lo = sem("s_lat_lo")
        s_kpet_e = sem("s_kpet_e")
        s_latx = sem("s_latx")
        s_lata = sem("s_lata")
        s_latm = sem("s_latm")
        s_lat_hi = sem("s_lat_hi")
        s_zeros_d = sem("s_zeros_d")
        s_act2 = sem("s_act2")
        s_dve2 = sem("s_dve2")
        s_nrm2 = sem("s_nrm2")
        s_xev2 = sem("s_xev2")
        s_xp2 = sem("s_xp2")
        s_expd = sem("s_expd")
        s_score2 = sem("s_score2")
        s_scaled = sem("s_scaled")
        s_wtev2 = sem("s_wtev2")
        s_tr2 = sem("s_tr2")
        s_av2 = sem("s_av2")
        s_zeros_e = sem("s_zeros_e")
        s_go_hi = sem("s_go_hi")
        s_go_lo = sem("s_go_lo")
        s_ysum = sem("s_ysum")
        s_row_ss = sem("s_row_ss")
        s_msq_d = sem("s_msq_d")
        s_sqd = sem("s_sqd")
        s_left = sem("s_left")
        s_lat_sum = sem("s_lat_sum")
        s_lat_ss = sem("s_lat_ss")
        s_sqk = sem("s_sqk")
        s_sum2 = sem("s_sum2")
        s_mean2 = sem("s_mean2")
        s_rope2 = sem("s_rope2")
        s_mean = sem("s_mean")
        s_negmax = sem("s_negmax")
        s_row_ms = sem("s_row_ms")
        s_row_r = sem("s_row_r")
        s_zeros_m = sem("s_zeros_m")
        s_rs = sem("s_rs")
        s_lat_ms = sem("s_lat_ms")
        s_lat_r = sem("s_lat_r")
        s_rs2 = sem("s_rs2")
        s_gscale = sem("s_gscale")
        s_rope = sem("s_rope")
        s_inv = sem("s_inv")

        def begun(v):
            return not isinstance(v, int) or v > 0

        def raw_count(g):
            return 32 * (g + 1)

        def wcol(g, part, k, c0, n, per):
            t = (whi, wlo)[part][g % 2]
            return t[:, k * per + c0:k * per + c0 + n]

        def acol(t, k, tile, width=TOK):
            return t[:, k * width + tile * P:k * width + tile * P + P]

        def three(eng, dst, pairs, ready=None):
            n = len(pairs)
            for k, (st, mv) in enumerate(pairs):
                if ready:
                    ready(k)
                eng.matmul(dst, st[0], mv[0], start=(k == 0), stop=False)
                eng.matmul(dst, st[0], mv[1], start=False, stop=False)
                mm = eng.matmul(dst, st[1], mv[0], start=False, stop=(k == n - 1))
            return mm

        block = ctx.enter_context(nc.Block())

        @block.sync
        def _(sp):
            def load_group(g, piece):
                for j in range(PIECES):
                    if not isinstance(g, int) or g:
                        known = isinstance(g, int)
                        split = j + 1
                        if known:
                            split = max(split, min(PIECES, -(-(j + 1) * COLS[g] // COLS[g - 1])))
                        sp.wait_ge(s_hi, PIECES * (g - 1) + split)
                        sp.wait_ge(s_lo, PIECES * (g - 1) + split)
                    for dst, src in piece(j):
                        sp.dma_start(dst, src).then_inc(s_raw[j], 16)

            def load_pair(g):
                v = raw[:, :].rearrange("p (k f c) -> p k f c", k=KD, f=4)
                load_group(g, lambda j: [(v[:, k, :, :], w_in[:, k, :, bass.ds(g * P, P)])
                                         for k in (2 * j, 2 * j + 1)])

            def load_cols(g, w, c0, n):
                v = raw[:, 0:KD * n].rearrange("p (k c) -> p k c", k=KD)
                load_group(g, lambda j: [(v[:, k, :], w[:, k, c0:c0 + n]) for k in (2 * j, 2 * j + 1)])

            def load_heads(m):
                v = raw[:, 0:COLS[G_D]].rearrange("p (k c) -> p k c", k=KL)
                load_group(G_D + m, lambda j: [(v[:, j, 0:WQ], w_qb[:, j, m * WQ:(m + 1) * WQ]),
                                               (v[:, j, WQ:], w_kvb[:, j, m * WK:(m + 1) * WK])])

            def load_late(g):
                if g < NP:
                    load_pair(g)
                elif g < G_LAT:
                    load_cols(g, w_oa, (g - G_OA) * 512, 512)
                elif g == G_LAT:
                    load_cols(g, w_kva, 0, LA)
                elif g == G_KPE:
                    load_cols(g, w_kva, LA, LB)
                elif g == G_QA:
                    load_cols(g, w_inb, 0, 512)
                elif g < G_D:
                    load_cols(g, w_inb, (g - G_GATE + 1) * 512, 512)
                elif g < G_OB:
                    load_heads(g - G_D)
                elif g < G_OB + 2:
                    load_cols(g, w_ob, (g - G_OB) * 512, 512)

            def cache_pair(q, par):
                sp.dma_start(kc[:, par, :], ck[:, bass.ds(q * P, P)]).then_inc(s_kcd[par], 16)
                sp.dma_start(vc[:, par, :], cv[:, bass.ds(q * P, P)]).then_inc(s_vcd[par], 16)

            for t in range(NT):
                sp.dma_start(x_in[:, t, :], x_p[:, t, :]).then_inc(s_x_in[t], 16)
            sp.dma_start(x_in[0:SMP, NT, :], x_s).then_inc(s_x_in[NT], 16)
            load_pair(0)
            for t, (dst, src) in enumerate([
                    (g_qk[:, 0, 0, :], a["g_q_a"].to_broadcast([P, HD])),
                    (g_qk[:, 0, 1, :], a["g_q_a"].to_broadcast([P, HD])),
                    (g_qk[:, 1, 0, :], a["g_k_a"].to_broadcast([P, HD])),
                    (g_qk[:, 1, 1, :], a["g_k_a"].to_broadcast([P, HD])),
                    (g_q[:, 0:NOPE], a["g_qn"].to_broadcast([P, NOPE])),
                    (g_q[:, NOPE:], a["g_qp"].to_broadcast([P, ROPE])),
                    (g_kn[:, :], a["g_knope"].rearrange("(a n) -> a n", a=1).to_broadcast([P, NOPE])),
                    (g_kp[:, :], a["g_kpe"].rearrange("(a n) -> a n", a=1).to_broadcast([P, ROPE])),
                    (g_rows[0:KD, :], a["g_pre_a"][0].rearrange("(k p) -> k p", p=P)),
                    (g_rows[KD:2 * KD, :], a["g_kv"].rearrange("(k p) -> k p", p=P)),
                    (g_rows[2 * KD:3 * KD, :], a["g_pre_b"][0].rearrange("(k p) -> k p", p=P)),
                    (cos_t[:, :, :], a["rope_cos"].rearrange("(t p) d -> p t d", p=P)),
                    (sin_t[:, :, :], a["rope_sin"].rearrange("(t p) d -> p t d", p=P))]):
                sp.dma_start(dst, src).then_inc(s_const_d, 16)
            load_pair(1)
            cache_pair(0, 0)
            cache_pair(1, 1)

            def outputs(q, par):
                sp.wait_ge(s_normed, TT * (q + 1))
                cols = bass.ds(q * P, P)
                sp.dma_start(ko_p[:, :, cols], qkn[:, 0:NT, 1, :]).then_inc(s_kout, 16)
                sp.dma_start(ko_s[:, cols], qkn[0:SMP, NT, 1, :]).then_inc(s_kout, 16)
                sp.wait_ge(s_act_c, CA * q + TT)
                sp.dma_start(vo_p[:, :, cols], vtok[:, par, 0:NT, :]).then_inc(s_vout[par], 16)
                sp.dma_start(vo_s[:, cols], vtok[0:SMP, par, NT, :]).then_inc(s_vout[par], 16)

            def step(p, par, last=False):
                if isinstance(p, int) and p + 3 >= NP:
                    load_late(p + 3)
                else:
                    load_pair(p + 3)
                if not (isinstance(p, int) and (p + 2 >= NP or p < 0)):
                    sp.wait_ge(s_av, 3 * p + 1)
                    cache_pair(p + 2, par)
                if not last:
                    outputs(p + 1, 1 - par)

            step(-1, 1)
            step(0, 0)
            with sp.Fori(0, 2) as i:
                step(2 * i + 1, 1)
                step(2 * i + 2, 0)
            step(5, 1)
            step(6, 0)
            step(7, 1, last=True)

            sp.wait_ge(s_glo, NP)
            sp.wait_ge(s_kout, 32 * NP)
            sp.wait_ge(s_vout[0], 16 * NP)
            sp.wait_ge(s_vout[1], 16 * NP)
            sp.dma_start(x2[0:SMP, NT, :], x_s).then_inc(s_x2d[NT], 16)
            for t in range(NT):
                sp.dma_start(x2[:, t, :], x_p[:, t, :]).then_inc(s_x2d[t], 16)
            sp.dma_start(g_lat[:, :], a["g_kv_a"].rearrange("(a n) -> a n", a=1).to_broadcast([P, KV])).then_inc(s_rows_g, 16)
            sp.dma_start(g_qar[:, :], a["g_qa"].to_broadcast([P, KV])).then_inc(s_rows_g, 16)
            load_late(G_KPE)
            for i, t in enumerate(ORDER):
                n = P if t < NT else SMP
                sp.wait_ge(s_x2sum, TT + i + 1)
                sp.dma_start(scratch[t * P:t * P + n, :], x2[0:n, t, :]).then_inc(s_x2out, 16)

            sp.wait_ge(s_ct, 2 * TT)
            sp.wait_ge(s_x2out, 16 * TT)
            sp.dma_start(lat[:, TT, :], a["cache_mla_latent"][0]).then_inc(s_latc, 16)
            for h in range(2):
                sp.dma_start(kpe[:, TT, h * ROPE:(h + 1) * ROPE], a["cache_mla_kpe"][0]).then_inc(s_latc, 16)
            load_late(G_QA)
            for i, t in enumerate(ORDER):
                n = P if t < NT else SMP
                sp.wait_ge(s_latn, i + 1)
                sp.wait_ge(s_kper, i + 1)
                lo_, ko_ = (lat_p, kpe_p) if t < NT else (lat_s, kpe_s)
                r0 = t * P if t < NT else 0
                sp.dma_start(lo_[0, r0:r0 + n, :], lat[0:n, t, :]).then_inc(s_latout, 16)
                sp.dma_start(ko_[0, r0:r0 + n, :], kpe[0:n, t, 0:ROPE]).then_inc(s_latout, 16)
            for g in range(G_GATE, G_OB + 2):
                load_late(g)
            sp.wait_ge(s_proj2, CD * MP)
            sp.wait_ge(s_od2, 3 * MP)
            sp.wait_ge(s_latout, 32 * TT)
            for t in range(TT):
                n = P if t < NT else SMP
                sp.dma_start(x2e[0:n, t, :], scratch[t * P:t * P + n, :]).then_inc(s_x2in[t], 16)
            sp.dma_start(g_fin[:, :], a["g_final"].rearrange("(a n) -> a n", a=1).to_broadcast([P, D])).then_inc(s_gfin, 16)
            for t in range(TT):
                n = P if t < NT else SMP
                sp.wait_ge(s_yn, t + 1)
                dst = y_p[0, t * P:t * P + n, :] if t < NT else y_s[0]
                sp.dma_start(dst, x2e[0:n, t, :]).then_inc(s_yout, 16)
            sp.wait_ge(s_yout, 16 * TT)

        @block.tensor
        def _(pe):
            def weights(g):
                pe.wait_ge(s_hi, PIECES * (g + 1))
                pe.wait_ge(s_lo, PIECES * (g + 1))

            def piece(g, kn=KD):
                def ready(k):
                    if k * PIECES % kn == 0:
                        pe.wait_ge(s_hi, PIECES * g + k * PIECES // kn + 1)
                        pe.wait_ge(s_lo, PIECES * g + k * PIECES // kn + 1)
                return ready

            def proj_a(q, par, c):
                ready = piece(q) if c == 0 else None
                if c == 0 and isinstance(q, int) and q == 0:
                    def ready(k):
                        piece(0)(k)
                        pe.wait_ge(s_xt_hi, k + 1)
                        pe.wait_ge(s_xt_lo, k + 1)
                if begun(CA * q + c - 1):
                    pe.wait_ge(s_act_c, CA * q + c - 1)
                if begun(CA * q + c - 1):
                    pe.wait_ge(s_dve_c, CA * q + c - 1)
                b = PRJ[(par + c) % 2]
                mm = three(pe, b[:, 0:3 * P], [
                    ([acol(ht[0], k, c), acol(ht[1], k, c)],
                     [whi[par][:, k * 512:k * 512 + 3 * P], wlo[par][:, k * 512:k * 512 + 3 * P]]) for k in range(KD)], ready)
                mm.then_inc(s_proj, 1)

            def gate_a(q, par, j):
                c = TT + j
                pe.wait_ge(s_act_c, CA * q + c - 1)
                if begun(CA * q + c - 1):
                    pe.wait_ge(s_dve_c, CA * q + c - 1)
                b = PRJ[(par + c) % 2]
                mm = three(pe, b[:, 0:HALF], [
                    ([whi[par][:, k * 512 + 384:k * 512 + 512], wlo[par][:, k * 512 + 384:k * 512 + 512]],
                     [ht[m][:, k * TOK + j * HALF:k * TOK + (j + 1) * HALF] for m in range(2)]) for k in range(KD)])
                mm.then_inc(s_proj, 1)

            def xpose_a(q, par, t):
                pe.wait_ge(s_normed, TT * q + t + 1)
                if begun(XA * q + t):
                    pe.wait_ge(s_xev, XA * q + t)
                for m in range(2):
                    mm = pe.transpose(XB[:, m * P:(m + 1) * P], qkn[:, t, m, :], ident[:, :])
                mm.then_inc(s_xpose, 1)

            def xpose_cache(q, par):
                pe.wait_ge(s_kcd[par], 8 * (q - par) + 16)
                pe.wait_ge(s_xev, XA * q + TT)
                pe.transpose(XB[:, 0:P], kc[:, par, :], ident[:, :]).then_inc(s_xpose, 1)

            def score_a(p, par, u):
                ub = (par + u) % 2
                if begun(UA * p + u - 1):
                    pe.wait_ge(s_stay, UA * p + u - 1)
                if u == 0:
                    pe.wait_ge(s_xev, XA * (p + 1))
                b = SCR[ub]
                if u == 0:
                    pe.matmul(b[0:2 * SMP, PAST:SKEY], ident_b[:, 0:2 * SMP], causal_s[:, :],
                              start=True, stop=False, skip_group_check=True)
                    for h in range(2):
                        r = slice(h * HD, (h + 1) * HD)
                        o = slice(h * SMP, (h + 1) * SMP)
                        qs = qkt[r, par, 0, SEQ:TOK]
                        pe.matmul(b[o, PAST:SKEY], qs, qkt[r, par, 1, SEQ:TOK], start=False, stop=True,
                                  skip_group_check=True)
                        mm = pe.matmul(b[o, 0:PAST], qs, kct[r, par, :], start=False, stop=True,
                                       skip_group_check=True)
                    mm.then_inc(s_score, 1)
                    return
                h, i = UNIT_A[u]
                r = slice(h * HD, (h + 1) * HD)
                pe.matmul(b[:, 0:(i + 1) * P], qkt[r, par, 0, i * P:(i + 1) * P], qkt[r, par, 1, 0:(i + 1) * P],
                          start=True, stop=True)
                pe.matmul(b[:, i * P:(i + 1) * P], ident_b[:, :], causal[:, :], start=False, stop=True,
                          skip_group_check=True).then_inc(s_score, 1)

            def turn_a(p, par, u):
                ub = (par + u) % 2
                pe.wait_ge(s_wgt, UA * p + u + 1)
                if begun(UA * p + u - 1):
                    pe.wait_ge(s_wtev, UA * p + u - 1)
                n = 2 if u == 0 else UNIT_A[u][1] + 1
                for j in range(n):
                    mm = pe.transpose(TRB[ub][:, j * P:(j + 1) * P], wgt[:, ub, j * P:(j + 1) * P], ident[:, :])
                mm.then_inc(s_tr, 1)

            def out_a(p, par, o):
                if begun(3 * p + o):
                    pe.wait_ge(s_odone, 3 * p + o)
                pe.wait_ge(s_wtev, UA * p + (1 if o == 0 else 1 + NT * o))
                if o == 0:
                    pe.wait_ge(s_vcd[par], 8 * (p - par) + 16)
                    pe.wait_ge(s_act_c, CA * p + TT)
                    for h in range(2):
                        r = slice(h * HD, (h + 1) * HD)
                        c = slice(h * SMP, (h + 1) * SMP)
                        pe.matmul(OUT[r, 0:SMP], vc[:, par, r], wts[:, 0, c], start=True, stop=False)
                        mm = pe.matmul(OUT[r, 0:SMP], vtok[0:SMP, par, NT, r], wts[0:SMP, 1, c], start=False, stop=True)
                    mm.then_inc(s_av, 1)
                    return
                r = slice((o - 1) * HD, o * HD)
                for j in range(NT):
                    mm = pe.matmul(OUT[r, j * P:SEQ], vtok[:, par, j, r], wt[:, j, j * P:SEQ],
                                   start=(j == 0), stop=(j == NT - 1))
                mm.then_inc(s_av, 1)

            def step_a(p, par, att=True, ahead=True):
                for what, n in STEP_A:
                    if what in AHEAD:
                        if not ahead:
                            continue
                        q, qpar = p + 1, 1 - par
                        if what == "C":
                            proj_a(q, qpar, n)
                        elif what == "G":
                            gate_a(q, qpar, n)
                        elif what == "X":
                            xpose_a(q, qpar, n)
                        elif what == "Z":
                            xpose_cache(q, qpar)
                    elif att:
                        if what == "S":
                            score_a(p, par, n)
                        elif what == "T":
                            turn_a(p, par, n)
                        elif what == "O":
                            out_a(p, par, n)

            def turn_x(K):
                b, bs = (bank[4 + K % 2], bank[6 + K % 2])
                if begun(K - 1):
                    pe.wait_ge(s_xt_lo, K - 1)
                if K == 1:
                    pe.wait_ge(s_gcol, 1)
                for t in range(NT):
                    if K == 0:
                        pe.wait_ge(s_xn, t + 1)
                    pe.transpose(b[:, t * P:(t + 1) * P], x_in[:, t, K * P:(K + 1) * P], ident[:, :])
                if K == 0:
                    pe.wait_ge(s_xn, TT)
                pe.transpose(bs[:, 0:SMP], x_in[0:SMP, NT, K * P:(K + 1) * P], ident[0:SMP, 0:SMP]).then_inc(s_xt, 1)

            pe.wait_ge(s_masks, 2)
            pe.wait_ge(s_const_d, 16 * 13)
            pe.transpose(XB[:, 0:3 * KD], g_rows[:, :], ident[0:3 * KD, 0:3 * KD]).then_inc(s_gcol_t, 1)
            for K in range(KD):
                turn_x(K)
            pe.wait_ge(s_pad, 4)

            pe.wait_ge(s_gcol, 1)
            step_a(-1, 1, att=False)
            pe.wait_ge(s_masks, 7)
            step_a(0, 0)
            with pe.Fori(0, 3) as i:
                step_a(2 * i + 1, 1)
                step_a(2 * i + 2, 0)
            step_a(7, 1, ahead=False)

            def residual(i, nh):
                n = TT * nh + i
                if begun(n - 3):
                    pe.wait_ge(s_x2sum, n - 3)
                three(pe, bank[n % 4][:, :], [
                    ([acol(gt[0], k, ORDER[i]), acol(gt[1], k, ORDER[i])],
                     [wcol(G_OA + nh, m, k, 0, 512, 512) for m in range(2)]) for k in range(KD)]).then_inc(s_yprod, 1)

            def turn_x2(i):
                t = ORDER[i]
                n = P if t < NT else SMP
                pe.wait_ge(s_xn, TT + i + 1)
                for j in range(2):
                    if begun(2 * (i - 2) + j + 1):
                        pe.wait_ge(s_ct_lo, 2 * (i - 2) + j + 1)
                    for k in range(KD // 2):
                        K = j * KD // 2 + k
                        mm = pe.transpose(bank[4 + 2 * (i % 2) + j][:, k * P:k * P + n],
                                          xn[0:n, t, K * P:(K + 1) * P], ident[0:n, 0:n])
                    mm.then_inc(s_ct, 1)

            weights(G_OA)
            weights(G_OA + 1)
            pe.wait_ge(s_ghi, NP)
            pe.wait_ge(s_glo, NP)
            pe.wait_ge(s_zeros_b, 2)
            for i in range(TT):
                residual(i, 0)
            for i in range(TT):
                residual(i, 1)
                if i:
                    turn_x2(i - 1)

            def lat_a(i):
                ready = 2 * max(2, i + 1)
                pe.wait_ge(s_ct_hi, ready)
                pe.wait_ge(s_ct_lo, ready)
                if i < 3:
                    pe.wait_ge(s_x2sum, 2 * TT - 2 + i)
                else:
                    pe.wait_ge(s_latn, i - 2)
                three(pe, LAB[i % 3][:, 0:LA], [
                    ([acol(gt[m], k, ORDER[i]) for m in range(2)], [wcol(G_LAT, m, k, 0, LA, LA) for m in range(2)])
                    for k in range(KD)], piece(G_LAT) if i == 0 else None).then_inc(s_lata, 1)

            def lat_b(i):
                if begun(i - 1):
                    pe.wait_ge(s_latn, i - 1)
                if i == 1:
                    pe.wait_ge(s_ct_lo, 2 * (TT - 1))
                three(pe, bank[3 + 3 * (i % 2)][:, 0:LB], [
                    ([acol(gt[m], k, ORDER[i]) for m in range(2)], [wcol(G_KPE, m, k, 0, LB, LB) for m in range(2)])
                    for k in range(KD)], piece(G_KPE) if i == 0 else None).then_inc(s_latm, 1)

            def lat_turn(i):
                t = ORDER[i] if i < TT else TT
                if begun(i):
                    pe.wait_ge(s_lat_lo, i)
                if begun(i):
                    pe.wait_ge(s_kpet_e, i)
                if i < TT:
                    pe.wait_ge(s_latn, i + 1)
                    pe.wait_ge(s_kper, i + 1)
                else:
                    pe.wait_ge(s_latc, 48)
                for k in range(KL):
                    pe.transpose(bank[4][:, k * P:(k + 1) * P], lat[:, t, k * P:(k + 1) * P], ident[:, :])
                pe.transpose(bank[5][:, 0:P], kpe[:, t, :], ident[:, :]).then_inc(s_latx, 1)

            lat_a(0)
            lat_a(1)
            turn_x2(TT - 1)
            for i in range(TT):
                lat_b(i)
                if i + 2 < TT:
                    lat_a(i + 2)
                if i:
                    if i == 1:
                        pe.wait_ge(s_ct_lo, 2 * TT)
                    lat_turn(i - 1)

            def qa_turn(t):
                pe.wait_ge(s_lat_lo, LT + t)
                pe.wait_ge(s_latn, TT + t + 1)
                for k in range(KL):
                    mm = pe.transpose(bank[4][:, k * P:(k + 1) * P], qan[:, k * P:(k + 1) * P], ident[:, :])
                mm.then_inc(s_latx, 1)

            for t in range(TT):
                n = TT + t
                pe.wait_ge(s_latn, n - 1)
                three(pe, QAB[t % 2][:, :], [
                    ([acol(ht[m], k, t) for m in range(2)], [wcol(G_QA, m, k, 0, 512, 512) for m in range(2)])
                    for k in range(KD)], piece(G_QA) if t == 0 else None).then_inc(s_latm, 1)
                if t == 0:
                    lat_turn(TT - 1)
                if t == 1:
                    lat_turn(TT)
                if t:
                    qa_turn(t - 1)
            for m8 in range(NH):
                g, mm4 = G_GATE + m8 // 4, m8 % 4
                if mm4 == 0:
                    weights(g)
                for j in range(2):
                    n = 2 * m8 + j
                    pe.wait_ge(s_dve_c, CA * NP + n - 1)
                    three(pe, bank[2 + n % 2][:, 0:HALF], [
                        ([wcol(g, m, k, mm4 * P, P, 512) for m in range(2)],
                         [ht[m][:, k * TOK + j * HALF:k * TOK + (j + 1) * HALF] for m in range(2)])
                        for k in range(KD)]).then_inc(s_proj, 1)
                    if n == 0:
                        qa_turn(TT - 1)
            pe.wait_ge(s_lat_hi, LT + TT)
            pe.wait_ge(s_lat_lo, LT + TT)
            pe.wait_ge(s_kpet_e, LT)
            pe.wait_ge(s_zeros_d, 2)

            def chunk_free(q, c):
                if begun(CD * q + c - 1):
                    pe.wait_ge(s_act2, CD * q + c - 1)
                if begun(CD * q + c - 1):
                    pe.wait_ge(s_dve2, CD * q + c - 1)

            def query_d(q, par, t):
                slot = (G_D + par) % 2
                c = CHUNK_D["Q", t]
                chunk_free(q, c)
                three(pe, PRJ[(par + c) % 2][:, 0:WQ], [
                    ([acol(qat[m], k, t) for m in range(2)],
                     [(whi, wlo)[m][slot][:, k * WD:k * WD + WQ] for m in range(2)]) for k in range(KL)],
                    piece(q + G_D, KL) if c == 0 else None).then_inc(s_proj2, 1)

            def keyval_d(q, par, t):
                slot = (G_D + par) % 2
                c = CHUNK_D["K", t]
                chunk_free(q, c)
                three(pe, PRJ[(par + c) % 2][:, 0:WK], [
                    ([latt[m][:, (k * LT + t) * P:(k * LT + t + 1) * P] for m in range(2)],
                     [(whi, wlo)[m][slot][:, k * WD + WQ:(k + 1) * WD] for m in range(2)]) for k in range(KL)]).then_inc(s_proj2, 1)

            def turn_qk(q, what, t):
                c = CHUNK_D["Q" if what == "X" else "K", t]
                if what == "X":
                    pe.wait_ge(s_nrm2, TT * q + t + 1)
                else:
                    pe.wait_ge(s_dve2, CD * q + c + 1)
                if begun(CD * q + c):
                    pe.wait_ge(s_xev2, CD * q + c)
                src, n = (qn2, 3) if what == "X" else (kn2, 2)
                for m in range(n):
                    mm = pe.transpose(XB[:, m * P:(m + 1) * P], src[:, t % 2, m * P:(m + 1) * P], ident[:, :])
                mm.then_inc(s_xp2, 1)

            def score_d(p, par, u):
                ub = (par + u) % 2
                if begun(UA * p + u - 1):
                    pe.wait_ge(s_expd, UA * p + u - 1)
                if u == 0:
                    pe.wait_ge(s_xev2, CD * (p + 1))
                b = SCR[ub]
                if u == 0:
                    for h in range(2):
                        r, o = slice(h * ROPE, (h + 1) * ROPE), slice(h * SMP, (h + 1) * SMP)
                        pe.matmul(b[o, 0:SKEY], q2t[:, par, h, SEQ:TOK], k2t[:, par, h, SEQ:KEYS],
                                  start=True, stop=False)
                        mm = pe.matmul(b[o, 0:SKEY], q2t[r, par, 2, SEQ:TOK], kpet[r, SEQ:KEYS],
                                       start=False, stop=True)
                    mm.then_inc(s_score2, 1)
                    return
                h, i = UNIT_A[u]
                r = slice(h * ROPE, (h + 1) * ROPE)
                pe.matmul(b[:, 0:(i + 1) * P], q2t[:, par, h, i * P:(i + 1) * P], k2t[:, par, h, 0:(i + 1) * P],
                          start=True, stop=False)
                pe.matmul(b[:, 0:(i + 1) * P], q2t[r, par, 2, i * P:(i + 1) * P], kpet[r, 0:(i + 1) * P],
                          start=False, stop=True)
                pe.matmul(b[:, i * P:(i + 1) * P], ident_b[:, :], chunk_mask[:, :], start=False, stop=True,
                          skip_group_check=True).then_inc(s_score2, 1)

            def turn_d(p, par, u):
                ub = (par + u) % 2
                pe.wait_ge(s_scaled, UA * p + u + 1)
                if begun(UA * p + u - 1):
                    pe.wait_ge(s_wtev2, UA * p + u - 1)
                offs = [0, SMP] if u == 0 else [j * P for j in range(UNIT_A[u][1] + 1)]
                for j, o in enumerate(offs):
                    mm = pe.transpose(TRB[ub][:, j * P:(j + 1) * P], prob[:, ub, o:o + P], ident[:, :])
                mm.then_inc(s_tr2, 1)

            def out_d(p, par, o):
                if begun(3 * p + o):
                    pe.wait_ge(s_od2, 3 * p + o)
                pe.wait_ge(s_wtev2, UA * p + (1 if o == 0 else 1 + NT * o))
                if o == 0:
                    pe.wait_ge(s_act2, CD * (p + 1))
                    for h in range(2):
                        c = slice(h * SMP, (h + 1) * SMP)
                        pe.matmul(OUT[:, c], v2[0:SMP, par, h, NT, :], wts2[0:SMP, 0, c], start=True, stop=False)
                        mm = pe.matmul(OUT[:, c], v2[:, par, h, TT, :], wts2[:, 1, c], start=False, stop=True)
                    mm.then_inc(s_av2, 1)
                    return
                for j in range(NT):
                    mm = pe.matmul(OUT[:, j * P:SEQ], v2[:, par, o - 1, j, :], wt2[:, j, j * P:SEQ],
                                   start=(j == 0), stop=(j == NT - 1))
                mm.then_inc(s_av2, 1)

            def step_d(p, par, att=True, ahead=True):
                for what, n in STEP_D:
                    if what in AHEAD:
                        if not ahead:
                            continue
                        if what == "Q":
                            query_d(p + 1, 1 - par, n)
                        elif what == "K":
                            keyval_d(p + 1, 1 - par, n)
                        elif what in "XY":
                            turn_qk(p + 1, what, n)
                    elif att:
                        if what == "P":
                            turn_qk(p, "Y", n)
                        elif what == "S":
                            score_d(p, par, n)
                        elif what == "T":
                            turn_d(p, par, n)
                        elif what == "O":
                            out_d(p, par, n)

            step_d(-1, 1, att=False)
            pe.wait_ge(s_zeros_d, 3)
            pe.wait_ge(s_dve_c, CA * NP + 2 * NH)
            for p in range(MP):
                step_d(p, p % 2, ahead=p + 1 < MP)

            weights(G_OB)
            weights(G_OB + 1)
            pe.wait_ge(s_zeros_e, 2)

            def split_out(k):
                pe.wait_ge(s_go_hi, k + 1)
                pe.wait_ge(s_go_lo, k + 1)

            for t in range(TT):
                for nh in range(2):
                    n = 2 * t + nh
                    if begun(n - 3):
                        pe.wait_ge(s_ysum, n - 3)
                    g = G_OB + nh
                    three(pe, bank[n % 4][:, :], [
                        ([acol(ht[0], k, t), acol(ht[1], k, t)],
                         [wcol(g, m, k, 0, 512, 512) for m in range(2)]) for k in range(KD)],
                        split_out if n == 0 else None).then_inc(s_yprod, 1)

        def last_reader(g):
            if not isinstance(g, int) or g < G_LAT:
                return s_proj, CA * (g - 1)
            if g <= G_KPE:
                return s_yprod, TT * (1 + g - G_LAT)
            if g == G_QA:
                return s_lata, TT
            if g <= G_GATE:
                return s_latm, TT
            if g == G_GATE + 1:
                return s_latm, 2 * TT
            return s_proj, CA * NP + NH * (g - G_D + 1)

        def last_reader_d(h):
            if isinstance(h, int) and h < 0:
                return last_reader(G_D + 1)
            return s_proj2, CD * (h + 1)

        OUT_A = [(slice(0, P), SEQ, SMP), (slice(0, HD), 0, SEQ), (slice(HD, P), 0, SEQ)]

        def gt_pair(t, p):
            return t[:, bass.ds(p * TOK, TOK)]

        def turned(t, tile, n, k=KL, width=LT * P):
            return t[:, 0:k * width].rearrange("p (k c) -> p k c", k=k)[:, :, tile * P:tile * P + n]

        @block.scalar
        def _(act):
            def split_piece(g, j, slot, cols):
                n = cols // PIECES
                act.wait_ge(s_raw[j], raw_count(g))
                c = slice(j * n, (j + 1) * n)
                nc.scalar.activation(whi[slot][:, c], raw[:, c], ACT.Copy).then_inc(s_hi, 1)

            def split_group(g):
                if g > 1:
                    sem, n = last_reader(g)
                    act.wait_ge(sem, n)
                for j in range(PIECES):
                    split_piece(g, j, g % 2, COLS[g])

            for t in range(TT):
                n = P if t < NT else SMP
                act.wait_ge(s_x_in[t], 16)
                if begun(t):
                    act.wait_ge(s_row_ss, t)
                nc.scalar.activation(dump_x[0:n, :], x_in[0:n, t, :], ACT.Square,
                                     accum_out=row_ss[0:n, 0, t:t + 1]).then_inc(s_row_ss, 1)
            act.wait_ge(s_gcol_t, 1)
            nc.scalar.activation(g_col[:, :, :].rearrange("p m k -> p (m k)"), XB[:, 0:3 * KD],
                                 ACT.Copy).then_inc(s_gcol, 1)
            act.wait_ge(s_gcol, 1)
            split_group(0)
            for K in range(KD):
                act.wait_ge(s_xt, K + 1)
                gain = g_col[:, 0, K:K + 1]
                nc.scalar.activation(ht[0][:, K * TOK:K * TOK + SEQ], bank[4 + K % 2][:, :], ACT.Copy, scale=gain)
                nc.scalar.activation(ht[0][:, K * TOK + SEQ:(K + 1) * TOK], bank[6 + K % 2][:, 0:SMP], ACT.Copy,
                                     scale=gain).then_inc(s_xt_hi, 1)

            def chunk_a(q, par, c):
                b = PRJ[(par + c) % 2]
                act.wait_ge(s_proj, CA * q + c + 1)
                if begun(TT * q + c):
                    act.wait_ge(s_msq_d, TT * q + c)
                if c == 0:
                    if begun(CA * q):
                        act.wait_ge(s_dve_c, CA * q)
                nc.scalar.activation(sq[:, :], b[:, 0:2 * P], ACT.Square).then_inc(s_sqd, 1)
                if c == 0:
                    if begun(3 * (q - 1)):
                        act.wait_ge(s_av, 3 * (q - 1))
                    if begun(16 * (q - par)):
                        act.wait_ge(s_vout[par], 16 * (q - par))
                nc.scalar.activation(vtok[:, par, c, :], b[:, 2 * P:3 * P], ACT.Copy).then_inc(s_act_c, 1)

            def gate_a(q, par, j):
                c = TT + j
                act.wait_ge(s_proj, CA * q + c + 1)
                act.wait_ge(s_dve_c, CA * q + c)
                act.wait_ge(s_normed, TT * (q + 1))
                nc.scalar.activation(sigm[:, :], PRJ[(par + c) % 2][:, 0:HALF], ACT.Sigmoid).then_inc(s_act_c, 1)

            def xev_a(q, par, t):
                n = P if t < NT else SMP
                act.wait_ge(s_xpose, XA * q + t + 1)
                nc.scalar.activation(qkt[:, par, :, t * P:t * P + n],
                                     XB[:, 0:2 * P].rearrange("p (m c) -> p m c", m=2)[:, :, 0:n],
                                     ACT.Copy).then_inc(s_xev, 1)

            def zev_a(q, par):
                act.wait_ge(s_xpose, XA * (q + 1))
                nc.scalar.activation(kct[:, par, :], XB[:, 0:P], ACT.Copy).then_inc(s_xev, 1)

            def stay_a(p, par, u):
                ub = (par + u) % 2
                act.wait_ge(s_score, UA * p + u + 1)
                if begun(UA * p + u - 1):
                    act.wait_ge(s_left, UA * p + u - 1)
                r, n = (2 * SMP, SKEY) if u == 0 else (P, (UNIT_A[u][1] + 1) * P)
                nc.scalar.activation(stay[0:r, ub, SEQ - n:SEQ], SCR[ub][0:r, 0:n], ACT.Sigmoid,
                                     scale=-1.0).then_inc(s_stay, 1)

            def wtev_a(p, par, u):
                ub = (par + u) % 2
                act.wait_ge(s_tr, UA * p + u + 1)
                if u == 0:
                    if begun(3 * p - 2):
                        act.wait_ge(s_av, 3 * p - 2)
                    nc.scalar.activation(wts[:, :, :],
                                         TRB[ub][:, 0:2 * P].rearrange("p (j c) -> p j c", j=2)[:, :, 0:2 * SMP],
                                         ACT.Copy).then_inc(s_wtev, 1)
                    return
                h, i = UNIT_A[u]
                if i == NT - 1:
                    if begun(3 * p + 2 * h):
                        act.wait_ge(s_av, 3 * p + 2 * h)
                nc.scalar.activation(wt[:, 0:i + 1, i * P:(i + 1) * P],
                                     TRB[ub][:, 0:(i + 1) * P].rearrange("p (j c) -> p j c", j=i + 1),
                                     ACT.Copy).then_inc(s_wtev, 1)

            def out_hi(p):
                act.wait_ge(s_odone, 3 * (p + 1))
                nc.scalar.activation(gt_pair(gt[0], p), gated[:, :], ACT.Copy).then_inc(s_ghi, 1)

            def step_a(p, par, att=True, ahead=True):
                for what, n in STEP_A:
                    if what in AHEAD:
                        if not ahead:
                            continue
                        q, qpar = p + 1, 1 - par
                        if what == "C":
                            chunk_a(q, qpar, n)
                        elif what == "G":
                            gate_a(q, qpar, n)
                        elif what == "X":
                            xev_a(q, qpar, n)
                        elif what == "Z":
                            zev_a(q, qpar)
                    elif what == "W":
                        if n == 0 and not (isinstance(p, int) and p < 0):
                            sem, count = last_reader(p + 2)
                            act.wait_ge(sem, count)
                        split_piece(p + 2, n, par, KD * 512)
                    elif att:
                        if what == "S":
                            stay_a(p, par, n)
                        elif what == "T":
                            wtev_a(p, par, n)
                        elif what == "O" and n == 2:
                            out_hi(p)

            step_a(-1, 1, att=False)
            step_a(0, 0)
            with act.Fori(0, 3) as i:
                step_a(2 * i + 1, 1)
                step_a(2 * i + 2, 0)
            step_a(7, 1, ahead=False)

            def square_x2(i):
                t = ORDER[i]
                n = P if t < NT else SMP
                act.wait_ge(s_x2sum, TT + i + 1)
                act.wait_ge(s_row_ss, TT + i)
                nc.scalar.activation(dump[0:n, :], x2[0:n, t, :], ACT.Square,
                                     accum_out=row_ss[0:n, 1, i:i + 1]).then_inc(s_row_ss, 1)

            def norm_x2(i):
                t = ORDER[i]
                n = P if t < NT else SMP
                act.wait_ge(s_row_r, TT + i + 1)
                nc.scalar.activation(xn[0:n, t, :], x2[0:n, t, :], ACT.Copy,
                                     scale=row_r[0:n, 1, i:i + 1]).then_inc(s_xn, 1)

            def x2_hi(i):
                t = ORDER[i]
                n = P if t < NT else SMP
                for j in range(2):
                    act.wait_ge(s_ct, 2 * i + j + 1)
                    for k in range(KD // 2):
                        K = j * KD // 2 + k
                        src = bank[4 + 2 * (i % 2) + j][:, k * P:k * P + n]
                        for m, dst in ((1, gt[0]), (2, ht[0])):
                            last = nc.scalar.activation(dst[:, K * TOK + t * P:K * TOK + t * P + n], src, ACT.Copy,
                                                        scale=g_col[:, m, K:K + 1])
                    last.then_inc(s_ct_hi, 1)

            split_group(G_LAT)
            for i in range(TT):
                square_x2(i)
                if i:
                    x2_hi(i - 1)
                norm_x2(i)
            split_group(G_KPE)
            x2_hi(TT - 1)

            def lat_hi(i):
                t = ORDER[i] if i < TT else TT
                act.wait_ge(s_latx, i + 1)
                nc.scalar.activation(turned(latt[0], t, P), bank[4][:, :].rearrange("p (k c) -> p k c", k=KL),
                                     ACT.Copy).then_inc(s_lat_hi, 1)
                c0, n = [(t * P, P), (SEQ, SMP), (TOK, P)][max(0, t - NT + 1)]
                nc.scalar.activation(kpet[:, c0:c0 + n], bank[5][:, 0:n], ACT.Copy).then_inc(s_kpet_e, 1)

            def qa_hi(t):
                n = P if t < NT else SMP
                act.wait_ge(s_latx, LT + t + 1)
                nc.scalar.activation(turned(qat[0], t, n, width=TOK),
                                     bank[4][:, :].rearrange("p (k c) -> p k c", k=KL)[:, :, 0:n],
                                     ACT.Copy).then_inc(s_lat_hi, 1)

            act.wait_ge(s_x2out, 16 * TT)
            for i in range(TT):
                act.wait_ge(s_lata, i + 1)
                if begun(i):
                    act.wait_ge(s_lat_ss, i)
                nc.scalar.activation(sqc[:, 0:LA], LAB[i % 3][:, 0:LA], ACT.Square, accum_out=lat_ss[:, i, 0:1])
                act.wait_ge(s_latm, i + 1)
                b = bank[3 + 3 * (i % 2)]
                nc.scalar.activation(sqc[:, LA:KV], b[:, 0:KV - LA], ACT.Square, accum_out=lat_ss[:, i, 2:3])
                nc.scalar.activation(sq_pe[:, :], b[:, KV - LA:LB], ACT.Square,
                                     accum_out=lat_ss[:, i, 1:2]).then_inc(s_lat_ss, 1)
                if i:
                    lat_hi(i - 1)
            split_group(G_QA)
            lat_hi(TT - 1)
            for t in range(TT):
                act.wait_ge(s_latm, TT + t + 1)
                act.wait_ge(s_lat_ss, TT + t)
                nc.scalar.activation(sqc[:, :], QAB[t % 2][:, :], ACT.Square,
                                     accum_out=lat_ss[:, TT + t, 0:1]).then_inc(s_lat_ss, 1)
                if t == 1:
                    lat_hi(TT)
                if t:
                    qa_hi(t - 1)
                if t == 2:
                    split_group(G_GATE)
            split_group(G_GATE + 1)
            for n in range(2 * NH):
                act.wait_ge(s_proj, CA * NP + n + 1)
                act.wait_ge(s_dve_c, CA * NP + n)
                act.wait_ge(s_lat_ss, 2 * TT)
                nc.scalar.activation(sigc[:, :], bank[2 + n % 2][:, 0:HALF], ACT.Sigmoid).then_inc(s_act_c, 1)
                if n == 0:
                    qa_hi(TT - 1)
                if n == NH:
                    split_group(G_D)

            def chunk_d(q, par, what, t):
                c = CHUNK_D[what, t]
                b = PRJ[(par + c) % 2]
                act.wait_ge(s_proj2, CD * q + c + 1)
                if begun(CD * q + c):
                    act.wait_ge(s_sum2, CD * q + c)
                if what == "Q":
                    nc.scalar.activation(sqd[:, :], b[:, 0:WQ], ACT.Square).then_inc(s_act2, 1)
                    return
                kv = b[:, 0:WK].rearrange("p (h s d) -> p h s d", h=2, s=2)
                nc.scalar.activation(sqd[:, 0:2 * NOPE].rearrange("p (h d) -> p h d", h=2), kv[:, :, 0, :],
                                     ACT.Square).then_inc(s_sqk, 1)
                if t == 0:
                    if begun(3 * (q - 1)):
                        act.wait_ge(s_av2, 3 * (q - 1))
                nc.scalar.activation(v2[:, par, :, t, :], kv[:, :, 1, :], ACT.Copy).then_inc(s_act2, 1)

            def xev_d(q, par, what, t):
                c = CHUNK_D["Q" if what == "X" else "K", t]
                act.wait_ge(s_xp2, CD * q + c + 1)
                if what == "X":
                    n = P if t < NT else SMP
                    nc.scalar.activation(q2t[:, par, :, t * P:t * P + n],
                                         XB[:, 0:3 * P].rearrange("p (m c) -> p m c", m=3)[:, :, 0:n],
                                         ACT.Copy).then_inc(s_xev2, 1)
                else:
                    c0, n = [(t * P, P), (SEQ, SMP), (TOK, P)][max(0, t - NT + 1)]
                    nc.scalar.activation(k2t[:, par, :, c0:c0 + n],
                                         XB[:, 0:2 * P].rearrange("p (m c) -> p m c", m=2)[:, :, 0:n],
                                         ACT.Copy).then_inc(s_xev2, 1)

            def exp_d(p, par, u):
                ub = (par + u) % 2
                act.wait_ge(s_negmax, UA * p + u + 1)
                if begun(UA * p + u - 1):
                    act.wait_ge(s_tr2, UA * p + u - 1)
                r, n = (2 * SMP, SKEY) if u == 0 else (P, (UNIT_A[u][1] + 1) * P)
                nc.scalar.activation(prob[0:r, ub, 0:n], SCR[ub][0:r, 0:n], ACT.Exp, bias=neg_max[0:r, ub:ub + 1],
                                     accum_out=p_sum[0:r, ub:ub + 1]).then_inc(s_expd, 1)

            def wtev_d(p, par, u):
                ub = (par + u) % 2
                act.wait_ge(s_tr2, UA * p + u + 1)
                if u == 0:
                    if begun(3 * p - 2):
                        act.wait_ge(s_av2, 3 * p - 2)
                    nc.scalar.activation(wts2[:, :, :],
                                         TRB[ub][:, 0:2 * P].rearrange("p (j c) -> p j c", j=2)[:, :, 0:2 * SMP],
                                         ACT.Copy).then_inc(s_wtev2, 1)
                    return
                h, i = UNIT_A[u]
                if i == NT - 1:
                    if begun(3 * p + 2 * h):
                        act.wait_ge(s_av2, 3 * p + 2 * h)
                nc.scalar.activation(wt2[:, 0:i + 1, i * P:(i + 1) * P],
                                     TRB[ub][:, 0:(i + 1) * P].rearrange("p (j c) -> p j c", j=i + 1),
                                     ACT.Copy).then_inc(s_wtev2, 1)

            def step_d(p, par, att=True, ahead=True):
                for what, n in STEP_D:
                    if what in AHEAD:
                        if not ahead:
                            continue
                        if what in "QK":
                            chunk_d(p + 1, 1 - par, what, n)
                        elif what in "XY":
                            xev_d(p + 1, 1 - par, what, n)
                    elif what == "W":
                        g = p + G_D + 2
                        if n == 0:
                            sem, count = last_reader_d(p)
                            act.wait_ge(sem, count)
                        split_piece(g, n, g % 2, COLS[g])
                    elif att:
                        if what == "P":
                            xev_d(p, par, "Y", n)
                        elif what == "S":
                            exp_d(p, par, n)
                        elif what == "T":
                            wtev_d(p, par, n)

            act.wait_ge(s_latout, 32 * TT)
            step_d(-1, 1, att=False)
            for p in range(MP):
                step_d(p, p % 2, ahead=p + 1 < MP)

            act.wait_ge(s_od2, 3 * MP)
            for K in range(KD):
                nc.scalar.activation(ht[0][:, K * TOK:(K + 1) * TOK], sg[:, K, :], ACT.Copy).then_inc(s_go_hi, 1)
            for t in range(TT):
                n = P if t < NT else SMP
                act.wait_ge(s_ysum, 2 * (t + 1))
                act.wait_ge(s_row_ss, 2 * TT + t)
                nc.scalar.activation(dump2[0:n, :], x2e[0:n, t, :], ACT.Square,
                                     accum_out=row_ss[0:n, 2, t:t + 1]).then_inc(s_row_ss, 1)

        @block.gpsimd
        def _(pool):
            def split_piece(g, j, slot, cols):
                n = cols // PIECES
                c = slice(j * n, (j + 1) * n)
                pool.wait_ge(s_hi, PIECES * g + j + 1)
                nc.gpsimd.tensor_tensor(wlo[slot][:, c], raw[:, c], whi[slot][:, c].bitcast(F32),
                                        ALU.subtract).then_inc(s_lo, 1)

            def split_group(g):
                if g > 1:
                    sem, n = last_reader(g)
                    pool.wait_ge(sem, n)
                for j in range(PIECES):
                    split_piece(g, j, g % 2, COLS[g])

            def rms_rows(phase, t):
                n = SMP if t == (0 if phase == 1 else NT) else P
                k = TT * phase + t
                pool.wait_ge(s_row_ss, k + 1)
                nc.gpsimd.tensor_scalar(row_ms[0:n, phase, t:t + 1], row_ss[0:n, phase, t:t + 1], 1.0 / D, EPS,
                                        ALU.mult, ALU.add).then_inc(s_row_ms, 1)
                pool.wait_ge(s_row_ms, k + 1)
                nc.gpsimd.tensor_tensor(row_r[0:n, phase, t:t + 1], row_ms[0:n, phase, t:t + 1],
                                        neg_half[0:n, 0:1], ALU.pow).then_inc(s_row_r, 1)

            nc.gpsimd.memset(neg_half[:, :], -0.5).then_inc(s_masks, 1)
            nc.gpsimd.memset(ident[:, :], 0.0).then_inc(s_pad, 1)
            pool.wait_ge(s_pad, 1)
            nc.gpsimd.affine_select(out=ident[:, :], in_=ident[:, :], compare_op=ALU.not_equal, fill=1.0,
                                    base=0, pattern=[[-1, P]], channel_multiplier=1).then_inc(s_masks, 1)
            nc.gpsimd.memset(ht[0][:, KD * TOK:FLAT].bitcast(F32), 0.0).then_inc(s_pad, 1)
            nc.gpsimd.memset(ht[1][:, KD * TOK:FLAT].bitcast(F32), 0.0).then_inc(s_pad, 1)
            nc.gpsimd.memset(wgt[:, :, :], 0.0).then_inc(s_pad, 1)
            for t in range(TT):
                rms_rows(0, t)
            pool.wait_ge(s_masks, 2)
            nc.gpsimd.tensor_copy(ident_b[:, :], ident[:, :]).then_inc(s_masks, 1)
            nc.gpsimd.memset(causal[:, :], 0.0).then_inc(s_zeros_m, 1)
            nc.gpsimd.memset(causal_s[:, :], 0.0).then_inc(s_zeros_m, 1)
            nc.gpsimd.memset(chunk_mask[:, :], 0.0).then_inc(s_zeros_m, 1)
            pool.wait_ge(s_zeros_m, 3)
            nc.gpsimd.affine_select(out=causal[:, :], in_=causal[:, :], compare_op=ALU.is_gt, fill=BIG,
                                    base=0, pattern=[[-1, P]], channel_multiplier=1).then_inc(s_masks, 1)
            for h in range(2):
                r = slice(h * SMP, (h + 1) * SMP)
                pool.wait_ge(s_masks, 4 + h)
                nc.gpsimd.affine_select(out=causal_s[r, :], in_=causal_s[r, :], compare_op=ALU.is_gt, fill=BIG,
                                        base=0, pattern=[[-1, SMP]], channel_multiplier=1).then_inc(s_masks, 1)
            pool.wait_ge(s_masks, 6)
            nc.gpsimd.memset(chunk_mask[0:HD, HD:P], BIG).then_inc(s_masks, 1)
            split_group(0)

            def rms_a(q, par, c):
                sl = (par + c) % 2
                pool.wait_ge(s_mean, TT * q + c + 1)
                nc.gpsimd.tensor_tensor(rstd[:, sl, :], msq[:, sl, :], neg_half[:, :], ALU.pow).then_inc(s_rs, 1)

            def out_lo(p):
                pool.wait_ge(s_ghi, p + 1)
                nc.gpsimd.tensor_tensor(gt_pair(gt[1], p), gated[:, :], gt_pair(gt[0], p).bitcast(F32),
                                        ALU.subtract).then_inc(s_glo, 1)

            def step_a(p, par, att=True, ahead=True):
                for what, n in STEP_A:
                    if what == "C" and ahead:
                        rms_a(p + 1, 1 - par, n)
                    elif what == "W":
                        if n == 0 and not (isinstance(p, int) and p < 0):
                            sem, count = last_reader(p + 2)
                            pool.wait_ge(sem, count)
                        split_piece(p + 2, n, par, KD * 512)
                    elif (what, n) == ("O", 2) and att:
                        out_lo(p)

            step_a(-1, 1, att=False)
            step_a(0, 0)
            with pool.Fori(0, 3) as i:
                step_a(2 * i + 1, 1)
                step_a(2 * i + 2, 0)
            step_a(7, 1, ahead=False)

            nc.gpsimd.memset(gt[0][:, KD * TOK:FLAT].bitcast(F32), 0.0).then_inc(s_zeros_b, 1)
            nc.gpsimd.memset(gt[1][:, KD * TOK:FLAT].bitcast(F32), 0.0).then_inc(s_zeros_b, 1)
            split_group(G_LAT)
            for i in range(TT):
                rms_rows(1, i)

            split_group(G_KPE)

            def rms_lat(n):
                pool.wait_ge(s_lat_ss, n + 1)
                if n < TT:
                    nc.gpsimd.tensor_tensor(lat_ss[:, n, 0:1], lat_ss[:, n, 0:1], lat_ss[:, n, 2:3],
                                            ALU.add).then_inc(s_lat_sum, 1)
                    pool.wait_ge(s_lat_sum, n + 1)
                nc.gpsimd.tensor_scalar(lat_ms[:, n, 0:1], lat_ss[:, n, 0:1], 1.0 / KV, EPS,
                                        ALU.mult, ALU.add).then_inc(s_lat_ms, 1)
                w = 1
                if n < TT:
                    nc.gpsimd.tensor_scalar(lat_ms[:, n, 1:2], lat_ss[:, n, 1:2], 1.0 / ROPE, EPS,
                                            ALU.mult, ALU.add).then_inc(s_lat_ms, 1)
                    w = 2
                pool.wait_ge(s_lat_ms, 2 * (n + 1) if n < TT else TT + n + 1)
                nc.gpsimd.tensor_tensor(lat_r[:, n, 0:w], lat_ms[:, n, 0:w], neg_half[:, 0:w],
                                        ALU.pow).then_inc(s_lat_r, 1)

            for t in range(TT):
                rms_lat(t)
            split_group(G_QA)
            for m in range(2):
                pool.wait_ge(s_latm, TT)
                nc.gpsimd.memset(qat[m][:, KL * TOK:QFLAT].bitcast(F32), 0.0).then_inc(s_zeros_d, 1)
            for t in range(TT):
                rms_lat(TT + t)
                if t == 2:
                    split_group(G_GATE)
            split_group(G_GATE + 1)
            split_group(G_D)

            pool.wait_ge(s_latout, 32 * TT)
            pool.wait_ge(s_kpet_e, LT)
            pool.wait_ge(s_latx, LT + TT)
            pool.wait_ge(s_dve_c, CA * NP + 2 * NH)
            nc.gpsimd.memset(prob[:, 0, 0:SKEY], 0.0).then_inc(s_zeros_d, 1)

            def rms_d(q, par, what, t):
                c = CHUNK_D[what, t]
                sl = (par + c) % 2
                w = 4 if what == "Q" else 2
                pool.wait_ge(s_mean2, CD * q + c + 1)
                nc.gpsimd.tensor_tensor(rstd[:, sl, 0:w], msq[:, sl, 0:w], neg_half[:, 0:w],
                                        ALU.pow).then_inc(s_rs2, 1)

            def step_d(p, par, ahead=True):
                for what, n in STEP_D:
                    if what in "QK" and ahead:
                        rms_d(p + 1, 1 - par, what, n)
                    elif what == "W":
                        g = p + G_D + 2
                        if n == 0:
                            sem, count = last_reader_d(p)
                            pool.wait_ge(sem, count)
                        split_piece(g, n, g % 2, COLS[g])

            step_d(-1, 1)
            for p in range(MP):
                step_d(p, p % 2, ahead=p + 1 < MP)

            for m in range(2):
                pool.wait_ge(s_od2, 3 * MP)
                nc.gpsimd.memset(ht[m][:, KD * TOK:FLAT].bitcast(F32), 0.0).then_inc(s_zeros_e, 1)
            for K in range(KD):
                c = slice(K * TOK, (K + 1) * TOK)
                pool.wait_ge(s_go_hi, K + 1)
                nc.gpsimd.tensor_tensor(ht[1][:, c], sg[:, K, :], ht[0][:, c].bitcast(F32),
                                        ALU.subtract).then_inc(s_go_lo, 1)
            for t in range(TT):
                rms_rows(2, t)

        @block.vector
        def _(dve):
            v = nc.vector
            for t in range(TT):
                n = P if t < NT else SMP
                dve.wait_ge(s_row_r, t + 1)
                v.tensor_scalar(x_in[0:n, t, :], x_in[0:n, t, :], row_r[0:n, 0, t:t + 1], None,
                                ALU.mult).then_inc(s_xn, 1)
            dve.wait_ge(s_const_d, 16 * 13)
            v.tensor_scalar(g_qk[:, 0, :, :], g_qk[:, 0, :, :], HD ** -0.5, None, ALU.mult).then_inc(s_gscale, 1)
            v.tensor_scalar(g_q[:, :], g_q[:, :], QK ** -0.5, None, ALU.mult).then_inc(s_gscale, 1)
            v.memset(left[:, :, SEQ:SEQ + 1], 1.0).then_inc(s_gscale, 1)

            def low(dst, b, bs, K, gain, hi):
                c, e = slice(K * TOK, K * TOK + SEQ), slice(K * TOK + SEQ, (K + 1) * TOK)
                v.scalar_tensor_tensor(out=dst[:, c], in0=b[:, :], scalar=gain, in1=hi[:, c].bitcast(F32),
                                       op0=ALU.mult, op1=ALU.subtract)
                return v.scalar_tensor_tensor(out=dst[:, e], in0=bs[:, 0:SMP], scalar=gain, in1=hi[:, e].bitcast(F32),
                                              op0=ALU.mult, op1=ALU.subtract)

            dve.wait_ge(s_gcol, 1)
            for K in range(KD):
                dve.wait_ge(s_xt_hi, K + 1)
                low(ht[1], bank[4 + K % 2], bank[6 + K % 2], K, g_col[:, 0, K:K + 1], ht[0]).then_inc(s_xt_lo, 1)
            dve.wait_ge(s_gscale, 3)

            def chunk_a(q, par, c):
                sl = (par + c) % 2
                b = PRJ[sl]
                dve.wait_ge(s_sqd, TT * q + c + 1)
                if begun(TT * q + c - 1):
                    dve.wait_ge(s_rs, TT * q + c - 1)
                v.tensor_reduce(ssq[:, sl, :], sq[:, :].rearrange("p (a d) -> p a d", a=4), AX.X,
                                ALU.add).then_inc(s_msq_d, 1)
                dve.wait_ge(s_msq_d, TT * q + c + 1)
                v.tensor_scalar(msq[:, sl, :], ssq[:, sl, :], 1.0 / HD, EPS, ALU.mult, ALU.add).then_inc(s_mean, 1)
                dve.wait_ge(s_rs, TT * q + c + 1)
                dve.wait_ge(s_act_c, CA * q + c + 1)
                v.tensor_tensor(qkr[:, :].rearrange("p (a d) -> p a d", a=4),
                                b[:, 0:2 * P].rearrange("p (a d) -> p a d", a=4),
                                rstd[:, sl, :].unsqueeze(2).to_broadcast([P, 4, HD]), ALU.mult).then_inc(s_dve_c, 1)
                dve.wait_ge(s_dve_c, CA * q + c + 1)
                if c == 0:
                    if begun(XA * q):
                        dve.wait_ge(s_xpose, XA * q)
                    if begun(32 * q):
                        dve.wait_ge(s_kout, 32 * q)
                v.tensor_tensor(qkn[:, c, :, :].rearrange("p m d -> p (m d)"), qkr[:, :],
                                g_qk[:, :, :, :].rearrange("p m h d -> p (m h d)"), ALU.mult).then_inc(s_normed, 1)

            def gate_a(q, par, j):
                c = TT + j
                dve.wait_ge(s_act_c, CA * q + c + 1)
                v.tensor_tensor(sgate[:, par, j * HALF:(j + 1) * HALF], PRJ[(par + c) % 2][:, 0:HALF], sigm[:, :],
                                ALU.mult).then_inc(s_dve_c, 1)

            def weight_a(p, par, u):
                ub = (par + u) % 2
                dve.wait_ge(s_stay, UA * p + u + 1)
                r, n = (2 * SMP, SKEY) if u == 0 else (P, (UNIT_A[u][1] + 1) * P)
                back = stay[0:r, ub, SEQ - n:SEQ][:, ::-1]
                v.tensor_tensor_scan(out=left[0:r, ub, SEQ - n:SEQ][:, ::-1], data0=back, data1=back, initial=1.0,
                                     op0=ALU.mult, op1=ALU.bypass).then_inc(s_left, 1)
                dve.wait_ge(s_left, UA * p + u + 1)
                if begun(UA * p + u - 1):
                    dve.wait_ge(s_tr, UA * p + u - 1)
                v.tensor_tensor(wgt[0:r, ub, 0:n], left[0:r, ub, SEQ - n + 1:SEQ + 1], left[0:r, ub, SEQ - n:SEQ],
                                ALU.subtract).then_inc(s_wgt, 1)

            def gate_out(p, par, o):
                dve.wait_ge(s_av, 3 * p + o + 1)
                if o == 0:
                    if begun(p):
                        dve.wait_ge(s_ghi, p)
                    if begun(p):
                        dve.wait_ge(s_glo, p)
                r, c0, n = OUT_A[o]
                v.tensor_tensor(gated[r, c0:c0 + n], OUT[r, 0:n], sgate[r, par, c0:c0 + n], ALU.mult).then_inc(s_odone, 1)

            def step_a(p, par, att=True, ahead=True):
                for what, n in STEP_A:
                    if what == "C" and ahead:
                        chunk_a(p + 1, 1 - par, n)
                    elif what == "G" and ahead:
                        gate_a(p + 1, 1 - par, n)
                    elif what == "S" and att:
                        weight_a(p, par, n)
                    elif what == "O" and att:
                        gate_out(p, par, n)

            step_a(-1, 1, att=False)
            step_a(0, 0)
            with dve.Fori(0, 3) as i:
                step_a(2 * i + 1, 1)
                step_a(2 * i + 2, 0)
            step_a(7, 1, ahead=False)

            def add_x(i, nh):
                t = ORDER[i]
                n = P if t < NT else SMP
                c = slice(nh * 512, (nh + 1) * 512)
                m = TT * nh + i
                dve.wait_ge(s_x2d[t], 16)
                dve.wait_ge(s_yprod, m + 1)
                v.tensor_tensor(x2[0:n, t, c], bank[m % 4][0:n, :], x2[0:n, t, c], ALU.add).then_inc(s_x2sum, 1)

            def x2_lo(i):
                t = ORDER[i]
                n = P if t < NT else SMP
                for j in range(2):
                    dve.wait_ge(s_ct_hi, 2 * i + j + 1)
                    for k in range(KD // 2):
                        K = j * KD // 2 + k
                        src = bank[4 + 2 * (i % 2) + j][:, k * P:k * P + n]
                        c = slice(K * TOK + t * P, K * TOK + t * P + n)
                        for m, dst, hi in ((1, gt[1], gt[0]), (2, ht[1], ht[0])):
                            last = v.scalar_tensor_tensor(out=dst[:, c], in0=src, scalar=g_col[:, m, K:K + 1],
                                                          in1=hi[:, c].bitcast(F32), op0=ALU.mult, op1=ALU.subtract)
                    last.then_inc(s_ct_lo, 1)

            for i in range(TT):
                add_x(i, 0)
            for i in range(TT):
                add_x(i, 1)
                if i:
                    x2_lo(i - 1)
            x2_lo(TT - 1)

            def rotary_norm(src, r, gain):
                v.scalar_tensor_tensor(out=pe_tmp[:, 0, :], in0=src, scalar=r, in1=gain, op0=ALU.mult,
                                       op1=ALU.mult).then_inc(s_rope, 1)

            def rotate(dst, t, n):
                dve.wait_ge(s_rope, 3 * n + 1)
                v.tensor_tensor(pe_tmp[:, 1, :].rearrange("p (h d) -> p h d", h=2),
                                pe_tmp[:, 0, :].rearrange("p (h d) -> p h d", h=2),
                                cos_t[:, t, :].unsqueeze(1).to_broadcast([P, 2, ROPE // 2]),
                                ALU.mult).then_inc(s_rope, 1)
                swapped = pe_tmp[:, 0, :].rearrange("p (h d) -> p h d", h=2)[:, ::-1, :]
                v.tensor_tensor(pe_tmp[:, 2, :].rearrange("p (h d) -> p h d", h=2), swapped,
                                sin_t[:, t, :].rearrange("p (h d) -> p h d", h=2), ALU.mult).then_inc(s_rope, 1)
                dve.wait_ge(s_rope, 3 * n + 3)
                return v.tensor_tensor(dst.rearrange("p (h d) -> p h d", h=2),
                                       pe_tmp[:, 1, :].unsqueeze(1).to_broadcast([P, 2, ROPE]),
                                       pe_tmp[:, 2, :].unsqueeze(1).to_broadcast([P, 2, ROPE]), ALU.add)

            def lat_lo(i):
                t = ORDER[i] if i < TT else TT
                dve.wait_ge(s_lat_hi, i + 1)
                v.tensor_tensor(turned(latt[1], t, P), bank[4][:, :].rearrange("p (k c) -> p k c", k=KL),
                                turned(latt[0], t, P).bitcast(F32), ALU.subtract).then_inc(s_lat_lo, 1)

            def qa_lo(t):
                n = P if t < NT else SMP
                dve.wait_ge(s_lat_hi, LT + t + 1)
                v.tensor_tensor(turned(qat[1], t, n, width=TOK),
                                bank[4][:, :].rearrange("p (k c) -> p k c", k=KL)[:, :, 0:n],
                                turned(qat[0], t, n, width=TOK).bitcast(F32), ALU.subtract).then_inc(s_lat_lo, 1)

            dve.wait_ge(s_rows_g, 32)
            dve.wait_ge(s_x2out, 16 * TT)
            for i, t in enumerate(ORDER):
                b = bank[3 + 3 * (i % 2)]
                dve.wait_ge(s_lat_r, i + 1)
                rotary_norm(b[:, KV - LA:LB], lat_r[:, i, 1:2], g_kp[:, :])
                v.scalar_tensor_tensor(out=lat[:, t, 0:LA], in0=LAB[i % 3][:, 0:LA], scalar=lat_r[:, i, 0:1],
                                       in1=g_lat[:, 0:LA], op0=ALU.mult, op1=ALU.mult)
                v.scalar_tensor_tensor(out=lat[:, t, LA:KV], in0=b[:, 0:KV - LA], scalar=lat_r[:, i, 0:1],
                                       in1=g_lat[:, LA:KV], op0=ALU.mult, op1=ALU.mult).then_inc(s_latn, 1)
                rotate(kpe[:, t, :], t, i).then_inc(s_kper, 1)
                if i:
                    lat_lo(i - 1)
            lat_lo(TT - 1)
            for t in range(TT):
                dve.wait_ge(s_lat_r, TT + t + 1)
                if t:
                    dve.wait_ge(s_latx, LT + t)
                v.scalar_tensor_tensor(out=qan[:, :], in0=QAB[t % 2][:, :], scalar=lat_r[:, TT + t, 0:1],
                                       in1=g_qar[:, :], op0=ALU.mult, op1=ALU.mult).then_inc(s_latn, 1)
                if t == 0:
                    lat_lo(TT)
                if t:
                    qa_lo(t - 1)
            for n in range(2 * NH):
                dve.wait_ge(s_act_c, CA * NP + n + 1)
                v.tensor_tensor(sg[:, n // 2, (n % 2) * HALF:(n % 2 + 1) * HALF], bank[2 + n % 2][:, 0:HALF], sigc[:, :],
                                ALU.mult).then_inc(s_dve_c, 1)
                if n == 0:
                    qa_lo(TT - 1)

            dve.wait_ge(s_latout, 32 * TT)
            dve.wait_ge(s_kpet_e, LT)

            def sums_d(q, par, what, t):
                c = CHUNK_D[what, t]
                sl = (par + c) % 2
                if begun(CD * q + c - 1):
                    dve.wait_ge(s_rs2, CD * q + c - 1)
                if what == "Q":
                    dve.wait_ge(s_act2, CD * q + c + 1)
                    by_head = sqd[:, 0:WQ].rearrange("p (h d) -> p h d", h=2)
                    v.tensor_reduce(ssq[:, sl, 0:2], by_head[:, :, 0:NOPE], AX.X, ALU.add)
                    v.tensor_reduce(ssq[:, sl, 2:4], by_head[:, :, NOPE:QK], AX.X, ALU.add).then_inc(s_sum2, 1)
                    dve.wait_ge(s_sum2, CD * q + c + 1)
                    v.tensor_scalar(msq[:, sl, 2:4], ssq[:, sl, 2:4], 1.0 / ROPE, EPS, ALU.mult, ALU.add)
                else:
                    dve.wait_ge(s_sqk, LT * q + t + 1)
                    v.tensor_reduce(ssq[:, sl, 0:2], sqd[:, 0:2 * NOPE].rearrange("p (h d) -> p h d", h=2), AX.X,
                                    ALU.add).then_inc(s_sum2, 1)
                    dve.wait_ge(s_sum2, CD * q + c + 1)
                v.tensor_scalar(msq[:, sl, 0:2], ssq[:, sl, 0:2], 1.0 / NOPE, EPS, ALU.mult,
                                ALU.add).then_inc(s_mean2, 1)

            def norm_d(q, par, what, t):
                c = CHUNK_D[what, t]
                sl = (par + c) % 2
                b = PRJ[sl]
                dve.wait_ge(s_rs2, CD * q + c + 1)
                dve.wait_ge(s_act2, CD * q + c + 1)
                before = CD * q + (CHUNK_D[what, t - 2] + 1 if t > 1 else 0)
                if begun(before):
                    dve.wait_ge(s_xp2, before)
                if what == "K":
                    for h in range(2):
                        last = v.scalar_tensor_tensor(out=kn2[:, t % 2, h * NOPE:(h + 1) * NOPE],
                                                      in0=b[:, h * 256:h * 256 + NOPE], scalar=rstd[:, sl, h:h + 1],
                                                      in1=g_kn[:, :], op0=ALU.mult, op1=ALU.mult)
                    last.then_inc(s_dve2, 1)
                    return
                n3 = 3 * (TT * q + t)
                for h in range(2):
                    last = v.scalar_tensor_tensor(out=pe_tmp2[:, 0, h * ROPE:(h + 1) * ROPE],
                                                  in0=b[:, h * QK + NOPE:(h + 1) * QK], scalar=rstd[:, sl, 2 + h:3 + h],
                                                  in1=g_q[:, NOPE:QK], op0=ALU.mult, op1=ALU.mult)
                last.then_inc(s_rope2, 1)
                for h in range(2):
                    last = v.scalar_tensor_tensor(out=qn2[:, t % 2, h * NOPE:(h + 1) * NOPE],
                                                  in0=b[:, h * QK:h * QK + NOPE], scalar=rstd[:, sl, h:h + 1],
                                                  in1=g_q[:, 0:NOPE], op0=ALU.mult, op1=ALU.mult)
                last.then_inc(s_dve2, 1)
                dve.wait_ge(s_rope2, n3 + 1)
                v.tensor_tensor(pe_tmp2[:, 1, :].rearrange("p (h d) -> p h d", h=4),
                                pe_tmp2[:, 0, :].rearrange("p (h d) -> p h d", h=4),
                                cos_t[:, t, :].unsqueeze(1).to_broadcast([P, 4, ROPE // 2]),
                                ALU.mult).then_inc(s_rope2, 1)
                swapped = pe_tmp2[:, 0, :].rearrange("p (h s d) -> p h s d", h=2, s=2)[:, :, ::-1, :]
                v.tensor_tensor(pe_tmp2[:, 2, :].rearrange("p (h s d) -> p h s d", h=2, s=2), swapped,
                                sin_t[:, t, :].rearrange("p (s d) -> p s d", s=2).unsqueeze(1)
                                .to_broadcast([P, 2, 2, ROPE // 2]), ALU.mult).then_inc(s_rope2, 1)
                dve.wait_ge(s_rope2, n3 + 3)
                v.tensor_tensor(qn2[:, t % 2, 2 * NOPE:WQ], pe_tmp2[:, 1, :], pe_tmp2[:, 2, :],
                                ALU.add).then_inc(s_nrm2, 1)

            def rows_d(par, u):
                ub = (par + u) % 2
                return (ub, 2 * SMP, SKEY) if u == 0 else (ub, P, (UNIT_A[u][1] + 1) * P)

            def max_d(p, par, u):
                ub, r, n = rows_d(par, u)
                dve.wait_ge(s_score2, UA * p + u + 1)
                v.tensor_reduce(neg_max[0:r, ub:ub + 1], SCR[ub][0:r, 0:n], AX.X, ALU.max,
                                negate=True).then_inc(s_negmax, 1)

            def scale_d(p, par, u):
                ub, r, n = rows_d(par, u)
                dve.wait_ge(s_expd, UA * p + u + 1)
                v.reciprocal(p_inv[0:r, ub:ub + 1], p_sum[0:r, ub:ub + 1]).then_inc(s_inv, 1)
                dve.wait_ge(s_inv, UA * p + u + 1)
                v.tensor_scalar(prob[0:r, ub, 0:n], prob[0:r, ub, 0:n], p_inv[0:r, ub:ub + 1], None,
                                ALU.mult).then_inc(s_scaled, 1)

            def gate_out_d(p, o):
                dve.wait_ge(s_av2, 3 * p + o + 1)
                if o == 0:
                    heads = sg[:, 2 * p:2 * p + 2, SEQ:TOK]
                    v.tensor_tensor(heads, OUT[:, 0:2 * SMP].rearrange("p (h c) -> p h c", h=2), heads,
                                    ALU.mult).then_inc(s_od2, 1)
                    return
                head = sg[:, 2 * p + o - 1, 0:SEQ]
                v.tensor_tensor(head, OUT[:, 0:SEQ], head, ALU.mult).then_inc(s_od2, 1)

            def step_d(p, par, att=True, ahead=True):
                for what, n in STEP_D:
                    if what in "QK" and ahead:
                        sums_d(p + 1, 1 - par, what, n)
                    elif what == "N" and ahead:
                        norm_d(p + 1, 1 - par, *CHUNKS[n])
                    elif what == "S" and att:
                        max_d(p, par, n)
                    elif what == "R" and att:
                        scale_d(p, par, n)
                    elif what == "O" and att:
                        gate_out_d(p, n)

            step_d(-1, 1, att=False)
            for p in range(MP):
                step_d(p, p % 2, ahead=p + 1 < MP)

            def norm_y(t):
                n = P if t < NT else SMP
                dve.wait_ge(s_row_r, 2 * TT + t + 1)
                v.scalar_tensor_tensor(out=x2e[0:n, t, :], in0=x2e[0:n, t, :], scalar=row_r[0:n, 2, t:t + 1],
                                       in1=g_fin[0:n, :], op0=ALU.mult, op1=ALU.mult).then_inc(s_yn, 1)

            dve.wait_ge(s_gfin, 16)
            for t in range(TT):
                n = P if t < NT else SMP
                dve.wait_ge(s_x2in[t], 16)
                for nh in range(2):
                    c = slice(nh * 512, (nh + 1) * 512)
                    m = 2 * t + nh
                    dve.wait_ge(s_yprod, 2 * TT + m + 1)
                    v.tensor_tensor(x2e[0:n, t, c], bank[m % 4][0:n, :], x2e[0:n, t, c], ALU.add).then_inc(s_ysum, 1)
                if t:
                    norm_y(t - 1)
            norm_y(TT - 1)


_INS = ["x_prompt", "x_sample", "cache_sb_k", "cache_sb_v", "cache_mla_latent", "cache_mla_kpe", "g_pre_a",
        "w_in_a", "g_q_a", "g_k_a", "w_o_a", "g_kv", "w_kv_a", "g_kv_a", "g_kpe", "w_kv_b", "g_knope", "g_pre_b",
        "w_in_b", "g_qa", "w_q_b", "g_qn", "g_qp", "w_o_b", "g_final"]
_OUTS = [(1, SEQ, D), (1, SMP, D), (1, 1, SEQ, 16, HD), (1, 1, SEQ, 16, HD), (1, SEQ, KV), (1, SEQ, ROPE),
         (1, 1, SMP, 16, HD), (1, 1, SMP, 16, HD), (1, SMP, KV), (1, SMP, ROPE)]


def kernel(**inputs):
    import concourse.bacc as bacc
    from concourse.bass_utils import run_bass_kernel_spmd

    nc = bacc.Bacc("TRN2", target_bir_lowering=False, num_devices=1)
    cos, sin = rope_tables()
    arrays = {f"in_{n}": np.ascontiguousarray(inputs[n]) for n in _INS}
    arrays["in_rope_cos"], arrays["in_rope_sin"] = cos, sin
    a = {n[3:]: nc.dram_tensor(n, v.shape, F32, kind="ExternalInput").ap() for n, v in arrays.items()}
    out = [nc.dram_tensor(f"out_{i}", sh, F32, kind="ExternalOutput").ap() for i, sh in enumerate(_OUTS)]
    scratch = nc.dram_tensor("x2_scratch", (TT * P, D), F32, kind="Internal").ap()
    build(nc, a, out, scratch)
    r = run_bass_kernel_spmd(nc, [arrays], core_ids=[0])
    return tuple(r.results[0][f"out_{i}"] for i in range(len(_OUTS)))
```

```python
from contextlib import ExitStack

import numpy as np

import concourse.bass as bass
from concourse import mybir

F32 = mybir.dt.float32
F32R = mybir.dt.float32r
BF16 = mybir.dt.bfloat16
ALU = mybir.AluOpType
ACT = mybir.ActivationFunctionType
AX = mybir.AxisListType

P = 128
D = 1024
KD = D // P
SEQ, SMP, PAST = 512, 32, 128
NT = SEQ // P
TT = NT + 1
TOK = SEQ + SMP
HALF = TOK // 2
FLAT = KD * TOK + P - SMP
HD = 64
NP = D // P
KV = 512
KL = KV // P
QFLAT = KL * TOK + P - SMP
NH = 8
MP = NH // 2
NOPE, ROPE, VD = 128, 64, 128
QK = NOPE + ROPE
WQ, WK = 2 * QK, 2 * (NOPE + VD)
WD = WQ + WK
LT = TT + 1
KEYS = TOK + PAST
SKEY = SMP + PAST
EPS = 1e-6
BIG = -1e30

G_OA, G_LAT, G_KPE, G_QA, G_GATE, G_D, G_OB = NP, NP + 2, NP + 3, NP + 4, NP + 5, NP + 7, NP + 7 + MP
LA = 320
LB = KV + ROPE - LA
POOL_SHARE = 512
PIECES = 4
COLS = {g: KD * 512 for g in range(G_OB + 2)}
COLS[G_LAT], COLS[G_KPE] = KD * LA, KD * LB
for _g in range(G_D, G_OB):
    COLS[_g] = KL * WD

UA = 1 + 2 * NT
UNIT_A = [None] + [(h, i) for i in reversed(range(NT)) for h in range(2)]
OA = 1 + NT
CA = TT + 2
XA = TT + 1
STEP_A = [("S", 0), ("C", 0), ("S", 1), ("W", 0), ("T", 0), ("C", 1), ("C", 2), ("S", 2), ("X", 0), ("W", 1),
          ("W", 2), ("T", 1), ("C", 3), ("O", 0), ("X", 1), ("S", 3), ("X", 2), ("T", 2), ("S", 4), ("W", 3),
          ("C", 4), ("O", 1), ("T", 3), ("S", 5), ("T", 4), ("G", 0), ("S", 6), ("X", 3), ("O", 2), ("T", 5),
          ("S", 7), ("T", 6), ("S", 8), ("G", 1), ("X", 4), ("T", 7), ("T", 8), ("O", 3), ("Z", 0), ("O", 4)]
ORDER = [NT] + list(range(NT))
UNIT_D = [None] + [(h, i) for h in range(2) for i in reversed(range(NT))]
CD = TT + LT
CHUNKS = [(w, t) for t in range(LT) for w in "QK" if (w, t) != ("Q", TT)]
CHUNK_D = {s: n for n, s in enumerate(CHUNKS)}
TURN = {"Q": "X", "K": "Y"}
STEP_D = [("Q", 0), ("P", 5), ("N", 0), ("K", 0), ("S", 0), ("N", 1), ("R", 0), ("Q", 1), ("X", 0), ("S", 1),
          ("N", 2), ("Y", 0), ("R", 1), ("T", 0), ("K", 1), ("S", 2), ("N", 3), ("W", 0), ("R", 2), ("O", 0),
          ("T", 1), ("Q", 2), ("S", 3), ("X", 1), ("N", 4), ("R", 3), ("K", 2), ("Y", 1), ("Q", 3), ("T", 2),
          ("S", 4), ("N", 5), ("W", 1), ("R", 4), ("T", 3), ("X", 2), ("S", 5), ("N", 6), ("R", 5), ("T", 4),
          ("K", 3), ("N", 7), ("Y", 2), ("S", 6), ("W", 2), ("R", 6), ("O", 1), ("T", 5), ("X", 3), ("Q", 4),
          ("S", 7), ("R", 7), ("N", 8), ("T", 6), ("K", 4), ("Y", 3), ("N", 9), ("W", 3), ("S", 8), ("R", 8),
          ("T", 7), ("K", 5), ("X", 4), ("N", 10), ("T", 8), ("Y", 4), ("O", 2)]
FILL_D = []
for _j, _chunk in enumerate(CHUNKS):
    FILL_D.append(_chunk)
    if _j:
        FILL_D.append(("N", _j - 1))
    if _j in (2, 4, 6, 8):
        FILL_D.append(("W", (_j - 2) // 2))
    if _j > 2:
        FILL_D.append((TURN[CHUNKS[_j - 3][0]], CHUNKS[_j - 3][1]))
FILL_D += [("N", CD - 1)] + [(TURN[CHUNKS[_j][0]], CHUNKS[_j][1]) for _j in (CD - 3, CD - 2)]
LAST_D = [("P", TT),
          ("S", 0), ("R", 0), ("H", 0), ("W", 0), ("S", 1), ("R", 1), ("H", 1), ("T", 0), ("S", 2), ("R", 2),
          ("E", 0), ("H", 2), ("W", 1), ("T", 1), ("O", 0), ("S", 3), ("R", 3), ("E", 1), ("H", 3), ("T", 2),
          ("S", 4), ("R", 4), ("E", 2), ("F", 0), ("H", 4), ("W", 2), ("T", 3), ("S", 5), ("R", 5), ("E", 3),
          ("F", 1), ("H", 5), ("T", 4), ("S", 6), ("R", 6), ("O", 1), ("E", 4), ("W", 3), ("T", 5), ("S", 7),
          ("R", 7), ("E", 5), ("F", 2), ("T", 6), ("S", 8), ("R", 8), ("F", 3), ("T", 7), ("H", 6), ("F", 4),
          ("F", 5), ("T", 8), ("E", 6), ("F", 6), ("O", 2)]
AHEAD = {"C", "G", "X", "Z", "Q", "K", "Y", "N"}


def order_d(p):
    return FILL_D if p < 0 else STEP_D if p + 1 < MP else LAST_D


def rope_tables():
    half = ROPE // 2
    inv = np.float32(10000.0) ** (-np.arange(half, dtype=np.float32) / np.float32(half))
    pos = np.zeros(TT * P, np.float32)
    pos[:SEQ] = np.arange(SEQ)
    pos[SEQ:TOK] = PAST + np.arange(SMP)
    ang = (pos[:, None] * inv[None, :].astype(np.float32)).astype(np.float32)
    cos, sin = np.cos(ang).astype(np.float32), np.sin(ang).astype(np.float32)
    return cos, np.concatenate([-sin, sin], 1)


def build(nc, a, out, scratch):
    x_p = a["x_prompt"][0].rearrange("(t p) d -> p t d", p=P)
    x_s = a["x_sample"][0]
    w_in = a["w_in_a"][0].rearrange("(k p) (f m) -> p k f m", p=P, f=4)
    w_oa = a["w_o_a"][0].rearrange("(k p) n -> p k n", p=P)
    w_ob = a["w_o_b"][0].rearrange("(k p) n -> p k n", p=P)
    w_kva = a["w_kv_a"].rearrange("(k p) n -> p k n", p=P)
    w_inb = a["w_in_b"][0].rearrange("(k p) n -> p k n", p=P)
    w_qb = a["w_q_b"][0].rearrange("(k p) n -> p k n", p=P)
    w_kvb = a["w_kv_b"].rearrange("(k p) n -> p k n", p=P)
    ck = a["cache_sb_k"][0, 0].rearrange("t h d -> t (h d)")
    cv = a["cache_sb_v"][0, 0].rearrange("t h d -> t (h d)")
    y_p, y_s, k_p, v_p, lat_p, kpe_p, k_s, v_s, lat_s, kpe_s = out
    ko_p = k_p[0, 0].rearrange("(t p) h d -> p t (h d)", p=P)
    vo_p = v_p[0, 0].rearrange("(t p) h d -> p t (h d)", p=P)
    ko_s = k_s[0, 0].rearrange("p h d -> p (h d)")
    vo_s = v_s[0, 0].rearrange("p h d -> p (h d)")

    with ExitStack() as ctx:
        base = (nc.sbuf_base + 63) // 64 * 64
        arena = nc.sbuf_usable_end - base
        at = [0]

        def place(name, shape, dt, off=None):
            size = int(np.prod(shape[1:])) * (2 if dt == BF16 else 4)
            size = (size + 31) // 32 * 32
            o = at[0] if off is None else off
            if off is None:
                at[0] += size
            assert o + size <= arena, (name, o + size, arena)
            return nc.alloc_sbuf_tensor_at(name, shape, dt, offset=base + o), o + size

        def keep(name, shape, dt=F32):
            return place(name, shape, dt)[0]

        def alias(name, shape, off, dt=F32):
            return place(name, shape, dt, off)

        ident = keep("ident", [P, P])
        ident_b = keep("ident_b", [P, P], BF16)
        causal = keep("causal", [P, P], BF16)
        causal_s = keep("causal_s", [P, SMP], BF16)
        chunk_mask = keep("chunk_mask", [P, P], BF16)
        g_qk = keep("g_qk", [P, 2, 2, HD])
        g_q = keep("g_q", [P, QK])
        g_kn = keep("g_kn", [P, NOPE])
        g_kp = keep("g_kp", [P, ROPE])
        g_col = keep("g_col", [P, 3, KD])
        cos_t = keep("cos_t", [P, TT, ROPE // 2])
        sin_t = keep("sin_t", [P, TT, ROPE])
        neg_half = keep("neg_half", [P, 4])
        lat_ss = keep("lat_ss", [P, 2 * TT, 3])
        lat_ms = keep("lat_ms", [P, 2 * TT, 2])
        lat_r = keep("lat_r", [P, 2 * TT, 2])
        sq_pe = keep("sq_pe", [P, ROPE])
        pe_tmp = keep("pe_tmp", [P, 3, ROPE])
        ssq = keep("ssq", [P, 2, 4])
        msq = keep("msq", [P, 2, 4])
        rstd = keep("rstd", [P, 2, 4])
        row_ss = keep("row_ss", [P, 3, TT])
        row_ms = keep("row_ms", [P, 3, TT])
        row_r = keep("row_r", [P, 3, TT])
        neg_max = keep("neg_max", [P, 2])
        p_sum = keep("p_sum", [P, 2])
        p_inv = keep("p_inv", [P, 2])
        raw = keep("raw", [P, KD * 512])
        whi = [keep(f"whi{s}", [P, KD * 512], F32R) for s in range(2)]
        wlo = [keep(f"wlo{s}", [P, KD * 512], F32R) for s in range(2)]
        o_ht = at[0]
        ht = [keep(f"ht{s}", [P, FLAT], F32R) for s in ("hi", "lo")]
        o_gt = at[0]
        gt = [keep(f"gt{s}", [P, FLAT], F32R) for s in ("hi", "lo")]
        o_s = at[0]
        x_in, _ = alias("x_in", [P, TT, D], o_gt)
        qkt, o = alias("qkt", [P, 2, 2, TOK], o_s)
        vtok, o = alias("vtok", [P, 2, TT, P], o)
        qkn, o = alias("qkn", [P, TT, 2, P], o)
        kc, o = alias("kc", [P, 2, P], o)
        vc, o = alias("vc", [P, 2, P], o)
        kct, o = alias("kct", [P, 2, P], o)
        sgate, o = alias("sgate", [P, 2, TOK], o)
        dump_x, og = alias("dump_x", [P, D], o)
        g_rows, _ = alias("g_rows", [3 * KD, P], og)
        wt, o = alias("wt", [P, 2, NT, 2, P], o)
        wts, o = alias("wts", [P, 2, 2 * SMP], o)
        stay, o = alias("stay", [P, 2, SEQ], o)
        left, o = alias("left", [P, 2, SEQ + 1], o)
        wgt, o = alias("wgt", [P, 2, SEQ], o)
        sigm, _ = alias("sigm", [P, HALF], o)
        sq, o = alias("sq", [P, 2 * P], o)
        qkr, o = alias("qkr", [P, 2 * P], o)
        gated, o = alias("gated", [P, TOK], o)
        x2, o = alias("x2", [P, TT, D], o_s)
        xn, o = alias("xn", [P, TT, D], o)
        dump, _ = alias("dump", [P, D], o)
        lath, o = alias("lath", [P, KL * LT * P], o_s, F32R)
        latl, o = alias("latl", [P, KL * LT * P], o, F32R)
        kpet, o_d = alias("kpet", [P, KEYS], o)
        lat, o = alias("lat", [P, LT, KV], o_d)
        kpe, o = alias("kpe", [P, LT, P], o)
        qan, o = alias("qan", [P, KV], o)
        sigc, _ = alias("sigc", [P, HALF], o)
        sqc, o = alias("sqc", [P, KV], o)
        g_lat, o = alias("g_lat", [P, KV], max(o, o_s + 8 * TT * D))
        g_qar, o = alias("g_qar", [P, KV], o)
        qat0, o = alias("qat0", [P, QFLAT], o_gt, F32R)
        qat1, o = alias("qat1", [P, QFLAT], o, F32R)
        qat = [qat0, qat1]
        latt = [lath, latl]
        o_sg = o
        sg_flat, _ = alias("sg", [P, NH * TOK], o)
        sg = sg_flat[:, :].rearrange("p (h t) -> p h t", h=NH)
        q2t, o = alias("q2t", [P, 2, 3, TOK], o_ht)
        k2t, o = alias("k2t", [P, 2, 2, KEYS], o)
        o_k2t = o
        wt2, o = alias("wt2", [P, NT, SEQ], o)
        sqd, o = alias("sqd", [P, WQ], o)
        pe_tmp2, o = alias("pe_tmp2", [P, 3, 2 * ROPE], o)
        assert o <= o_gt
        v2, o = alias("v2", [P, 2, 2, LT, P], o_d)
        qn2, o = alias("qn2", [P, 2, WQ], o)
        kn2, o = alias("kn2", [P, 2, 2 * NOPE], o)
        wts2, o = alias("wts2", [P, 2, 2 * SMP], o)
        prob, o = alias("prob", [P, 2, SEQ], o)
        ghi, o = alias("ghi", [P, FLAT], o_gt, F32R)
        assert o <= o_sg
        glo, o = alias("glo", [P, FLAT], o_s, F32R)
        g_fin, _ = alias("g_fin", [P, D], o)
        x2e, o = alias("x2e", [P, TT, D], o_ht)
        assert o <= o_k2t
        dump2, o = alias("dump2", [P, D], o)

        bank = [ctx.enter_context(nc.psum_tensor(f"bank{b}", [P, 512], F32)) for b in range(8)]
        XTB = [(bank[4], bank[5]), (bank[2], bank[3])]
        LAB, QAB = [bank[2], bank[0], bank[1]], [bank[1], bank[0]]
        PRJ, SCR, TRB, OUT, XB = bank[0:2], bank[2:4], bank[4:6], bank[6], bank[7]

        def sem(name):
            return ctx.enter_context(nc.semaphore(name))

        s_hi = sem("s_hi")
        s_lo = sem("s_lo")
        s_lo_dve = sem("s_lo_dve")
        s_raw = [sem(f"s_raw{j}") for j in range(PIECES)]
        s_kcd = [sem(f"s_kcd{i}") for i in range(2)]
        s_vcd = [sem(f"s_vcd{i}") for i in range(2)]
        s_x_in = [sem(f"s_x_in{i}") for i in range(TT)]
        s_rope_d = sem("s_rope_d")
        s_rows_d = sem("s_rows_d")
        s_const_d = sem("s_const_d")
        s_normed = sem("s_normed")
        s_kout = sem("s_kout")
        s_act_c = sem("s_act_c")
        s_vout = [sem(f"s_vout{i}") for i in range(2)]
        s_av = sem("s_av")
        s_glo = sem("s_glo")
        s_x2d = [sem(f"s_x2d{i}") for i in range(TT)]
        s_rows_g = sem("s_rows_g")
        s_x2sum = sem("s_x2sum")
        s_x2out = sem("s_x2out")
        s_ct = sem("s_ct")
        s_latc = sem("s_latc")
        s_latn = sem("s_latn")
        s_kper = sem("s_kper")
        s_latout = sem("s_latout")
        s_proj2 = sem("s_proj2")
        s_proj = sem("s_proj")
        s_od2 = sem("s_od2")
        s_x2in = [sem(f"s_x2in{i}") for i in range(TT)]
        s_gfin = sem("s_gfin")
        s_yn = sem("s_yn")
        s_yout = sem("s_yout")
        s_xt_hi = sem("s_xt_hi")
        s_xt = sem("s_xt")
        s_xt_lo = sem("s_xt_lo")
        s_dve_c = sem("s_dve_c")
        s_xev = sem("s_xev")
        s_xpose = sem("s_xpose")
        s_stay = sem("s_stay")
        s_score = sem("s_score")
        s_wgt = sem("s_wgt")
        s_wtev = sem("s_wtev")
        s_tr = sem("s_tr")
        s_odone = sem("s_odone")
        s_gcol = sem("s_gcol")
        s_xn = sem("s_xn")
        s_masks = sem("s_masks")
        s_gcol_t = sem("s_gcol_t")
        s_pad = sem("s_pad")
        s_ghi = sem("s_ghi")
        s_zeros_b = sem("s_zeros_b")
        s_yprod = sem("s_yprod")
        s_ct_lo = sem("s_ct_lo")
        s_ct_hi = sem("s_ct_hi")
        s_lat_lo = sem("s_lat_lo")
        s_kpet_e = sem("s_kpet_e")
        s_latx = sem("s_latx")
        s_lata = sem("s_lata")
        s_latm = sem("s_latm")
        s_lat_hi = sem("s_lat_hi")
        s_zeros_d = sem("s_zeros_d")
        s_act2 = sem("s_act2")
        s_dve2 = sem("s_dve2")
        s_nrm2 = sem("s_nrm2")
        s_xev2 = sem("s_xev2")
        s_xp2 = sem("s_xp2")
        s_expd = sem("s_expd")
        s_score2 = sem("s_score2")
        s_scaled = sem("s_scaled")
        s_wtev2 = sem("s_wtev2")
        s_tr2 = sem("s_tr2")
        s_av2 = sem("s_av2")
        s_zeros_e = sem("s_zeros_e")
        s_go_hi = sem("s_go_hi")
        s_go_lo = sem("s_go_lo")
        s_ysum = sem("s_ysum")
        s_row_ss = sem("s_row_ss")
        s_msq_d = sem("s_msq_d")
        s_sqd = sem("s_sqd")
        s_left = sem("s_left")
        s_lat_sum = sem("s_lat_sum")
        s_lat_ss = sem("s_lat_ss")
        s_sqk = sem("s_sqk")
        s_sum2 = sem("s_sum2")
        s_mean2 = sem("s_mean2")
        s_rope2 = sem("s_rope2")
        s_mean = sem("s_mean")
        s_negmax = sem("s_negmax")
        s_row_ms = sem("s_row_ms")
        s_row_r = sem("s_row_r")
        s_zeros_m = sem("s_zeros_m")
        s_rs = sem("s_rs")
        s_lat_ms = sem("s_lat_ms")
        s_lat_r = sem("s_lat_r")
        s_rs2 = sem("s_rs2")
        s_gscale = sem("s_gscale")
        s_rope = sem("s_rope")
        s_inv = sem("s_inv")

        def begun(v):
            return not isinstance(v, int) or v > 0

        def chunk_bank(q, par, c):
            return (PRJ + TRB)[c % 4] if q == 0 else PRJ[(par + c) % 2]

        def raw_count(g):
            return 32 * (g + 1)

        def wcol(g, part, k, c0, n, per):
            t = (whi, wlo)[part][g % 2]
            return t[:, k * per + c0:k * per + c0 + n]

        def acol(t, k, tile, width=TOK):
            return t[:, k * width + tile * P:k * width + tile * P + P]

        def three(eng, dst, pairs, ready=None):
            n = len(pairs)
            for k, (st, mv) in enumerate(pairs):
                if ready:
                    ready(k)
                eng.matmul(dst, st[0], mv[0], start=(k == 0), stop=False)
                eng.matmul(dst, st[0], mv[1], start=False, stop=False)
                mm = eng.matmul(dst, st[1], mv[0], start=False, stop=(k == n - 1))
            return mm

        block = ctx.enter_context(nc.Block())

        @block.sync
        def _(sp):
            def load_group(g, piece):
                for j in range(PIECES):
                    if not isinstance(g, int) or g:
                        known = isinstance(g, int)
                        split = j + 1
                        if known:
                            split = max(split, min(PIECES, -(-(j + 1) * COLS[g] // COLS[g - 1])))
                        sp.wait_ge(s_hi, PIECES * (g - 1) + split)
                        sp.wait_ge(s_lo, PIECES * (g - 1) + split)
                        if known and g == 1:
                            sp.wait_ge(s_lo_dve, split)
                    for dst, src in piece(j):
                        sp.dma_start(dst, src).then_inc(s_raw[j], 16)

            def load_pair(g):
                v = raw[:, :].rearrange("p (k f c) -> p k f c", k=KD, f=4)
                load_group(g, lambda j: [(v[:, k, :, :], w_in[:, k, :, bass.ds(g * P, P)])
                                         for k in (2 * j, 2 * j + 1)])

            def load_cols(g, w, c0, n):
                v = raw[:, 0:KD * n].rearrange("p (k c) -> p k c", k=KD)
                load_group(g, lambda j: [(v[:, k, :], w[:, k, c0:c0 + n]) for k in (2 * j, 2 * j + 1)])

            def load_heads(m):
                v = raw[:, 0:COLS[G_D]].rearrange("p (k c) -> p k c", k=KL)
                load_group(G_D + m, lambda j: [(v[:, j, 0:WQ], w_qb[:, j, m * WQ:(m + 1) * WQ]),
                                               (v[:, j, WQ:], w_kvb[:, j, m * WK:(m + 1) * WK])])

            def load_late(g):
                if g < NP:
                    load_pair(g)
                elif g < G_LAT:
                    load_cols(g, w_oa, (g - G_OA) * 512, 512)
                elif g == G_LAT:
                    load_cols(g, w_kva, 0, LA)
                elif g == G_KPE:
                    load_cols(g, w_kva, LA, LB)
                elif g == G_QA:
                    load_cols(g, w_inb, 0, 512)
                elif g < G_D:
                    load_cols(g, w_inb, (g - G_GATE + 1) * 512, 512)
                elif g < G_OB:
                    load_heads(g - G_D)
                elif g < G_OB + 2:
                    load_cols(g, w_ob, (g - G_OB) * 512, 512)

            def cache_pair(q, par):
                sp.dma_start(kc[:, par, :], ck[:, bass.ds(q * P, P)]).then_inc(s_kcd[par], 16)
                sp.dma_start(vc[:, par, :], cv[:, bass.ds(q * P, P)]).then_inc(s_vcd[par], 16)

            def load_x(t):
                if t < NT:
                    sp.dma_start(x_in[:, t, :], x_p[:, t, :]).then_inc(s_x_in[t], 16)
                else:
                    sp.dma_start(x_in[0:SMP, NT, :], x_s).then_inc(s_x_in[NT], 16)

            load_x(0)
            for m, g in enumerate((a["g_pre_a"][0], a["g_kv"], a["g_pre_b"][0])):
                sp.dma_start(g_rows[m * KD:(m + 1) * KD, :], g.rearrange("(k p) -> k p", p=P)).then_inc(s_rows_d, 16)
            load_x(1)
            load_pair(0)
            load_x(2)
            for dst, src in [
                    (g_qk[:, 0, 0, :], a["g_q_a"].to_broadcast([P, HD])),
                    (g_qk[:, 0, 1, :], a["g_q_a"].to_broadcast([P, HD])),
                    (g_qk[:, 1, 0, :], a["g_k_a"].to_broadcast([P, HD])),
                    (g_qk[:, 1, 1, :], a["g_k_a"].to_broadcast([P, HD])),
                    (g_q[:, 0:NOPE], a["g_qn"].to_broadcast([P, NOPE])),
                    (g_q[:, NOPE:], a["g_qp"].to_broadcast([P, ROPE])),
                    (g_kn[:, :], a["g_knope"].rearrange("(a n) -> a n", a=1).to_broadcast([P, NOPE])),
                    (g_kp[:, :], a["g_kpe"].rearrange("(a n) -> a n", a=1).to_broadcast([P, ROPE]))]:
                sp.dma_start(dst, src).then_inc(s_const_d, 16)
            load_x(3)
            load_x(4)
            for dst, src in [(cos_t[:, :, :], a["rope_cos"].rearrange("(t p) d -> p t d", p=P)),
                             (sin_t[:, :, :], a["rope_sin"].rearrange("(t p) d -> p t d", p=P))]:
                sp.dma_start(dst, src).then_inc(s_rope_d, 16)
            load_pair(1)
            cache_pair(0, 0)
            cache_pair(1, 1)

            def outputs(q, par):
                sp.wait_ge(s_normed, TT * (q + 1))
                cols = bass.ds(q * P, P)
                sp.dma_start(ko_p[:, :, cols], qkn[:, 0:NT, 1, :]).then_inc(s_kout, 16)
                sp.dma_start(ko_s[:, cols], qkn[0:SMP, NT, 1, :]).then_inc(s_kout, 16)
                sp.wait_ge(s_act_c, CA * q + TT)
                sp.dma_start(vo_p[:, :, cols], vtok[:, par, 0:NT, :]).then_inc(s_vout[par], 16)
                sp.dma_start(vo_s[:, cols], vtok[0:SMP, par, NT, :]).then_inc(s_vout[par], 16)

            def step(p, par, last=False):
                if isinstance(p, int) and p + 3 >= NP:
                    load_late(p + 3)
                else:
                    load_pair(p + 3)
                if not (isinstance(p, int) and (p + 2 >= NP or p < 0)):
                    sp.wait_ge(s_av, OA * p + 1)
                    cache_pair(p + 2, par)
                if not last:
                    outputs(p + 1, 1 - par)

            step(-1, 1)
            step(0, 0)
            with sp.Fori(0, 2) as i:
                step(2 * i + 1, 1)
                step(2 * i + 2, 0)
            step(5, 1)
            step(6, 0)
            step(7, 1, last=True)

            sp.wait_ge(s_glo, NP)
            sp.wait_ge(s_kout, 32 * NP)
            sp.wait_ge(s_vout[0], 16 * NP)
            sp.wait_ge(s_vout[1], 16 * NP)
            sp.dma_start(x2[0:SMP, NT, :], x_s).then_inc(s_x2d[NT], 16)
            for t in range(NT):
                sp.dma_start(x2[:, t, :], x_p[:, t, :]).then_inc(s_x2d[t], 16)
            sp.dma_start(g_lat[:, :], a["g_kv_a"].rearrange("(a n) -> a n", a=1).to_broadcast([P, KV])).then_inc(s_rows_g, 16)
            sp.dma_start(g_qar[:, :], a["g_qa"].to_broadcast([P, KV])).then_inc(s_rows_g, 16)
            load_late(G_KPE)
            for i, t in enumerate(ORDER):
                n = P if t < NT else SMP
                sp.wait_ge(s_x2sum, TT + i + 1)
                sp.dma_start(scratch[t * P:t * P + n, :], x2[0:n, t, :]).then_inc(s_x2out, 16)

            sp.wait_ge(s_ct, 2 * TT)
            sp.wait_ge(s_x2out, 16 * TT)
            sp.dma_start(lat[:, TT, :], a["cache_mla_latent"][0]).then_inc(s_latc, 16)
            for h in range(2):
                sp.dma_start(kpe[:, TT, h * ROPE:(h + 1) * ROPE], a["cache_mla_kpe"][0]).then_inc(s_latc, 16)
            load_late(G_QA)
            for i, t in enumerate(ORDER):
                n = P if t < NT else SMP
                sp.wait_ge(s_latn, i + 1)
                sp.wait_ge(s_kper, i + 1)
                lo_, ko_ = (lat_p, kpe_p) if t < NT else (lat_s, kpe_s)
                r0 = t * P if t < NT else 0
                sp.dma_start(lo_[0, r0:r0 + n, :], lat[0:n, t, :]).then_inc(s_latout, 16)
                sp.dma_start(ko_[0, r0:r0 + n, :], kpe[0:n, t, 0:ROPE]).then_inc(s_latout, 16)
            for g in range(G_GATE, G_OB + 2):
                load_late(g)
            sp.wait_ge(s_proj2, CD * MP)
            sp.dma_start(g_fin[:, :], a["g_final"].rearrange("(a n) -> a n", a=1).to_broadcast([P, D])).then_inc(s_gfin, 16)
            sp.wait_ge(s_score2, UA * MP)
            sp.wait_ge(s_latout, 32 * TT)
            for t in range(TT):
                n = P if t < NT else SMP
                sp.dma_start(x2e[0:n, t, :], scratch[t * P:t * P + n, :]).then_inc(s_x2in[t], 16)
            for t in range(TT):
                n = P if t < NT else SMP
                sp.wait_ge(s_yn, t + 1)
                dst = y_p[0, t * P:t * P + n, :] if t < NT else y_s[0]
                sp.dma_start(dst, x2e[0:n, t, :]).then_inc(s_yout, 16)
            sp.wait_ge(s_yout, 16 * TT)

        @block.tensor
        def _(pe):
            def weights(g):
                pe.wait_ge(s_hi, PIECES * (g + 1))
                pe.wait_ge(s_lo, PIECES * (g + 1))

            def piece(g, kn=KD):
                def ready(k):
                    if k * PIECES % kn == 0:
                        pe.wait_ge(s_hi, PIECES * g + k * PIECES // kn + 1)
                        pe.wait_ge(s_lo, PIECES * g + k * PIECES // kn + 1)
                        if isinstance(g, int) and g == 0:
                            pe.wait_ge(s_lo_dve, k * PIECES // kn + 1)
                return ready

            def proj_a(q, par, c):
                ready = piece(q) if c == 0 else None
                if c == 0 and isinstance(q, int) and q == 0:
                    def ready(k):
                        if k == KD - 2:
                            turn_x(2)
                        piece(0)(k)
                if isinstance(q, int) and q == 0:
                    pe.wait_ge(s_xt_hi, 2 * (c + 1))
                    pe.wait_ge(s_xt_lo, 2 * (c + 1))
                if begun(CA * q + c - 1):
                    pe.wait_ge(s_act_c, CA * q + c - 1)
                if begun(CA * q + c - 1):
                    pe.wait_ge(s_dve_c, CA * q + c - 1)
                b = PRJ[(par + c) % 2]
                mm = three(pe, b[:, 0:3 * P], [
                    ([acol(ht[0], k, c), acol(ht[1], k, c)],
                     [whi[par][:, k * 512:k * 512 + 3 * P], wlo[par][:, k * 512:k * 512 + 3 * P]]) for k in range(KD)], ready)
                mm.then_inc(s_proj, 1)

            def gate_a(q, par, j):
                c = TT + j
                pe.wait_ge(s_act_c, CA * q + c - 1)
                if begun(CA * q + c - 1):
                    pe.wait_ge(s_dve_c, CA * q + c - 1)
                b = PRJ[(par + c) % 2]
                mm = three(pe, b[:, 0:HALF], [
                    ([whi[par][:, k * 512 + 384:k * 512 + 512], wlo[par][:, k * 512 + 384:k * 512 + 512]],
                     [ht[m][:, k * TOK + j * HALF:k * TOK + (j + 1) * HALF] for m in range(2)]) for k in range(KD)])
                mm.then_inc(s_proj, 1)

            def xpose_a(q, par, t):
                pe.wait_ge(s_normed, TT * q + t + 1)
                if begun(XA * q + t):
                    pe.wait_ge(s_xev, XA * q + t)
                for m in range(2):
                    mm = pe.transpose(XB[:, m * P:(m + 1) * P], qkn[:, t, m, :], ident[:, :])
                mm.then_inc(s_xpose, 1)

            def xpose_cache(q, par):
                pe.wait_ge(s_kcd[par], 8 * (q - par) + 16)
                pe.wait_ge(s_xev, XA * q + TT)
                pe.transpose(XB[:, 0:P], kc[:, par, :], ident[:, :]).then_inc(s_xpose, 1)

            def score_a(p, par, u):
                ub = (par + u) % 2
                if begun(UA * p + u - 1):
                    pe.wait_ge(s_stay, UA * p + u - 1)
                if u == 0:
                    pe.wait_ge(s_xev, XA * (p + 1))
                b = SCR[ub]
                if u == 0:
                    pe.matmul(b[0:2 * SMP, PAST:SKEY], ident_b[:, 0:2 * SMP], causal_s[:, :],
                              start=True, stop=False, skip_group_check=True)
                    for h in range(2):
                        r = slice(h * HD, (h + 1) * HD)
                        o = slice(h * SMP, (h + 1) * SMP)
                        qs = qkt[r, par, 0, SEQ:TOK]
                        pe.matmul(b[o, PAST:SKEY], qs, qkt[r, par, 1, SEQ:TOK], start=False, stop=True,
                                  skip_group_check=True)
                        mm = pe.matmul(b[o, 0:PAST], qs, kct[r, par, :], start=False, stop=True,
                                       skip_group_check=True)
                    mm.then_inc(s_score, 1)
                    return
                h, i = UNIT_A[u]
                r = slice(h * HD, (h + 1) * HD)
                pe.matmul(b[:, 0:(i + 1) * P], qkt[r, par, 0, i * P:(i + 1) * P], qkt[r, par, 1, 0:(i + 1) * P],
                          start=True, stop=True)
                pe.matmul(b[:, i * P:(i + 1) * P], ident_b[:, :], causal[:, :], start=False, stop=True,
                          skip_group_check=True).then_inc(s_score, 1)

            def turn_a(p, par, u):
                ub = (par + u) % 2
                pe.wait_ge(s_wgt, UA * p + u + 1)
                if begun(UA * p + u - 1):
                    pe.wait_ge(s_wtev, UA * p + u - 1)
                n = 2 if u == 0 else UNIT_A[u][1] + 1
                for j in range(n):
                    mm = pe.transpose(TRB[ub][:, j * P:(j + 1) * P], wgt[:, ub, j * P:(j + 1) * P], ident[:, :])
                mm.then_inc(s_tr, 1)

            def out_a(p, par, o):
                if begun(OA * p + o):
                    pe.wait_ge(s_odone, OA * p + o)
                pe.wait_ge(s_wtev, UA * p + 2 * o + 1)
                if o == 0:
                    pe.wait_ge(s_vcd[par], 8 * (p - par) + 16)
                    pe.wait_ge(s_act_c, CA * p + TT)
                    for h in range(2):
                        r = slice(h * HD, (h + 1) * HD)
                        c = slice(h * SMP, (h + 1) * SMP)
                        pe.matmul(OUT[r, 0:SMP], vc[:, par, r], wts[:, 0, c], start=True, stop=False)
                        mm = pe.matmul(OUT[r, 0:SMP], vtok[0:SMP, par, NT, r], wts[0:SMP, 1, c], start=False, stop=True)
                    mm.then_inc(s_av, 1)
                    return
                i = NT - o
                for j in range(i + 1):
                    for h in range(2):
                        r = slice(h * HD, (h + 1) * HD)
                        mm = pe.matmul(OUT[r, i * P:(i + 1) * P], vtok[:, par, j, r], wt[:, i % 2, j, h, :],
                                       start=(j == 0), stop=(j == i))
                mm.then_inc(s_av, 1)

            def step_a(p, par, att=True, ahead=True):
                for what, n in STEP_A:
                    if what in AHEAD:
                        if not ahead:
                            continue
                        q, qpar = p + 1, 1 - par
                        if what == "C":
                            proj_a(q, qpar, n)
                            if not att and n + 3 < TT:
                                turn_x(n + 3)
                        elif what == "G":
                            gate_a(q, qpar, n)
                        elif what == "X":
                            xpose_a(q, qpar, n)
                        elif what == "Z":
                            xpose_cache(q, qpar)
                    elif att:
                        if what == "S":
                            score_a(p, par, n)
                        elif what == "T":
                            turn_a(p, par, n)
                        elif what == "O":
                            out_a(p, par, n)

            def turn_x(t):
                n = P if t < NT else SMP
                pe.wait_ge(s_xn, t + 1)
                for j in range(2):
                    if begun(2 * (t - 2) + j + 1):
                        pe.wait_ge(s_xt_lo, 2 * (t - 2) + j + 1)
                    for k in range(KD // 2):
                        K = j * KD // 2 + k
                        mm = pe.transpose(XTB[t % 2][j][:, k * P:k * P + n], x_in[0:n, t, K * P:(K + 1) * P],
                                          ident[0:n, 0:n])
                    mm.then_inc(s_xt, 1)

            pe.wait_ge(s_masks, 2)
            pe.wait_ge(s_rows_d, 16 * 3)
            pe.transpose(XB[:, 0:3 * KD], g_rows[:, :], ident[0:3 * KD, 0:3 * KD]).then_inc(s_gcol_t, 1)
            turn_x(0)
            turn_x(1)
            pe.wait_ge(s_pad, 4)

            pe.wait_ge(s_gcol, 1)
            step_a(-1, 1, att=False)
            pe.wait_ge(s_masks, 7)
            step_a(0, 0)
            with pe.Fori(0, 3) as i:
                step_a(2 * i + 1, 1)
                step_a(2 * i + 2, 0)
            step_a(7, 1, ahead=False)

            def residual(i, nh):
                n = TT * nh + i

                def last_pair(k):
                    if k == KD - 2:
                        pe.wait_ge(s_ghi, NP)
                        pe.wait_ge(s_glo, NP)

                if begun(n - 3):
                    pe.wait_ge(s_x2sum, n - 3)
                three(pe, bank[n % 4][:, :], [
                    ([acol(gt[0], k, ORDER[i]), acol(gt[1], k, ORDER[i])],
                     [wcol(G_OA + nh, m, k, 0, 512, 512) for m in range(2)]) for k in range(KD)],
                    last_pair if n == 0 else None).then_inc(s_yprod, 1)

            def turn_x2(i):
                t = ORDER[i]
                n = P if t < NT else SMP
                pe.wait_ge(s_xn, TT + i + 1)
                for j in range(2):
                    if begun(2 * (i - 2) + j + 1):
                        pe.wait_ge(s_ct_lo, 2 * (i - 2) + j + 1)
                    for k in range(KD // 2):
                        K = j * KD // 2 + k
                        mm = pe.transpose(bank[4 + 2 * (i % 2) + j][:, k * P:k * P + n],
                                          xn[0:n, t, K * P:(K + 1) * P], ident[0:n, 0:n])
                    mm.then_inc(s_ct, 1)

            weights(G_OA)
            weights(G_OA + 1)
            pe.wait_ge(s_ghi, NP - 1)
            pe.wait_ge(s_glo, NP - 1)
            pe.wait_ge(s_zeros_b, 2)
            pe.wait_ge(s_stay, UA * NP)
            for i in range(TT):
                residual(i, 0)
            for i in range(TT):
                residual(i, 1)
                if i:
                    turn_x2(i - 1)

            def lat_a(i):
                ready = 2 * max(2, i + 1)
                pe.wait_ge(s_ct_hi, ready)
                pe.wait_ge(s_ct_lo, ready)
                if i < 3:
                    pe.wait_ge(s_x2sum, 2 * TT - 2 + i)
                else:
                    pe.wait_ge(s_latn, i - 2)
                three(pe, LAB[i % 3][:, 0:LA], [
                    ([acol(gt[m], k, ORDER[i]) for m in range(2)], [wcol(G_LAT, m, k, 0, LA, LA) for m in range(2)])
                    for k in range(KD)], piece(G_LAT) if i == 0 else None).then_inc(s_lata, 1)

            def lat_b(i):
                if begun(i - 1):
                    pe.wait_ge(s_latn, i - 1)
                if i == 1:
                    pe.wait_ge(s_ct_lo, 2 * (TT - 1))
                three(pe, bank[3 + 3 * (i % 2)][:, 0:LB], [
                    ([acol(gt[m], k, ORDER[i]) for m in range(2)], [wcol(G_KPE, m, k, 0, LB, LB) for m in range(2)])
                    for k in range(KD)], piece(G_KPE) if i == 0 else None).then_inc(s_latm, 1)

            def lat_turn(i):
                t = ORDER[i] if i < TT else TT
                if begun(i):
                    pe.wait_ge(s_lat_lo, i)
                if begun(i):
                    pe.wait_ge(s_kpet_e, i)
                if i < TT:
                    pe.wait_ge(s_latn, i + 1)
                    pe.wait_ge(s_kper, i + 1)
                else:
                    pe.wait_ge(s_latc, 48)
                for k in range(KL):
                    pe.transpose(bank[4][:, k * P:(k + 1) * P], lat[:, t, k * P:(k + 1) * P], ident[:, :])
                pe.transpose(bank[5][:, 0:P], kpe[:, t, :], ident[:, :]).then_inc(s_latx, 1)

            lat_a(0)
            lat_a(1)
            turn_x2(TT - 1)
            lat_a(2)
            lat_b(0)
            lat_b(1)
            lat_a(3)
            pe.wait_ge(s_ct_lo, 2 * TT)
            lat_turn(0)
            lat_a(4)
            lat_turn(1)
            for i in range(2, TT):
                lat_b(i)
                if i > 2:
                    lat_turn(i - 1)

            def qa_turn(t):
                pe.wait_ge(s_lat_lo, LT + t)
                pe.wait_ge(s_latn, TT + t + 1)
                for k in range(KL):
                    mm = pe.transpose(bank[4][:, k * P:(k + 1) * P], qan[:, k * P:(k + 1) * P], ident[:, :])
                mm.then_inc(s_latx, 1)

            for t in range(TT):
                n = TT + t
                pe.wait_ge(s_latn, n - 1)
                three(pe, QAB[t % 2][:, :], [
                    ([acol(ht[m], k, t) for m in range(2)], [wcol(G_QA, m, k, 0, 512, 512) for m in range(2)])
                    for k in range(KD)], piece(G_QA) if t == 0 else None).then_inc(s_latm, 1)
                if t == 0:
                    lat_turn(TT - 1)
                if t == 1:
                    lat_turn(TT)
                if t:
                    qa_turn(t - 1)
            for m8 in range(NH):
                g, mm4 = G_GATE + m8 // 4, m8 % 4
                if mm4 == 0:
                    weights(g)
                for j in range(2):
                    n = 2 * m8 + j
                    pe.wait_ge(s_dve_c, CA * NP + n - 1)
                    three(pe, bank[2 + n % 2][:, 0:HALF], [
                        ([wcol(g, m, k, mm4 * P, P, 512) for m in range(2)],
                         [ht[m][:, k * TOK + j * HALF:k * TOK + (j + 1) * HALF] for m in range(2)])
                        for k in range(KD)]).then_inc(s_proj, 1)
                    if n == 1:
                        qa_turn(TT - 1)
            pe.wait_ge(s_lat_hi, LT + TT)
            pe.wait_ge(s_lat_lo, LT + TT)
            pe.wait_ge(s_kpet_e, LT)
            pe.wait_ge(s_zeros_d, 2)

            def chunk_free(q, c):
                left = CD * q + c - (3 if q == 0 else 1)
                if begun(left):
                    pe.wait_ge(s_act2, left)
                if begun(left):
                    pe.wait_ge(s_dve2, left)

            def query_d(q, par, t):
                slot = (G_D + par) % 2
                c = CHUNK_D["Q", t]
                chunk_free(q, c)
                three(pe, chunk_bank(q, par, c)[:, 0:WQ], [
                    ([acol(qat[m], k, t) for m in range(2)],
                     [(whi, wlo)[m][slot][:, k * WD:k * WD + WQ] for m in range(2)]) for k in range(KL)],
                    piece(q + G_D, KL) if c == 0 else None).then_inc(s_proj2, 1)

            def keyval_d(q, par, t):
                slot = (G_D + par) % 2
                c = CHUNK_D["K", t]
                chunk_free(q, c)
                three(pe, chunk_bank(q, par, c)[:, 0:WK], [
                    ([latt[m][:, (k * LT + t) * P:(k * LT + t + 1) * P] for m in range(2)],
                     [(whi, wlo)[m][slot][:, k * WD + WQ:(k + 1) * WD] for m in range(2)]) for k in range(KL)]).then_inc(s_proj2, 1)

            def turn_qk(q, what, t):
                c = CHUNK_D["Q" if what == "X" else "K", t]
                if what == "X":
                    pe.wait_ge(s_nrm2, TT * q + t + 1)
                else:
                    pe.wait_ge(s_dve2, CD * q + c + 1)
                if begun(CD * q + c):
                    pe.wait_ge(s_xev2, CD * q + c)
                src, n = (qn2, 3) if what == "X" else (kn2, 2)
                for m in range(n):
                    mm = pe.transpose(XB[:, m * P:(m + 1) * P], src[:, t % 2, m * P:(m + 1) * P], ident[:, :])
                mm.then_inc(s_xp2, 1)

            def score_d(p, par, u):
                ub = (par + u) % 2
                if begun(UA * p + u - 1):
                    pe.wait_ge(s_expd, UA * p + u - 1)
                if u == 0:
                    pe.wait_ge(s_xev2, CD * (p + 1))
                b = SCR[ub]
                if u == 0:
                    for h in range(2):
                        r, o = slice(h * ROPE, (h + 1) * ROPE), slice(h * SMP, (h + 1) * SMP)
                        pe.matmul(b[o, 0:SKEY], q2t[:, par, h, SEQ:TOK], k2t[:, par, h, SEQ:KEYS],
                                  start=True, stop=False)
                        mm = pe.matmul(b[o, 0:SKEY], q2t[r, par, 2, SEQ:TOK], kpet[r, SEQ:KEYS],
                                       start=False, stop=True)
                    mm.then_inc(s_score2, 1)
                    return
                h, i = UNIT_D[u]
                r = slice(h * ROPE, (h + 1) * ROPE)
                pe.matmul(b[:, 0:(i + 1) * P], q2t[:, par, h, i * P:(i + 1) * P], k2t[:, par, h, 0:(i + 1) * P],
                          start=True, stop=False)
                pe.matmul(b[:, 0:(i + 1) * P], q2t[r, par, 2, i * P:(i + 1) * P], kpet[r, 0:(i + 1) * P],
                          start=False, stop=True)
                pe.matmul(b[:, i * P:(i + 1) * P], ident_b[:, :], chunk_mask[:, :], start=False, stop=True,
                          skip_group_check=True).then_inc(s_score2, 1)

            def turn_d(p, par, u):
                ub = (par + u) % 2
                pe.wait_ge(s_scaled, UA * p + u + 1)
                if begun(UA * p + u - 1):
                    pe.wait_ge(s_wtev2, UA * p + u - 1)
                offs = [0, SMP] if u == 0 else [j * P for j in range(UNIT_D[u][1] + 1)]
                for j, o in enumerate(offs):
                    mm = pe.transpose(TRB[ub][:, j * P:(j + 1) * P], prob[:, ub, o:o + P], ident[:, :])
                mm.then_inc(s_tr2, 1)

            def out_d(p, par, o):
                if begun(3 * p + o):
                    pe.wait_ge(s_od2, 3 * p + o)
                pe.wait_ge(s_wtev2, UA * p + (1 if o == 0 else 1 + NT * o))
                if o == 0:
                    pe.wait_ge(s_act2, CD * (p + 1))
                    for h in range(2):
                        c = slice(h * SMP, (h + 1) * SMP)
                        pe.matmul(OUT[:, c], v2[0:SMP, par, h, NT, :], wts2[0:SMP, 0, c], start=True, stop=False)
                        mm = pe.matmul(OUT[:, c], v2[:, par, h, TT, :], wts2[:, 1, c], start=False, stop=True)
                    mm.then_inc(s_av2, 1)
                    return
                for j in range(NT):
                    mm = pe.matmul(OUT[:, j * P:SEQ], v2[:, par, o - 1, j, :], wt2[:, j, j * P:SEQ],
                                   start=(j == 0), stop=(j == NT - 1))
                mm.then_inc(s_av2, 1)

            def last_product(t, nh, k):
                if t < 2:
                    pe.wait_ge(s_go_hi, k + 1)
                    pe.wait_ge(s_go_lo, k + 1)
                    piece(G_OB + nh)(k)
                if t == 0 and k == 0:
                    pe.wait_ge(s_act2, CD * MP)
                    pe.wait_ge(s_dve2, CD * MP)
                b = bank[(2 * t + nh) % 4][:, :]
                st = [acol(ghi, k, t), acol(glo, k, t)]
                mv = [wcol(G_OB + nh, m, k, 0, 512, 512) for m in range(2)]
                pe.matmul(b, st[0], mv[0], start=(k == 0), stop=False)
                pe.matmul(b, st[0], mv[1], start=False, stop=False)
                return pe.matmul(b, st[1], mv[0], start=False, stop=(k == KD - 1))

            def step_d(p, par, att=True, ahead=True):
                for what, n in order_d(p):
                    if what in AHEAD:
                        if not ahead:
                            continue
                        if what == "Q":
                            query_d(p + 1, 1 - par, n)
                        elif what == "K":
                            keyval_d(p + 1, 1 - par, n)
                        elif what in "XY":
                            turn_qk(p + 1, what, n)
                    elif att:
                        if what == "P":
                            turn_qk(p, "Y", n)
                        elif what in "EF":
                            last_product(0, "EF".index(what), n)
                        elif what == "S":
                            score_d(p, par, n)
                        elif what == "T":
                            turn_d(p, par, n)
                        elif what == "O":
                            out_d(p, par, n)

            step_d(-1, 1, att=False)
            pe.wait_ge(s_zeros_d, 3)
            pe.wait_ge(s_dve_c, CA * NP + 2 * NH)
            for p in range(MP):
                step_d(p, p % 2, ahead=p + 1 < MP)

            weights(G_OB)
            weights(G_OB + 1)
            pe.wait_ge(s_zeros_e, 2)

            pe.wait_ge(s_expd, UA * MP)
            for k in range(KD - 1):
                last_product(1, 0, k)
            for t in range(TT):
                for nh in range(2):
                    n = 2 * t + nh
                    if begun(n - 3):
                        pe.wait_ge(s_ysum, n - 3)
                    for k in range(KD - 1 if n < 3 else 0, KD):
                        mm = last_product(t, nh, k)
                    mm.then_inc(s_yprod, 1)

        def last_reader(g):
            if not isinstance(g, int) or g < G_LAT:
                return s_proj, CA * (g - 1)
            if g <= G_KPE:
                return s_yprod, TT * (1 + g - G_LAT)
            if g == G_QA:
                return s_lata, TT
            if g <= G_GATE:
                return s_latm, TT
            if g == G_GATE + 1:
                return s_latm, 2 * TT
            return s_proj, CA * NP + NH * (g - G_D + 1)

        def last_reader_d(h):
            if isinstance(h, int) and h < 0:
                return last_reader(G_D + 1)
            return s_proj2, CD * (h + 1)

        def gt_pair(t, p):
            return t[:, bass.ds(p * TOK, TOK)]

        def turned(t, tile, n, k=KL, width=LT * P):
            return t[:, 0:k * width].rearrange("p (k c) -> p k c", k=k)[:, :, tile * P:tile * P + n]

        @block.scalar
        def _(act):
            def split_piece(g, j, slot, cols):
                n = cols // PIECES
                act.wait_ge(s_raw[j], raw_count(g))
                c = slice(j * n, (j + 1) * n)
                nc.scalar.activation(whi[slot][:, c], raw[:, c], ACT.Copy).then_inc(s_hi, 1)

            def split_group(g):
                if g > 1:
                    sem, n = last_reader(g)
                    act.wait_ge(sem, n)
                for j in range(PIECES):
                    split_piece(g, j, g % 2, COLS[g])

            def square_x(t):
                n = P if t < NT else SMP
                act.wait_ge(s_x_in[t], 16)
                if begun(t):
                    act.wait_ge(s_row_ss, t)
                nc.scalar.activation(dump_x[0:n, :], x_in[0:n, t, :], ACT.Square,
                                     accum_out=row_ss[0:n, 0, t:t + 1]).then_inc(s_row_ss, 1)

            def x_hi(t):
                n = P if t < NT else SMP
                for j in range(2):
                    act.wait_ge(s_xt, 2 * t + j + 1)
                    for k in range(KD // 2):
                        K = j * KD // 2 + k
                        last = nc.scalar.activation(ht[0][:, K * TOK + t * P:K * TOK + t * P + n],
                                                    XTB[t % 2][j][:, k * P:k * P + n], ACT.Copy,
                                                    scale=g_col[:, 0, K:K + 1])
                    last.then_inc(s_xt_hi, 1)

            square_x(0)
            act.wait_ge(s_gcol_t, 1)
            nc.scalar.activation(g_col[:, :, :].rearrange("p m k -> p (m k)"), XB[:, 0:3 * KD],
                                 ACT.Copy).then_inc(s_gcol, 1)
            act.wait_ge(s_gcol, 1)
            square_x(1)
            x_hi(0)
            split_piece(0, 0, 0, COLS[0])
            x_hi(1)
            split_piece(0, 1, 0, COLS[0])
            split_piece(0, 2, 0, COLS[0])
            square_x(2)
            split_piece(0, 3, 0, COLS[0])
            square_x(3)
            x_hi(2)

            def chunk_a(q, par, c):
                b = PRJ[(par + c) % 2]
                act.wait_ge(s_proj, CA * q + c + 1)
                if begun(TT * q + c):
                    act.wait_ge(s_msq_d, TT * q + c)
                if c == 0:
                    if begun(CA * q):
                        act.wait_ge(s_dve_c, CA * q)
                nc.scalar.activation(sq[:, :], b[:, 0:2 * P], ACT.Square).then_inc(s_sqd, 1)
                if c == 0:
                    if begun(OA * (q - 1)):
                        act.wait_ge(s_av, OA * (q - 1))
                    if begun(16 * (q - par)):
                        act.wait_ge(s_vout[par], 16 * (q - par))
                nc.scalar.activation(vtok[:, par, c, :], b[:, 2 * P:3 * P], ACT.Copy).then_inc(s_act_c, 1)

            def gate_a(q, par, j):
                c = TT + j
                act.wait_ge(s_proj, CA * q + c + 1)
                act.wait_ge(s_dve_c, CA * q + c)
                act.wait_ge(s_normed, TT * (q + 1))
                nc.scalar.activation(sigm[:, :], PRJ[(par + c) % 2][:, 0:HALF], ACT.Sigmoid).then_inc(s_act_c, 1)

            def xev_a(q, par, t):
                n = P if t < NT else SMP
                act.wait_ge(s_xpose, XA * q + t + 1)
                nc.scalar.activation(qkt[:, par, :, t * P:t * P + n],
                                     XB[:, 0:2 * P].rearrange("p (m c) -> p m c", m=2)[:, :, 0:n],
                                     ACT.Copy).then_inc(s_xev, 1)

            def zev_a(q, par):
                act.wait_ge(s_xpose, XA * (q + 1))
                nc.scalar.activation(kct[:, par, :], XB[:, 0:P], ACT.Copy).then_inc(s_xev, 1)

            def stay_a(p, par, u):
                ub = (par + u) % 2
                act.wait_ge(s_score, UA * p + u + 1)
                if begun(UA * p + u - 1):
                    act.wait_ge(s_left, UA * p + u - 1)
                r, n = (2 * SMP, SKEY) if u == 0 else (P, (UNIT_A[u][1] + 1) * P)
                nc.scalar.activation(stay[0:r, ub, SEQ - n:SEQ], SCR[ub][0:r, 0:n], ACT.Sigmoid,
                                     scale=-1.0).then_inc(s_stay, 1)

            def wtev_a(p, par, u):
                ub = (par + u) % 2
                act.wait_ge(s_tr, UA * p + u + 1)
                if u == 0:
                    if begun(OA * (p - 1) + 1):
                        act.wait_ge(s_av, OA * (p - 1) + 1)
                    nc.scalar.activation(wts[:, :, :],
                                         TRB[ub][:, 0:2 * P].rearrange("p (j c) -> p j c", j=2)[:, :, 0:2 * SMP],
                                         ACT.Copy).then_inc(s_wtev, 1)
                    return
                h, i = UNIT_A[u]
                if h == 0:
                    used = OA * p + NT - i - 1 - (1 if i >= 2 else 0)
                    if begun(used):
                        act.wait_ge(s_av, used)
                nc.scalar.activation(wt[:, i % 2, 0:i + 1, h, :],
                                     TRB[ub][:, 0:(i + 1) * P].rearrange("p (j c) -> p j c", j=i + 1),
                                     ACT.Copy).then_inc(s_wtev, 1)

            def out_hi(p):
                act.wait_ge(s_odone, OA * (p + 1))
                nc.scalar.activation(gt_pair(gt[0], p), gated[:, :], ACT.Copy).then_inc(s_ghi, 1)

            def step_a(p, par, att=True, ahead=True):
                for what, n in STEP_A:
                    if what in AHEAD:
                        if not ahead:
                            continue
                        q, qpar = p + 1, 1 - par
                        if what == "C":
                            if not att and n + 3 < TT:
                                x_hi(n + 3)
                            chunk_a(q, qpar, n)
                            if not att and n + 4 < TT:
                                square_x(n + 4)
                        elif what == "G":
                            gate_a(q, qpar, n)
                        elif what == "X":
                            xev_a(q, qpar, n)
                        elif what == "Z":
                            zev_a(q, qpar)
                    elif what == "W":
                        if n == 0 and not (isinstance(p, int) and p < 0):
                            sem, count = last_reader(p + 2)
                            act.wait_ge(sem, count)
                        split_piece(p + 2, n, par, KD * 512)
                    elif att:
                        if what == "S":
                            stay_a(p, par, n)
                        elif what == "T":
                            wtev_a(p, par, n)
                        elif what == "O" and n == OA - 1:
                            out_hi(p)

            step_a(-1, 1, att=False)
            step_a(0, 0)
            with act.Fori(0, 3) as i:
                step_a(2 * i + 1, 1)
                step_a(2 * i + 2, 0)
            step_a(7, 1, ahead=False)

            def square_x2(i):
                t = ORDER[i]
                n = P if t < NT else SMP
                act.wait_ge(s_x2sum, TT + i + 1)
                act.wait_ge(s_row_ss, TT + i)
                nc.scalar.activation(dump[0:n, :], x2[0:n, t, :], ACT.Square,
                                     accum_out=row_ss[0:n, 1, i:i + 1]).then_inc(s_row_ss, 1)

            def norm_x2(i):
                t = ORDER[i]
                n = P if t < NT else SMP
                act.wait_ge(s_row_r, TT + i + 1)
                nc.scalar.activation(xn[0:n, t, :], x2[0:n, t, :], ACT.Copy,
                                     scale=row_r[0:n, 1, i:i + 1]).then_inc(s_xn, 1)

            def x2_hi(i):
                t = ORDER[i]
                n = P if t < NT else SMP
                for j in range(2):
                    act.wait_ge(s_ct, 2 * i + j + 1)
                    for k in range(KD // 2):
                        K = j * KD // 2 + k
                        src = bank[4 + 2 * (i % 2) + j][:, k * P:k * P + n]
                        for m, dst in ((1, gt[0]), (2, ht[0])):
                            last = nc.scalar.activation(dst[:, K * TOK + t * P:K * TOK + t * P + n], src, ACT.Copy,
                                                        scale=g_col[:, m, K:K + 1])
                    last.then_inc(s_ct_hi, 1)

            split_group(G_LAT)
            for i in range(TT):
                square_x2(i)
                if i:
                    x2_hi(i - 1)
                norm_x2(i)
            split_group(G_KPE)
            x2_hi(TT - 1)

            def split_late(g, j):
                if j == 0:
                    sem, n = last_reader(g)
                    act.wait_ge(sem, n)
                split_piece(g, j, g % 2, COLS[g])

            def lat_hi(i):
                t = ORDER[i] if i < TT else TT
                act.wait_ge(s_latx, i + 1)
                nc.scalar.activation(turned(latt[0], t, P), bank[4][:, :].rearrange("p (k c) -> p k c", k=KL),
                                     ACT.Copy).then_inc(s_lat_hi, 1)
                c0, n = [(t * P, P), (SEQ, SMP), (TOK, P)][max(0, t - NT + 1)]
                nc.scalar.activation(kpet[:, c0:c0 + n], bank[5][:, 0:n], ACT.Copy).then_inc(s_kpet_e, 1)

            def qa_hi(t):
                n = P if t < NT else SMP
                act.wait_ge(s_latx, LT + t + 1)
                nc.scalar.activation(turned(qat[0], t, n, width=TOK),
                                     bank[4][:, :].rearrange("p (k c) -> p k c", k=KL)[:, :, 0:n],
                                     ACT.Copy).then_inc(s_lat_hi, 1)

            act.wait_ge(s_x2out, 16 * TT)
            for i in range(TT):
                if i > 1:
                    split_late(G_QA, i - 2)
                act.wait_ge(s_lata, i + 1)
                if begun(i):
                    act.wait_ge(s_lat_ss, i)
                nc.scalar.activation(sqc[:, 0:LA], LAB[i % 3][:, 0:LA], ACT.Square, accum_out=lat_ss[:, i, 0:1])
                act.wait_ge(s_latm, i + 1)
                b = bank[3 + 3 * (i % 2)]
                nc.scalar.activation(sqc[:, LA:KV], b[:, 0:KV - LA], ACT.Square, accum_out=lat_ss[:, i, 2:3])
                nc.scalar.activation(sq_pe[:, :], b[:, KV - LA:LB], ACT.Square,
                                     accum_out=lat_ss[:, i, 1:2]).then_inc(s_lat_ss, 1)
                if i:
                    lat_hi(i - 1)
            split_late(G_QA, 3)
            lat_hi(TT - 1)
            for t in range(TT):
                act.wait_ge(s_latm, TT + t + 1)
                act.wait_ge(s_lat_ss, TT + t)
                nc.scalar.activation(sqc[:, :], QAB[t % 2][:, :], ACT.Square,
                                     accum_out=lat_ss[:, TT + t, 0:1]).then_inc(s_lat_ss, 1)
                if t == 1:
                    lat_hi(TT)
                if t:
                    qa_hi(t - 1)
                if t < PIECES:
                    split_late(G_GATE, t)
            for n in range(2 * NH):
                act.wait_ge(s_proj, CA * NP + n + 1)
                act.wait_ge(s_dve_c, CA * NP + n)
                act.wait_ge(s_lat_ss, 2 * TT)
                nc.scalar.activation(sigc[:, :], bank[2 + n % 2][:, 0:HALF], ACT.Sigmoid).then_inc(s_act_c, 1)
                if n == 1:
                    qa_hi(TT - 1)
                if 1 < n < 2 + PIECES:
                    split_late(G_GATE + 1, n - 2)
                if NH <= n < NH + PIECES:
                    split_late(G_D, n - NH)

            def chunk_d(q, par, what, t):
                c = CHUNK_D[what, t]
                b = chunk_bank(q, par, c)
                act.wait_ge(s_proj2, CD * q + c + 1)
                if begun(CD * q + c):
                    act.wait_ge(s_sum2, CD * q + c)
                if what == "Q":
                    nc.scalar.activation(sqd[:, :], b[:, 0:WQ], ACT.Square).then_inc(s_act2, 1)
                    return
                kv = b[:, 0:WK].rearrange("p (h s d) -> p h s d", h=2, s=2)
                nc.scalar.activation(sqd[:, 0:2 * NOPE].rearrange("p (h d) -> p h d", h=2), kv[:, :, 0, :],
                                     ACT.Square).then_inc(s_sqk, 1)
                if t == 0:
                    if begun(3 * (q - 1)):
                        act.wait_ge(s_av2, 3 * (q - 1))
                nc.scalar.activation(v2[:, par, :, t, :], kv[:, :, 1, :], ACT.Copy).then_inc(s_act2, 1)

            def xev_d(q, par, what, t):
                c = CHUNK_D["Q" if what == "X" else "K", t]
                act.wait_ge(s_xp2, CD * q + c + 1)
                if what == "X":
                    n = P if t < NT else SMP
                    nc.scalar.activation(q2t[:, par, :, t * P:t * P + n],
                                         XB[:, 0:3 * P].rearrange("p (m c) -> p m c", m=3)[:, :, 0:n],
                                         ACT.Copy).then_inc(s_xev2, 1)
                else:
                    c0, n = [(t * P, P), (SEQ, SMP), (TOK, P)][max(0, t - NT + 1)]
                    nc.scalar.activation(k2t[:, par, :, c0:c0 + n],
                                         XB[:, 0:2 * P].rearrange("p (m c) -> p m c", m=2)[:, :, 0:n],
                                         ACT.Copy).then_inc(s_xev2, 1)

            def exp_d(p, par, u):
                ub = (par + u) % 2
                act.wait_ge(s_negmax, UA * p + u + 1)
                if begun(UA * p + u - 1):
                    act.wait_ge(s_tr2, UA * p + u - 1)
                r, n = (2 * SMP, SKEY) if u == 0 else (P, (UNIT_D[u][1] + 1) * P)
                nc.scalar.activation(prob[0:r, ub, 0:n], SCR[ub][0:r, 0:n], ACT.Exp, bias=neg_max[0:r, ub:ub + 1],
                                     accum_out=p_sum[0:r, ub:ub + 1]).then_inc(s_expd, 1)

            def wtev_d(p, par, u):
                ub = (par + u) % 2
                act.wait_ge(s_tr2, UA * p + u + 1)
                if u == 0:
                    if begun(3 * p - 2):
                        act.wait_ge(s_av2, 3 * p - 2)
                    nc.scalar.activation(wts2[:, :, :],
                                         TRB[ub][:, 0:2 * P].rearrange("p (j c) -> p j c", j=2)[:, :, 0:2 * SMP],
                                         ACT.Copy).then_inc(s_wtev2, 1)
                    return
                h, i = UNIT_D[u]
                if i == NT - 1:
                    if begun(3 * p + 2 * h):
                        act.wait_ge(s_av2, 3 * p + 2 * h)
                nc.scalar.activation(wt2[:, 0:i + 1, i * P:(i + 1) * P],
                                     TRB[ub][:, 0:(i + 1) * P].rearrange("p (j c) -> p j c", j=i + 1),
                                     ACT.Copy).then_inc(s_wtev2, 1)

            def gated_hi(K):
                nc.scalar.activation(ghi[:, K * TOK:(K + 1) * TOK], sg[:, K, :], ACT.Copy).then_inc(s_go_hi, 1)

            def step_d(p, par, att=True, ahead=True):
                for what, n in order_d(p):
                    if what in AHEAD:
                        if not ahead:
                            continue
                        if what in "QK":
                            chunk_d(p + 1, 1 - par, what, n)
                        elif what in "XY":
                            xev_d(p + 1, 1 - par, what, n)
                    elif what == "W":
                        g = p + G_D + 2
                        if n == 0:
                            sem, count = last_reader_d(p)
                            act.wait_ge(sem, count)
                        split_piece(g, n, g % 2, COLS[g])
                    elif att:
                        if what == "P":
                            xev_d(p, par, "Y", n)
                        elif what == "S":
                            exp_d(p, par, n)
                        elif what == "H":
                            act.wait_ge(s_proj2, CD * MP)
                            act.wait_ge(s_od2, 3 * (MP - 1) + (2 if n == KD - 2 else 0))
                            gated_hi(n)
                        elif what == "T":
                            wtev_d(p, par, n)

            act.wait_ge(s_latout, 32 * TT)
            step_d(-1, 1, att=False)
            for p in range(MP):
                step_d(p, p % 2, ahead=p + 1 < MP)

            act.wait_ge(s_od2, 3 * MP)
            gated_hi(KD - 1)
            for t in range(TT):
                n = P if t < NT else SMP
                act.wait_ge(s_ysum, 2 * (t + 1))
                act.wait_ge(s_row_ss, 2 * TT + t)
                nc.scalar.activation(dump2[0:n, :], x2e[0:n, t, :], ACT.Square,
                                     accum_out=row_ss[0:n, 2, t:t + 1]).then_inc(s_row_ss, 1)

        @block.gpsimd
        def _(pool):
            def split_piece(g, j, slot, cols):
                n = cols // PIECES
                c = slice(j * n, (j + 1) * n)
                pool.wait_ge(s_hi, PIECES * g + j + 1)
                nc.gpsimd.tensor_tensor(wlo[slot][:, c], raw[:, c], whi[slot][:, c].bitcast(F32),
                                        ALU.subtract).then_inc(s_lo, 1)

            def split_group(g):
                if g > 1:
                    sem, n = last_reader(g)
                    pool.wait_ge(sem, n)
                for j in range(PIECES):
                    split_piece(g, j, g % 2, COLS[g])

            def rms_rows(phase, t):
                n = SMP if t == (0 if phase == 1 else NT) else P
                k = TT * phase + t
                pool.wait_ge(s_row_ss, k + 1)
                nc.gpsimd.tensor_scalar(row_ms[0:n, phase, t:t + 1], row_ss[0:n, phase, t:t + 1], 1.0 / D, EPS,
                                        ALU.mult, ALU.add).then_inc(s_row_ms, 1)
                pool.wait_ge(s_row_ms, k + 1)
                nc.gpsimd.tensor_tensor(row_r[0:n, phase, t:t + 1], row_ms[0:n, phase, t:t + 1],
                                        neg_half[0:n, 0:1], ALU.pow).then_inc(s_row_r, 1)

            nc.gpsimd.memset(neg_half[:, :], -0.5).then_inc(s_masks, 1)
            nc.gpsimd.memset(ident[:, :], 0.0).then_inc(s_pad, 1)
            pool.wait_ge(s_pad, 1)
            nc.gpsimd.affine_select(out=ident[:, :], in_=ident[:, :], compare_op=ALU.not_equal, fill=1.0,
                                    base=0, pattern=[[-1, P]], channel_multiplier=1).then_inc(s_masks, 1)
            nc.gpsimd.memset(ht[0][:, KD * TOK:FLAT].bitcast(F32), 0.0).then_inc(s_pad, 1)
            nc.gpsimd.memset(ht[1][:, KD * TOK:FLAT].bitcast(F32), 0.0).then_inc(s_pad, 1)
            nc.gpsimd.memset(wgt[:, :, :], 0.0).then_inc(s_pad, 1)
            rms_rows(0, 0)
            rms_rows(0, 1)
            for j in range(PIECES):
                c = slice(j * 2 * 512, j * 2 * 512 + POOL_SHARE)
                pool.wait_ge(s_hi, j + 1)
                nc.gpsimd.tensor_tensor(wlo[0][:, c], raw[:, c], whi[0][:, c].bitcast(F32),
                                        ALU.subtract).then_inc(s_lo, 1)
                if j == 2:
                    rms_rows(0, 2)
            pool.wait_ge(s_masks, 2)
            nc.gpsimd.tensor_copy(ident_b[:, :], ident[:, :]).then_inc(s_masks, 1)
            nc.gpsimd.memset(causal[:, :], 0.0).then_inc(s_zeros_m, 1)
            nc.gpsimd.memset(causal_s[:, :], 0.0).then_inc(s_zeros_m, 1)
            nc.gpsimd.memset(chunk_mask[:, :], 0.0).then_inc(s_zeros_m, 1)
            pool.wait_ge(s_zeros_m, 3)
            nc.gpsimd.affine_select(out=causal[:, :], in_=causal[:, :], compare_op=ALU.is_gt, fill=BIG,
                                    base=0, pattern=[[-1, P]], channel_multiplier=1).then_inc(s_masks, 1)
            for h in range(2):
                r = slice(h * SMP, (h + 1) * SMP)
                pool.wait_ge(s_masks, 4 + h)
                nc.gpsimd.affine_select(out=causal_s[r, :], in_=causal_s[r, :], compare_op=ALU.is_gt, fill=BIG,
                                        base=0, pattern=[[-1, SMP]], channel_multiplier=1).then_inc(s_masks, 1)
            pool.wait_ge(s_masks, 6)
            nc.gpsimd.memset(chunk_mask[0:HD, HD:P], BIG).then_inc(s_masks, 1)
            rms_rows(0, 3)

            def rms_a(q, par, c):
                sl = (par + c) % 2
                pool.wait_ge(s_mean, TT * q + c + 1)
                nc.gpsimd.tensor_tensor(rstd[:, sl, :], msq[:, sl, :], neg_half[:, :], ALU.pow).then_inc(s_rs, 1)

            def out_lo(p):
                pool.wait_ge(s_ghi, p + 1)
                nc.gpsimd.tensor_tensor(gt_pair(gt[1], p), gated[:, :], gt_pair(gt[0], p).bitcast(F32),
                                        ALU.subtract).then_inc(s_glo, 1)

            def step_a(p, par, att=True, ahead=True):
                for what, n in STEP_A:
                    if what == "C" and ahead:
                        rms_a(p + 1, 1 - par, n)
                        if not att and n + 4 < TT:
                            rms_rows(0, n + 4)
                    elif what == "W":
                        if n == 0 and not (isinstance(p, int) and p < 0):
                            sem, count = last_reader(p + 2)
                            pool.wait_ge(sem, count)
                        split_piece(p + 2, n, par, KD * 512)
                    elif (what, n) == ("O", OA - 1) and att:
                        out_lo(p)

            step_a(-1, 1, att=False)
            step_a(0, 0)
            pool.wait_ge(s_xt, 2 * TT)
            nc.gpsimd.memset(gt[0][:, KD * TOK:FLAT].bitcast(F32), 0.0).then_inc(s_zeros_b, 1)
            nc.gpsimd.memset(gt[1][:, KD * TOK:FLAT].bitcast(F32), 0.0).then_inc(s_zeros_b, 1)
            with pool.Fori(0, 3) as i:
                step_a(2 * i + 1, 1)
                step_a(2 * i + 2, 0)
            step_a(7, 1, ahead=False)

            split_group(G_LAT)
            for i in range(TT):
                rms_rows(1, i)

            split_group(G_KPE)

            def rms_lat(n):
                pool.wait_ge(s_lat_ss, n + 1)
                if n < TT:
                    nc.gpsimd.tensor_tensor(lat_ss[:, n, 0:1], lat_ss[:, n, 0:1], lat_ss[:, n, 2:3],
                                            ALU.add).then_inc(s_lat_sum, 1)
                    pool.wait_ge(s_lat_sum, n + 1)
                nc.gpsimd.tensor_scalar(lat_ms[:, n, 0:1], lat_ss[:, n, 0:1], 1.0 / KV, EPS,
                                        ALU.mult, ALU.add).then_inc(s_lat_ms, 1)
                w = 1
                if n < TT:
                    nc.gpsimd.tensor_scalar(lat_ms[:, n, 1:2], lat_ss[:, n, 1:2], 1.0 / ROPE, EPS,
                                            ALU.mult, ALU.add).then_inc(s_lat_ms, 1)
                    w = 2
                pool.wait_ge(s_lat_ms, 2 * (n + 1) if n < TT else TT + n + 1)
                nc.gpsimd.tensor_tensor(lat_r[:, n, 0:w], lat_ms[:, n, 0:w], neg_half[:, 0:w],
                                        ALU.pow).then_inc(s_lat_r, 1)

            def split_late(g, j):
                if j == 0:
                    sem, n = last_reader(g)
                    pool.wait_ge(sem, n)
                split_piece(g, j, g % 2, COLS[g])

            for i in range(TT):
                if i > 1:
                    split_late(G_QA, i - 2)
                rms_lat(i)
            split_late(G_QA, 3)
            for m in range(2):
                pool.wait_ge(s_latm, TT)
                nc.gpsimd.memset(qat[m][:, KL * TOK:QFLAT].bitcast(F32), 0.0).then_inc(s_zeros_d, 1)
            for t in range(TT):
                rms_lat(TT + t)
                if t < PIECES:
                    split_late(G_GATE, t)
            split_group(G_GATE + 1)
            split_group(G_D)

            pool.wait_ge(s_latout, 32 * TT)
            pool.wait_ge(s_kpet_e, LT)
            pool.wait_ge(s_latx, LT + TT)
            pool.wait_ge(s_dve_c, CA * NP + 2 * NH)
            nc.gpsimd.memset(prob[:, 0, 0:SKEY], 0.0).then_inc(s_zeros_d, 1)

            def rms_d(q, par, what, t):
                c = CHUNK_D[what, t]
                sl = (par + c) % 2
                w = 4 if what == "Q" else 2
                pool.wait_ge(s_mean2, CD * q + c + 1)
                nc.gpsimd.tensor_tensor(rstd[:, sl, 0:w], msq[:, sl, 0:w], neg_half[:, 0:w],
                                        ALU.pow).then_inc(s_rs2, 1)

            def step_d(p, par, ahead=True):
                for what, n in order_d(p):
                    if what in "QK" and ahead:
                        rms_d(p + 1, 1 - par, what, n)
                    elif what == "W":
                        g = p + G_D + 2
                        if n == 0:
                            sem, count = last_reader_d(p)
                            pool.wait_ge(sem, count)
                        split_piece(g, n, g % 2, COLS[g])

            step_d(-1, 1)
            for p in range(MP):
                step_d(p, p % 2, ahead=p + 1 < MP)

            pool.wait_ge(s_proj2, CD * MP)
            nc.gpsimd.memset(ghi[:, KD * TOK:FLAT].bitcast(F32), 0.0).then_inc(s_zeros_e, 1)
            nc.gpsimd.memset(glo[:, KD * TOK:FLAT].bitcast(F32), 0.0).then_inc(s_zeros_e, 1)
            for t in range(TT):
                rms_rows(2, t)

        @block.vector
        def _(dve):
            v = nc.vector
            def norm_x(t):
                n = P if t < NT else SMP
                dve.wait_ge(s_row_r, t + 1)
                v.tensor_scalar(x_in[0:n, t, :], x_in[0:n, t, :], row_r[0:n, 0, t:t + 1], None,
                                ALU.mult).then_inc(s_xn, 1)

            def x_lo(t):
                n = P if t < NT else SMP
                for j in range(2):
                    dve.wait_ge(s_xt_hi, 2 * t + j + 1)
                    for k in range(KD // 2):
                        K = j * KD // 2 + k
                        c = slice(K * TOK + t * P, K * TOK + t * P + n)
                        last = v.scalar_tensor_tensor(out=ht[1][:, c], in0=XTB[t % 2][j][:, k * P:k * P + n],
                                                      scalar=g_col[:, 0, K:K + 1], in1=ht[0][:, c].bitcast(F32),
                                                      op0=ALU.mult, op1=ALU.subtract)
                    last.then_inc(s_xt_lo, 1)

            def w_lo(j):
                c = slice(j * 2 * 512 + POOL_SHARE, (j + 1) * 2 * 512)
                dve.wait_ge(s_hi, j + 1)
                v.tensor_tensor(wlo[0][:, c], raw[:, c], whi[0][:, c].bitcast(F32),
                                ALU.subtract).then_inc(s_lo_dve, 1)

            norm_x(0)
            dve.wait_ge(s_gcol, 1)
            norm_x(1)
            x_lo(0)
            w_lo(0)
            x_lo(1)
            for j in range(1, PIECES):
                w_lo(j)
            norm_x(2)
            v.memset(left[:, :, SEQ:SEQ + 1], 1.0).then_inc(s_gscale, 1)
            dve.wait_ge(s_const_d, 16 * 8)
            v.tensor_scalar(g_qk[:, 0, :, :], g_qk[:, 0, :, :], HD ** -0.5, None, ALU.mult).then_inc(s_gscale, 1)
            v.tensor_scalar(g_q[:, :], g_q[:, :], QK ** -0.5, None, ALU.mult).then_inc(s_gscale, 1)
            dve.wait_ge(s_gscale, 3)
            norm_x(3)
            x_lo(2)

            def sums_a(q, par, c):
                sl = (par + c) % 2
                dve.wait_ge(s_sqd, TT * q + c + 1)
                if begun(TT * q + c - 1):
                    dve.wait_ge(s_rs, TT * q + c - 1)
                v.tensor_reduce(ssq[:, sl, :], sq[:, :].rearrange("p (a d) -> p a d", a=4), AX.X,
                                ALU.add).then_inc(s_msq_d, 1)
                dve.wait_ge(s_msq_d, TT * q + c + 1)
                v.tensor_scalar(msq[:, sl, :], ssq[:, sl, :], 1.0 / HD, EPS, ALU.mult, ALU.add).then_inc(s_mean, 1)

            def scale_a(q, par, c):
                sl = (par + c) % 2
                b = PRJ[sl]
                dve.wait_ge(s_rs, TT * q + c + 1)
                dve.wait_ge(s_act_c, CA * q + c + 1)
                v.tensor_tensor(qkr[:, :].rearrange("p (a d) -> p a d", a=4),
                                b[:, 0:2 * P].rearrange("p (a d) -> p a d", a=4),
                                rstd[:, sl, :].unsqueeze(2).to_broadcast([P, 4, HD]), ALU.mult).then_inc(s_dve_c, 1)
                dve.wait_ge(s_dve_c, CA * q + c + 1)
                if c == 0:
                    if begun(XA * q):
                        dve.wait_ge(s_xpose, XA * q)
                    if begun(32 * q):
                        dve.wait_ge(s_kout, 32 * q)
                v.tensor_tensor(qkn[:, c, :, :].rearrange("p m d -> p (m d)"), qkr[:, :],
                                g_qk[:, :, :, :].rearrange("p m h d -> p (m h d)"), ALU.mult).then_inc(s_normed, 1)

            def gate_a(q, par, j):
                c = TT + j
                dve.wait_ge(s_act_c, CA * q + c + 1)
                v.tensor_tensor(sgate[:, par, j * HALF:(j + 1) * HALF], PRJ[(par + c) % 2][:, 0:HALF], sigm[:, :],
                                ALU.mult).then_inc(s_dve_c, 1)

            def weight_a(p, par, u):
                ub = (par + u) % 2
                dve.wait_ge(s_stay, UA * p + u + 1)
                r, n = (2 * SMP, SKEY) if u == 0 else (P, (UNIT_A[u][1] + 1) * P)
                back = stay[0:r, ub, SEQ - n:SEQ][:, ::-1]
                v.tensor_tensor_scan(out=left[0:r, ub, SEQ - n:SEQ][:, ::-1], data0=back, data1=back, initial=1.0,
                                     op0=ALU.mult, op1=ALU.bypass).then_inc(s_left, 1)
                dve.wait_ge(s_left, UA * p + u + 1)
                if begun(UA * p + u - 1):
                    dve.wait_ge(s_tr, UA * p + u - 1)
                v.tensor_tensor(wgt[0:r, ub, 0:n], left[0:r, ub, SEQ - n + 1:SEQ + 1], left[0:r, ub, SEQ - n:SEQ],
                                ALU.subtract).then_inc(s_wgt, 1)

            def gate_out(p, par, o):
                dve.wait_ge(s_av, OA * p + o + 1)
                if o == 0:
                    if begun(p):
                        dve.wait_ge(s_ghi, p)
                    if begun(p):
                        dve.wait_ge(s_glo, p)
                c0, n = (SEQ, SMP) if o == 0 else ((NT - o) * P, P)
                b0 = 0 if o == 0 else c0
                v.tensor_tensor(gated[:, c0:c0 + n], OUT[:, b0:b0 + n], sgate[:, par, c0:c0 + n],
                                ALU.mult).then_inc(s_odone, 1)

            def step_a(p, par, att=True, ahead=True):
                for what, n in STEP_A:
                    if what == "C" and ahead:
                        if not att and n + 3 < TT:
                            x_lo(n + 3)
                        sums_a(p + 1, 1 - par, n)
                        if not att and n + 4 < TT:
                            norm_x(n + 4)
                        scale_a(p + 1, 1 - par, n)
                    elif what == "G" and ahead:
                        gate_a(p + 1, 1 - par, n)
                    elif what == "S" and att:
                        weight_a(p, par, n)
                    elif what == "O" and att:
                        gate_out(p, par, n)

            step_a(-1, 1, att=False)
            step_a(0, 0)
            with dve.Fori(0, 3) as i:
                step_a(2 * i + 1, 1)
                step_a(2 * i + 2, 0)
            step_a(7, 1, ahead=False)

            def add_x(i, nh):
                t = ORDER[i]
                n = P if t < NT else SMP
                c = slice(nh * 512, (nh + 1) * 512)
                m = TT * nh + i
                dve.wait_ge(s_x2d[t], 16)
                dve.wait_ge(s_yprod, m + 1)
                v.tensor_tensor(x2[0:n, t, c], bank[m % 4][0:n, :], x2[0:n, t, c], ALU.add).then_inc(s_x2sum, 1)

            def x2_lo(i):
                t = ORDER[i]
                n = P if t < NT else SMP
                for j in range(2):
                    dve.wait_ge(s_ct_hi, 2 * i + j + 1)
                    for k in range(KD // 2):
                        K = j * KD // 2 + k
                        src = bank[4 + 2 * (i % 2) + j][:, k * P:k * P + n]
                        c = slice(K * TOK + t * P, K * TOK + t * P + n)
                        for m, dst, hi in ((1, gt[1], gt[0]), (2, ht[1], ht[0])):
                            last = v.scalar_tensor_tensor(out=dst[:, c], in0=src, scalar=g_col[:, m, K:K + 1],
                                                          in1=hi[:, c].bitcast(F32), op0=ALU.mult, op1=ALU.subtract)
                    last.then_inc(s_ct_lo, 1)

            for i in range(TT):
                add_x(i, 0)
            for i in range(TT):
                add_x(i, 1)
                if i:
                    x2_lo(i - 1)
            x2_lo(TT - 1)

            def rotary_norm(src, r, gain):
                v.scalar_tensor_tensor(out=pe_tmp[:, 0, :], in0=src, scalar=r, in1=gain, op0=ALU.mult,
                                       op1=ALU.mult).then_inc(s_rope, 1)

            def rotate(dst, t, n):
                dve.wait_ge(s_rope, 3 * n + 1)
                v.tensor_tensor(pe_tmp[:, 1, :].rearrange("p (h d) -> p h d", h=2),
                                pe_tmp[:, 0, :].rearrange("p (h d) -> p h d", h=2),
                                cos_t[:, t, :].unsqueeze(1).to_broadcast([P, 2, ROPE // 2]),
                                ALU.mult).then_inc(s_rope, 1)
                swapped = pe_tmp[:, 0, :].rearrange("p (h d) -> p h d", h=2)[:, ::-1, :]
                v.tensor_tensor(pe_tmp[:, 2, :].rearrange("p (h d) -> p h d", h=2), swapped,
                                sin_t[:, t, :].rearrange("p (h d) -> p h d", h=2), ALU.mult).then_inc(s_rope, 1)
                dve.wait_ge(s_rope, 3 * n + 3)
                return v.tensor_tensor(dst.rearrange("p (h d) -> p h d", h=2),
                                       pe_tmp[:, 1, :].unsqueeze(1).to_broadcast([P, 2, ROPE]),
                                       pe_tmp[:, 2, :].unsqueeze(1).to_broadcast([P, 2, ROPE]), ALU.add)

            def lat_lo(i):
                t = ORDER[i] if i < TT else TT
                dve.wait_ge(s_lat_hi, i + 1)
                v.tensor_tensor(turned(latt[1], t, P), bank[4][:, :].rearrange("p (k c) -> p k c", k=KL),
                                turned(latt[0], t, P).bitcast(F32), ALU.subtract).then_inc(s_lat_lo, 1)

            def qa_lo(t):
                n = P if t < NT else SMP
                dve.wait_ge(s_lat_hi, LT + t + 1)
                v.tensor_tensor(turned(qat[1], t, n, width=TOK),
                                bank[4][:, :].rearrange("p (k c) -> p k c", k=KL)[:, :, 0:n],
                                turned(qat[0], t, n, width=TOK).bitcast(F32), ALU.subtract).then_inc(s_lat_lo, 1)

            dve.wait_ge(s_rows_g, 32)
            dve.wait_ge(s_rope_d, 32)
            dve.wait_ge(s_x2out, 16 * TT)
            for i, t in enumerate(ORDER):
                b = bank[3 + 3 * (i % 2)]
                dve.wait_ge(s_lat_r, i + 1)
                rotary_norm(b[:, KV - LA:LB], lat_r[:, i, 1:2], g_kp[:, :])
                v.scalar_tensor_tensor(out=lat[:, t, 0:LA], in0=LAB[i % 3][:, 0:LA], scalar=lat_r[:, i, 0:1],
                                       in1=g_lat[:, 0:LA], op0=ALU.mult, op1=ALU.mult)
                v.scalar_tensor_tensor(out=lat[:, t, LA:KV], in0=b[:, 0:KV - LA], scalar=lat_r[:, i, 0:1],
                                       in1=g_lat[:, LA:KV], op0=ALU.mult, op1=ALU.mult).then_inc(s_latn, 1)
                rotate(kpe[:, t, :], t, i).then_inc(s_kper, 1)
                if i:
                    lat_lo(i - 1)
            lat_lo(TT - 1)
            for t in range(TT):
                dve.wait_ge(s_lat_r, TT + t + 1)
                if t:
                    dve.wait_ge(s_latx, LT + t)
                v.scalar_tensor_tensor(out=qan[:, :], in0=QAB[t % 2][:, :], scalar=lat_r[:, TT + t, 0:1],
                                       in1=g_qar[:, :], op0=ALU.mult, op1=ALU.mult).then_inc(s_latn, 1)
                if t == 0:
                    lat_lo(TT)
                if t:
                    qa_lo(t - 1)
            for n in range(2 * NH):
                dve.wait_ge(s_act_c, CA * NP + n + 1)
                v.tensor_tensor(sg[:, n // 2, (n % 2) * HALF:(n % 2 + 1) * HALF], bank[2 + n % 2][:, 0:HALF], sigc[:, :],
                                ALU.mult).then_inc(s_dve_c, 1)
                if n == 1:
                    qa_lo(TT - 1)

            dve.wait_ge(s_latout, 32 * TT)
            dve.wait_ge(s_kpet_e, LT)

            def sums_d(q, par, what, t):
                c = CHUNK_D[what, t]
                sl = (par + c) % 2
                if begun(CD * q + c - 1):
                    dve.wait_ge(s_rs2, CD * q + c - 1)
                if what == "Q":
                    dve.wait_ge(s_act2, CD * q + c + 1)
                    by_head = sqd[:, 0:WQ].rearrange("p (h d) -> p h d", h=2)
                    v.tensor_reduce(ssq[:, sl, 0:2], by_head[:, :, 0:NOPE], AX.X, ALU.add)
                    v.tensor_reduce(ssq[:, sl, 2:4], by_head[:, :, NOPE:QK], AX.X, ALU.add).then_inc(s_sum2, 1)
                    dve.wait_ge(s_sum2, CD * q + c + 1)
                    v.tensor_scalar(msq[:, sl, 2:4], ssq[:, sl, 2:4], 1.0 / ROPE, EPS, ALU.mult, ALU.add)
                else:
                    dve.wait_ge(s_sqk, LT * q + t + 1)
                    v.tensor_reduce(ssq[:, sl, 0:2], sqd[:, 0:2 * NOPE].rearrange("p (h d) -> p h d", h=2), AX.X,
                                    ALU.add).then_inc(s_sum2, 1)
                    dve.wait_ge(s_sum2, CD * q + c + 1)
                v.tensor_scalar(msq[:, sl, 0:2], ssq[:, sl, 0:2], 1.0 / NOPE, EPS, ALU.mult,
                                ALU.add).then_inc(s_mean2, 1)

            def norm_d(q, par, what, t):
                c = CHUNK_D[what, t]
                sl = (par + c) % 2
                b = chunk_bank(q, par, c)
                dve.wait_ge(s_rs2, CD * q + c + 1)
                dve.wait_ge(s_act2, CD * q + c + 1)
                before = CD * q + (CHUNK_D[what, t - 2] + 1 if t > 1 else 0)
                if begun(before):
                    dve.wait_ge(s_xp2, before)
                if what == "K":
                    for h in range(2):
                        last = v.scalar_tensor_tensor(out=kn2[:, t % 2, h * NOPE:(h + 1) * NOPE],
                                                      in0=b[:, h * 256:h * 256 + NOPE], scalar=rstd[:, sl, h:h + 1],
                                                      in1=g_kn[:, :], op0=ALU.mult, op1=ALU.mult)
                    last.then_inc(s_dve2, 1)
                    return
                n3 = 3 * (TT * q + t)
                for h in range(2):
                    last = v.scalar_tensor_tensor(out=pe_tmp2[:, 0, h * ROPE:(h + 1) * ROPE],
                                                  in0=b[:, h * QK + NOPE:(h + 1) * QK], scalar=rstd[:, sl, 2 + h:3 + h],
                                                  in1=g_q[:, NOPE:QK], op0=ALU.mult, op1=ALU.mult)
                last.then_inc(s_rope2, 1)
                for h in range(2):
                    last = v.scalar_tensor_tensor(out=qn2[:, t % 2, h * NOPE:(h + 1) * NOPE],
                                                  in0=b[:, h * QK:h * QK + NOPE], scalar=rstd[:, sl, h:h + 1],
                                                  in1=g_q[:, 0:NOPE], op0=ALU.mult, op1=ALU.mult)
                last.then_inc(s_dve2, 1)
                dve.wait_ge(s_rope2, n3 + 1)
                v.tensor_tensor(pe_tmp2[:, 1, :].rearrange("p (h d) -> p h d", h=4),
                                pe_tmp2[:, 0, :].rearrange("p (h d) -> p h d", h=4),
                                cos_t[:, t, :].unsqueeze(1).to_broadcast([P, 4, ROPE // 2]),
                                ALU.mult).then_inc(s_rope2, 1)
                swapped = pe_tmp2[:, 0, :].rearrange("p (h s d) -> p h s d", h=2, s=2)[:, :, ::-1, :]
                v.tensor_tensor(pe_tmp2[:, 2, :].rearrange("p (h s d) -> p h s d", h=2, s=2), swapped,
                                sin_t[:, t, :].rearrange("p (s d) -> p s d", s=2).unsqueeze(1)
                                .to_broadcast([P, 2, 2, ROPE // 2]), ALU.mult).then_inc(s_rope2, 1)
                dve.wait_ge(s_rope2, n3 + 3)
                v.tensor_tensor(qn2[:, t % 2, 2 * NOPE:WQ], pe_tmp2[:, 1, :], pe_tmp2[:, 2, :],
                                ALU.add).then_inc(s_nrm2, 1)

            def rows_d(par, u):
                ub = (par + u) % 2
                return (ub, 2 * SMP, SKEY) if u == 0 else (ub, P, (UNIT_D[u][1] + 1) * P)

            def max_d(p, par, u):
                ub, r, n = rows_d(par, u)
                dve.wait_ge(s_score2, UA * p + u + 1)
                v.tensor_reduce(neg_max[0:r, ub:ub + 1], SCR[ub][0:r, 0:n], AX.X, ALU.max,
                                negate=True).then_inc(s_negmax, 1)

            def scale_d(p, par, u):
                ub, r, n = rows_d(par, u)
                dve.wait_ge(s_expd, UA * p + u + 1)
                v.reciprocal(p_inv[0:r, ub:ub + 1], p_sum[0:r, ub:ub + 1]).then_inc(s_inv, 1)
                dve.wait_ge(s_inv, UA * p + u + 1)
                v.tensor_scalar(prob[0:r, ub, 0:n], prob[0:r, ub, 0:n], p_inv[0:r, ub:ub + 1], None,
                                ALU.mult).then_inc(s_scaled, 1)

            def gate_out_d(p, o):
                dve.wait_ge(s_av2, 3 * p + o + 1)
                if o == 0:
                    heads = sg[:, 2 * p:2 * p + 2, SEQ:TOK]
                    v.tensor_tensor(heads, OUT[:, 0:2 * SMP].rearrange("p (h c) -> p h c", h=2), heads,
                                    ALU.mult).then_inc(s_od2, 1)
                    return
                head = sg[:, 2 * p + o - 1, 0:SEQ]
                v.tensor_tensor(head, OUT[:, 0:SEQ], head, ALU.mult).then_inc(s_od2, 1)

            def gated_lo(K):
                c = slice(K * TOK, (K + 1) * TOK)
                dve.wait_ge(s_go_hi, K + 1)
                v.tensor_tensor(glo[:, c], sg[:, K, :], ghi[:, c].bitcast(F32), ALU.subtract).then_inc(s_go_lo, 1)

            def step_d(p, par, att=True, ahead=True):
                for what, n in order_d(p):
                    if what in "QK" and ahead:
                        sums_d(p + 1, 1 - par, what, n)
                    elif what == "N" and ahead:
                        norm_d(p + 1, 1 - par, *CHUNKS[n])
                    elif what == "S" and att:
                        max_d(p, par, n)
                    elif what == "R" and att:
                        scale_d(p, par, n)
                    elif what == "H":
                        gated_lo(n)
                    elif what == "O" and att:
                        gate_out_d(p, n)

            step_d(-1, 1, att=False)
            for p in range(MP):
                step_d(p, p % 2, ahead=p + 1 < MP)

            gated_lo(KD - 1)

            def norm_y(t):
                n = P if t < NT else SMP
                dve.wait_ge(s_row_r, 2 * TT + t + 1)
                v.scalar_tensor_tensor(out=x2e[0:n, t, :], in0=x2e[0:n, t, :], scalar=row_r[0:n, 2, t:t + 1],
                                       in1=g_fin[0:n, :], op0=ALU.mult, op1=ALU.mult).then_inc(s_yn, 1)

            dve.wait_ge(s_gfin, 16)
            for t in range(TT):
                n = P if t < NT else SMP
                dve.wait_ge(s_x2in[t], 16)
                for nh in range(2):
                    c = slice(nh * 512, (nh + 1) * 512)
                    m = 2 * t + nh
                    dve.wait_ge(s_yprod, 2 * TT + m + 1)
                    v.tensor_tensor(x2e[0:n, t, c], bank[m % 4][0:n, :], x2e[0:n, t, c], ALU.add).then_inc(s_ysum, 1)
                if t:
                    norm_y(t - 1)
            norm_y(TT - 1)


_INS = ["x_prompt", "x_sample", "cache_sb_k", "cache_sb_v", "cache_mla_latent", "cache_mla_kpe", "g_pre_a",
        "w_in_a", "g_q_a", "g_k_a", "w_o_a", "g_kv", "w_kv_a", "g_kv_a", "g_kpe", "w_kv_b", "g_knope", "g_pre_b",
        "w_in_b", "g_qa", "w_q_b", "g_qn", "g_qp", "w_o_b", "g_final"]
_OUTS = [(1, SEQ, D), (1, SMP, D), (1, 1, SEQ, 16, HD), (1, 1, SEQ, 16, HD), (1, SEQ, KV), (1, SEQ, ROPE),
         (1, 1, SMP, 16, HD), (1, 1, SMP, 16, HD), (1, SMP, KV), (1, SMP, ROPE)]


def kernel(**inputs):
    import concourse.bacc as bacc
    from concourse.bass_utils import run_bass_kernel_spmd

    nc = bacc.Bacc("TRN2", target_bir_lowering=False, num_devices=1)
    cos, sin = rope_tables()
    arrays = {f"in_{n}": np.ascontiguousarray(inputs[n]) for n in _INS}
    arrays["in_rope_cos"], arrays["in_rope_sin"] = cos, sin
    a = {n[3:]: nc.dram_tensor(n, v.shape, F32, kind="ExternalInput").ap() for n, v in arrays.items()}
    out = [nc.dram_tensor(f"out_{i}", sh, F32, kind="ExternalOutput").ap() for i, sh in enumerate(_OUTS)]
    scratch = nc.dram_tensor("x2_scratch", (TT * P, D), F32, kind="Internal").ap()
    build(nc, a, out, scratch)
    r = run_bass_kernel_spmd(nc, [arrays], core_ids=[0])
    return tuple(r.results[0][f"out_{i}"] for i in range(len(_OUTS)))
```
